# Optimizing a Trainium2 kernel written in Bass

```python
import math
import jax
import jax.numpy as jnp
from jax import lax
import numpy as np

D_MODEL = 2048
BATCH = 1
SEQ = 512
DEPTH = 2

HEAD_DIM = 128
ROPE_DIM = HEAD_DIM // 4
ROPE_THETA = 500000.0
Q_BLOCK = 128

NSA_HEADS = 6
NSA_KV_HEADS = 2
NSA_GROUP = NSA_HEADS // NSA_KV_HEADS
CMP_LEN = 32
CMP_STRIDE = 16
SLC_LEN = 64
SLC_TOPK = 16
WINDOW = 512
FORCE_BONUS = 1.0e4

GDN_HEADS = 6
GDN_CONV = 4
GDN_CHUNK = 64

SB_HEADS = 4

NSA_W = NSA_HEADS * HEAD_DIM
KV_W = NSA_KV_HEADS * HEAD_DIM
GDN_W = GDN_HEADS * HEAD_DIM
SB_W = SB_HEADS * HEAD_DIM
MIX_W = NSA_W + GDN_W + SB_W
IN_SPLITS = (NSA_W, KV_W, KV_W, KV_W, KV_W, KV_W, KV_W, 3 * NSA_HEADS, NSA_W,
             3 * GDN_W, GDN_HEADS, GDN_HEADS, GDN_W,
             SB_W, SB_W, SB_W, SB_W)
IN_COLS = sum(IN_SPLITS)

DEEPNORM_ALPHA = (2 * DEPTH) ** 0.25
DEEPNORM_BETA = (8 * DEPTH) ** -0.25
LN_EPS = 1e-5
RMS_EPS = 1e-6
NEG_INF = -1e30

kernel_name = 'hybrid_nsa_gdn_stickbreak_trunk'

def _layernorm(x, g, b):
    xf = x.astype(jnp.float32)
    mu = jnp.mean(xf, axis=-1, keepdims=True)
    var = jnp.mean(jnp.square(xf - mu), axis=-1, keepdims=True)
    return ((xf - mu) * lax.rsqrt(var + LN_EPS) * g + b).astype(x.dtype)

def _rope(x, pos):
    half = ROPE_DIM // 2
    inv = ROPE_THETA ** (-jnp.arange(half, dtype=jnp.float32) * 2.0 / ROPE_DIM)
    ang = pos.astype(jnp.float32)[..., None] * inv
    cos = jnp.cos(ang)[:, :, None, :].astype(x.dtype)
    sin = jnp.sin(ang)[:, :, None, :].astype(x.dtype)
    x1 = x[..., :half]
    x2 = x[..., half:ROPE_DIM]
    return jnp.concatenate([x1 * cos - x2 * sin, x2 * cos + x1 * sin, x[..., ROPE_DIM:]], axis=-1)

def _masked_softmax(s, mask, axis):
    s = jnp.where(mask, s, NEG_INF)
    m = jnp.max(s, axis=axis, keepdims=True)
    e = jnp.where(mask, jnp.exp(s - m), 0.0)
    return e / jnp.maximum(jnp.sum(e, axis=axis, keepdims=True), 1e-30)

def _to_blocks(x):
    b, s = x.shape[:2]
    return jnp.moveaxis(x.reshape((b, s // Q_BLOCK, Q_BLOCK) + x.shape[2:]), 1, 0)

def _from_blocks(y):
    n, b = y.shape[:2]
    return jnp.moveaxis(y, 0, 1).reshape((b, n * Q_BLOCK) + y.shape[3:])

def _split(p, sizes):
    cuts = np.cumsum(np.array(sizes))[:-1].tolist()
    return jnp.split(p, cuts, axis=-1)

def _nsa(q, gates, k_cmp, v_cmp, k_slc, v_slc, k_win, v_win, positions,
         pe_k, pe_v, w1_k, w2_k, w1_v, w2_v):
    b, s = q.shape[:2]
    dt = q.dtype
    n_cmp = (s - CMP_LEN) // CMP_STRIDE + 1
    n_slc = s // SLC_LEN
    n_top = min(SLC_TOPK, n_slc)
    scale = HEAD_DIM ** -0.5
    starts = jnp.arange(n_cmp) * CMP_STRIDE
    cmp_end = starts + CMP_LEN - 1
    cidx = starts[:, None] + jnp.arange(CMP_LEN)[None, :]

    def compress(kv, pe, w1, w2):
        blk = kv[:, cidx] + pe[None, None, :, None, :]
        flat = jnp.swapaxes(blk, 2, 3).reshape(b, n_cmp, NSA_KV_HEADS, CMP_LEN * HEAD_DIM)
        return jax.nn.silu(flat @ w1) @ w2

    kc = _rope(compress(k_cmp, pe_k, w1_k, w2_k), positions[:, cmp_end])
    vc = compress(v_cmp, pe_v, w1_v, w2_v)
    slc_ids = jnp.arange(n_slc)
    ov = (jnp.minimum(cmp_end[:, None] + 1, (slc_ids[None, :] + 1) * SLC_LEN)
          - jnp.maximum(starts[:, None], slc_ids[None, :] * SLC_LEN))
    overlap = jnp.maximum(ov, 0).astype(jnp.float32) / CMP_LEN
    kblk = jnp.moveaxis(k_slc.reshape(b, n_slc, SLC_LEN, NSA_KV_HEADS, HEAD_DIM), 3, 1)
    vblk = jnp.moveaxis(v_slc.reshape(b, n_slc, SLC_LEN, NSA_KV_HEADS, HEAD_DIM), 3, 1)
    pad = ((0, 0), (WINDOW, 0), (0, 0), (0, 0))
    kwp = jnp.pad(k_win, pad)
    vwp = jnp.pad(v_win, pad)
    gather = jax.vmap(jax.vmap(lambda tab, ix: tab[ix]))
    slc_off = jnp.arange(SLC_LEN)
    win_off = jnp.arange(WINDOW + Q_BLOCK) - WINDOW

    def block(args):
        qb, gb, i = args
        t = i * Q_BLOCK + jnp.arange(Q_BLOCK)
        sc = jnp.einsum('btgrd,bngd->bgrtn', qb, kc).astype(jnp.float32) * scale
        pc = _masked_softmax(sc, cmp_end[None, :] <= t[:, None], -1)
        o_c = jnp.einsum('bgrtn,bngd->btgrd', pc.astype(dt), vc)
        imp = jnp.einsum('bgrtn,nj->bgtj', pc, overlap)
        cur = t // SLC_LEN
        future = slc_ids[None, :] * SLC_LEN > t[:, None]
        forced = ((slc_ids[None, :] == 0) | (slc_ids[None, :] == cur[:, None])
                  | (slc_ids[None, :] == cur[:, None] - 1))
        imp = jnp.where(future, NEG_INF, jnp.where(forced, imp + FORCE_BONUS, imp))
        top_v, top_i = lax.top_k(imp, n_top)
        ok = top_v > 0.5 * NEG_INF
        ks = gather(kblk, top_i)
        vs = gather(vblk, top_i)
        ss = jnp.einsum('btgrd,bgtkld->bgrtkl', qb, ks).astype(jnp.float32) * scale
        tok = top_i[..., None] * SLC_LEN + slc_off
        ms = ok[..., None] & (tok <= t[None, None, :, None, None])
        ps = _masked_softmax(ss, ms[:, :, None], (-2, -1))
        o_s = jnp.einsum('bgrtkl,bgtkld->btgrd', ps.astype(dt), vs)
        kw = lax.dynamic_slice_in_dim(kwp, i * Q_BLOCK, WINDOW + Q_BLOCK, axis=1)
        vw = lax.dynamic_slice_in_dim(vwp, i * Q_BLOCK, WINDOW + Q_BLOCK, axis=1)
        spos = i * Q_BLOCK + win_off
        dpos = t[:, None] - spos[None, :]
        mw = (dpos >= 0) & (dpos < WINDOW) & (spos[None, :] >= 0)
        sw = jnp.einsum('btgrd,bsgd->bgrts', qb, kw).astype(jnp.float32) * scale
        pw = _masked_softmax(sw, mw, -1)
        o_w = jnp.einsum('bgrts,bsgd->btgrd', pw.astype(dt), vw)
        return gb[..., 0:1] * o_c + gb[..., 1:2] * o_s + gb[..., 2:3] * o_w

    qg = q.reshape(b, s, NSA_KV_HEADS, NSA_GROUP, HEAD_DIM)
    gg = gates.reshape(b, s, NSA_KV_HEADS, NSA_GROUP, 3)
    out = lax.map(block, (_to_blocks(qg), _to_blocks(gg), jnp.arange(s // Q_BLOCK)))
    return _from_blocks(out).reshape(b, s, NSA_W)

def _causal_conv(x, w):
    ch = x.shape[-1]
    return lax.conv_general_dilated(x, w[:, None, :], (1,), [(GDN_CONV - 1, 0)],
                                    dimension_numbers=('NWC', 'WIO', 'NWC'),
                                    feature_group_count=ch)

def _gated_delta(q, k, v, beta, g):
    b, s, h, d = q.shape
    nc = s // GDN_CHUNK

    def chunks(a):
        return jnp.moveaxis(a.reshape((b, nc, GDN_CHUNK, h) + a.shape[3:]), 3, 1)

    q = chunks(q) * (d ** -0.5)
    k = chunks(k)
    v = chunks(v)
    beta = chunks(beta)
    gc = jnp.cumsum(chunks(g), axis=-1)
    idx = jnp.arange(GDN_CHUNK)
    incl = idx[:, None] >= idx[None, :]
    strict = idx[:, None] > idx[None, :]
    diff = gc[..., :, None] - gc[..., None, :]
    decay = jnp.where(incl, jnp.exp(jnp.where(incl, diff, 0.0)), 0.0)
    kb = k * beta[..., None]
    lower = jnp.where(strict, jnp.einsum('bhncd,bhned->bhnce', kb, k) * decay, 0.0)
    tri = lower + jnp.eye(GDN_CHUNK, dtype=jnp.float32)
    rhs = jnp.concatenate([v * beta[..., None], kb * jnp.exp(gc)[..., None]], axis=-1)
    sol = lax.linalg.triangular_solve(tri, rhs, left_side=True, lower=True, unit_diagonal=True)
    u = sol[..., :d]
    w = sol[..., d:]
    intra = jnp.einsum('bhncd,bhned->bhnce', q, k) * decay
    g_last = gc[..., -1]
    k_tail = k * jnp.exp(g_last[..., None] - gc)[..., None]
    q_head = q * jnp.exp(gc)[..., None]

    def step(state, xs):
        u_i, w_i, qh_i, kt_i, intra_i, gl_i = xs
        v_new = u_i - jnp.einsum('bhcd,bhde->bhce', w_i, state)
        o = (jnp.einsum('bhcd,bhde->bhce', qh_i, state)
             + jnp.einsum('bhce,bhef->bhcf', intra_i, v_new))
        state = (state * jnp.exp(gl_i)[..., None, None]
                 + jnp.einsum('bhcd,bhce->bhde', kt_i, v_new))
        return state, o

    xs = tuple(jnp.moveaxis(a, 2, 0) for a in (u, w, q_head, k_tail, intra, g_last))
    _, o = lax.scan(step, jnp.zeros((b, h, d, d), jnp.float32), xs)
    return jnp.transpose(o, (1, 0, 3, 2, 4)).reshape(b, s, h, d)

def _stick_breaking(q, k, v):
    b, s = q.shape[:2]
    dt = q.dtype
    scale = HEAD_DIM ** -0.5
    kpos = jnp.arange(s)

    def block(args):
        qb, i = args
        t = i * Q_BLOCK + jnp.arange(Q_BLOCK)
        z = jnp.einsum('bthd,bshd->bhts', qb, k).astype(jnp.float32) * scale
        past = kpos[None, :] < t[:, None]
        log_beta = jax.nn.log_sigmoid(z)
        log_1m = jnp.where(past, jax.nn.log_sigmoid(-z), 0.0)
        after = lax.cumsum(log_1m, axis=3, reverse=True) - log_1m
        a = jnp.where(past, jnp.exp(log_beta + after), 0.0)
        return jnp.einsum('bhts,bshd->bthd', a.astype(dt), v)

    out = lax.map(block, (_to_blocks(q), jnp.arange(s // Q_BLOCK)))
    return _from_blocks(out)

def setup_inputs(seed: int = 0) -> dict:
    key = jax.random.key(seed)
    ks = jax.random.split(key, 20)
    f32 = jnp.float32

    def nrm(k, shape, std):
        return jax.random.normal(k, shape, f32) * std

    x = nrm(ks[0], (BATCH, SEQ, D_MODEL), 1.0)
    c = nrm(ks[1], (BATCH, D_MODEL), 1.0)
    positions = (jnp.arange(SEQ, dtype=jnp.int32)[None, :]
                 + jax.random.randint(ks[2], (BATCH, 1), 0, 1024, dtype=jnp.int32))
    w_mod = nrm(ks[3], (DEPTH, D_MODEL, 3 * D_MODEL), 0.1 * D_MODEL ** -0.5)
    b_mod = nrm(ks[4], (DEPTH, 3 * D_MODEL), 0.01)
    w_in = nrm(ks[5], (DEPTH, D_MODEL, IN_COLS), D_MODEL ** -0.5)
    w_out = nrm(ks[6], (DEPTH, MIX_W, D_MODEL), DEEPNORM_BETA * MIX_W ** -0.5)
    ln_g = 1.0 + nrm(ks[7], (DEPTH, D_MODEL), 0.02)
    ln_b = nrm(ks[8], (DEPTH, D_MODEL), 0.02)
    cmp_pe_k = nrm(ks[9], (DEPTH, CMP_LEN, HEAD_DIM), 0.02)
    cmp_pe_v = nrm(ks[10], (DEPTH, CMP_LEN, HEAD_DIM), 0.02)
    cmp_w1_k = nrm(ks[11], (DEPTH, CMP_LEN * HEAD_DIM, HEAD_DIM), (CMP_LEN * HEAD_DIM) ** -0.5)
    cmp_w2_k = nrm(ks[12], (DEPTH, HEAD_DIM, HEAD_DIM), HEAD_DIM ** -0.5)
    cmp_w1_v = nrm(ks[13], (DEPTH, CMP_LEN * HEAD_DIM, HEAD_DIM), (CMP_LEN * HEAD_DIM) ** -0.5)
    cmp_w2_v = nrm(ks[14], (DEPTH, HEAD_DIM, HEAD_DIM), HEAD_DIM ** -0.5)
    gdn_conv_w = nrm(ks[15], (DEPTH, GDN_CONV, 3 * GDN_W), GDN_CONV ** -0.5)
    gdn_a_log = jnp.log(jax.random.uniform(ks[16], (DEPTH, GDN_HEADS), f32, 1.0, 16.0))
    dt0 = jnp.exp(jax.random.uniform(ks[17], (DEPTH, GDN_HEADS), f32,
                                     math.log(1e-3), math.log(1e-1)))
    gdn_dt_bias = dt0 + jnp.log(-jnp.expm1(-dt0))
    gdn_norm_g = 1.0 + nrm(ks[18], (DEPTH, HEAD_DIM), 0.02)
    return {'x': x, 'c': c, 'positions': positions, 'w_mod': w_mod, 'b_mod': b_mod,
            'w_in': w_in, 'w_out': w_out, 'ln_g': ln_g, 'ln_b': ln_b,
            'cmp_pe_k': cmp_pe_k, 'cmp_pe_v': cmp_pe_v, 'cmp_w1_k': cmp_w1_k,
            'cmp_w2_k': cmp_w2_k, 'cmp_w1_v': cmp_w1_v, 'cmp_w2_v': cmp_w2_v,
            'gdn_conv_w': gdn_conv_w, 'gdn_a_log': gdn_a_log, 'gdn_dt_bias': gdn_dt_bias,
            'gdn_norm_g': gdn_norm_g}

def reference(x, c, positions, w_mod, b_mod, w_in, w_out, ln_g, ln_b,
              cmp_pe_k, cmp_pe_v, cmp_w1_k, cmp_w2_k, cmp_w1_v, cmp_w2_v,
              gdn_conv_w, gdn_a_log, gdn_dt_bias, gdn_norm_g):
    b, s, _ = x.shape
    dt = x.dtype
    f32 = jnp.float32
    c_act = jax.nn.silu(c)

    def heads(a, n):
        return a.reshape(b, s, n, HEAD_DIM)

    for l in range(DEPTH):
        mod = c_act @ w_mod[l] + b_mod[l]
        shift, scale, gate = jnp.split(mod, 3, axis=-1)
        h = x * (1.0 + scale[:, None, :]) + shift[:, None, :]
        p = h @ w_in[l]
        (nq, nkc, nvc, nks, nvs, nkw, nvw, ng, nz,
         gqkv, gb, ga, gz, sq, sk, sv, sz) = _split(p, IN_SPLITS)

        q_n = _rope(heads(nq, NSA_HEADS), positions)
        gates_n = jax.nn.sigmoid(ng.astype(f32)).reshape(b, s, NSA_HEADS, 3).astype(dt)
        o_nsa = _nsa(q_n, gates_n, heads(nkc, NSA_KV_HEADS), heads(nvc, NSA_KV_HEADS),
                     _rope(heads(nks, NSA_KV_HEADS), positions), heads(nvs, NSA_KV_HEADS),
                     _rope(heads(nkw, NSA_KV_HEADS), positions), heads(nvw, NSA_KV_HEADS),
                     positions, cmp_pe_k[l], cmp_pe_v[l], cmp_w1_k[l], cmp_w2_k[l],
                     cmp_w1_v[l], cmp_w2_v[l])
        y_nsa = o_nsa * jax.nn.silu(nz)

        qkv = jax.nn.silu(_causal_conv(gqkv, gdn_conv_w[l])).astype(f32)
        gq, gk, gv = jnp.split(qkv, 3, axis=-1)
        gq = heads(gq, GDN_HEADS)
        gk = heads(gk, GDN_HEADS)
        gv = heads(gv, GDN_HEADS)
        gq = gq * lax.rsqrt(jnp.sum(gq * gq, axis=-1, keepdims=True) + RMS_EPS)
        gk = gk * lax.rsqrt(jnp.sum(gk * gk, axis=-1, keepdims=True) + RMS_EPS)
        beta = jax.nn.sigmoid(gb.astype(f32))
        g = -jnp.exp(gdn_a_log[l].astype(f32)) * jax.nn.softplus(ga.astype(f32) + gdn_dt_bias[l])
        o_g = _gated_delta(gq, gk, gv, beta, g)
        o_g = o_g * lax.rsqrt(jnp.mean(o_g * o_g, axis=-1, keepdims=True) + RMS_EPS) * gdn_norm_g[l]
        y_gdn = o_g.astype(dt).reshape(b, s, GDN_W) * jax.nn.silu(gz)

        o_sb = _stick_breaking(heads(sq, SB_HEADS), heads(sk, SB_HEADS), heads(sv, SB_HEADS))
        y_sb = o_sb.reshape(b, s, SB_W) * jax.nn.silu(sz)

        y = jnp.concatenate([y_nsa, y_gdn, y_sb], axis=-1) @ w_out[l]
        x = _layernorm(DEEPNORM_ALPHA * x + (1.0 + gate[:, None, :]) * y, ln_g[l], ln_b[l])
    return x


_drawn_inputs = setup_inputs


def setup_inputs(seed=0):
    import zlib

    import numpy as np

    out = dict(_drawn_inputs(seed))
    spreads = {}
    factors = {'b_mod': 8.0,
     'cmp_pe_k': 30.329,
     'cmp_pe_v': 50.277,
     'cmp_w1_k': 6.625,
     'cmp_w2_k': 6.453,
     'gdn_norm_g': 8.0}
    for name, (base, spread) in spreads.items():
        noise = np.random.default_rng([zlib.crc32(name.encode()), seed]).standard_normal(out[name].shape)
        drawn = base * np.exp(spread * noise) if base else spread * noise
        out[name] = jnp.asarray(drawn.astype(out[name].dtype))
    for name, factor in factors.items():
        out[name] = (out[name] * factor).astype(out[name].dtype)
    return out
```

```python
from contextlib import ExitStack

import numpy as np

import concourse.bass as bass
from concourse import mybir

F32 = mybir.dt.float32
I32 = mybir.dt.int32
ALU = mybir.AluOpType
ACT = mybir.ActivationFunctionType
AX = mybir.AxisListType.X

P = 128
DEPTH, SEQ, DM, HD = 2, 512, 2048, 128
ROPE_HALF, ROPE_THETA = 16, 500000.0
KVH, GROUP, CMP_LEN, CMP_STRIDE = 2, 3, 32, 16
GDN_H, TAPS, CHUNK = 6, 4, 64
SB_H = 4
NSA_H = KVH * GROUP
NSA_W, KV_W, GDN_W, SB_W = 6 * HD, 2 * HD, 6 * HD, 4 * HD
N_CMP = (SEQ - CMP_LEN) // CMP_STRIDE + 1
SCALE = HD ** -0.5
ALPHA = (2 * DEPTH) ** 0.25
LN_EPS, RMS_EPS, NEG = 1e-5, 1e-6, -1e30
WIDTHS = (NSA_W, KV_W, KV_W, KV_W, KV_W, KV_W, KV_W, 18, NSA_W, GDN_W, GDN_W, GDN_W, 6, 6, GDN_W,
          SB_W, SB_W, SB_W, SB_W)
STARTS = [0]
for _w in WIDTHS:
    STARTS.append(STARTS[-1] + _w)
(C_NQ, C_KC, C_VC, C_KS, C_VS, C_KW, C_VW, C_NG, C_NZ, C_GQ, C_GK, C_GV, C_GB, C_GA, C_GZ,
 C_SQ, C_SK, C_SV, C_SZ, IN_COLS) = STARTS

KT = DM // P
TT = SEQ // P
NS = 4
SLOT = KT * P
MOD_J = 3
N_SMALL = 30
MIX_T = (NSA_W + GDN_W + SB_W) // P

MOD_LOADS = KT * MOD_J
GROUP_LOADS = 16
LOT = 4
COL_LOADS = KVH * GROUP_LOADS + (GDN_H + SB_H) * LOT
OUT_LOADS = 16
PE_LOADS = COL_LOADS + OUT_LOADS
LAYER_LOADS = MOD_LOADS + PE_LOADS
GROUP_TILES = 12
LAYER_TILES = KVH * GROUP_TILES + (GDN_H + SB_H) * LOT
LEVELS = (2, 4, 8, 16, 32)


SMALL = {"w_small": KT * N_SMALL, "w2": 2 * HD, "taps": TAPS * 18, "norm_g": 1, "pe": 2 * CMP_LEN,
         "dt_bias": GDN_H, "a_log": GDN_H}
SMALL_AT, SMALL_W = {}, 0
for _name, _w in SMALL.items():
    SMALL_AT[_name] = (SMALL_W, _w)
    SMALL_W += _w


def constants():
    r = np.arange(P)
    row, col = r[:, None], r[None, :]
    same = row // CHUNK == col // CHUNK
    blocks = {
        "ident": (row == col),
        "ones": np.ones((P, P)),
        "after": (row > col),
        "causal": np.where(col <= row, 0.0, NEG),
        "past": (row < col),
        "cumul": same & (row <= col),
        "chunk": same,
        "incl": same & (row >= col),
        "merge1": (row // 2 == col // 2) & (row % 2 == 1) & (col % 2 == 0),
    }
    for m in (1,) + LEVELS:
        lower = (row // (2 * m) == col // (2 * m)) & (row % (2 * m) >= m) & (col % (2 * m) < m)
        blocks[f"mergeT{m}"] = lower.T
    t = np.arange(TT)[None, :, None] * P + r[:, None, None]
    seen = (np.arange(N_CMP) * CMP_STRIDE + CMP_LEN - 1)[None, None, :] <= t
    blocks["cmp_add"] = np.where(seen, 0.0, NEG).reshape(P, -1)
    blocks["cmp_mul"] = seen.reshape(P, -1)
    rot = np.zeros((P, 2 * ROPE_HALF))
    for i in range(ROPE_HALF):
        rot[ROPE_HALF + i, i] = -1.0
        rot[i, ROPE_HALF + i] = 1.0
    blocks["rot"] = rot
    inv = np.float32(ROPE_THETA) ** (-np.arange(ROPE_HALF, dtype=np.float32) * np.float32(2.0)
                                     / np.float32(2 * ROPE_HALF))
    misc = np.zeros((P, 2))
    misc[:2 * ROPE_HALF, 0] = np.tile(inv, 2)
    blocks["misc"] = misc
    at, where = 0, {}
    for name, b in blocks.items():
        where[name] = (at, b.shape[1])
        at += b.shape[1]
    return np.concatenate([np.asarray(b, np.float32) for b in blocks.values()], 1), where


def build(nc, x, positions, c, b_mod, stream, small, lns, const, out, where, layers=DEPTH):
    ctx = ExitStack()
    with ctx:
        def sb(name, shape, dt=F32):
            return ctx.enter_context(nc.sbuf_tensor(name, shape, dt))

        xres = sb("xres", [P, TT, DM])
        hT = sb("hT", [P, KT, SEQ])
        yT = sb("yT", [P, MIX_T, SEQ])
        ring = sb("ring", [P, NS, SLOT])
        gateb = sb("gateb", [P, DM])
        cst = sb("cst", [P, const.shape[1]])
        rope_cs = sb("rope_cs", [2 * ROPE_HALF, 2, SEQ])
        raw = sb("raw", [P, LOT, TAPS - 1 + SEQ])
        arena = sb("arena", [P, 20, SEQ])
        state = sb("state", [P, HD])
        vnew = sb("vnew", [P, 2, HD])
        sm_all = sb("sm_all", [P, SMALL_W])
        cact = sb("cact", [P, 2, KT])
        modT = sb("modT", [P, 2, KT])
        ea = sb("ea", [P, GDN_H])
        gates = sb("gates", [P, TT, 18])
        gate_g = sb("gate_g", [P, TT, 9])
        coef = sb("coef", [P, 6, TT, GDN_H])
        coef_h = sb("coef_h", [P, 6, TT])
        conv_h = sb("conv_h", [P, TAPS, 3])
        tiny = sb("tiny", [P, 40])
        stats = sb("stats", [P, TT, 4, 6])
        meanvar = sb("meanvar", [P, TT, 2])
        cmpb = sb("cmpb", [P, 6, 32])
        vcmp = sb("vcmp", [P, HD])

        def C(name, parts=P):
            at, n = where[name]
            return cst[0:parts, at:at + n]

        def small_part(name):
            at, n = SMALL_AT[name]
            return sm_all[:, at:at + n]

        w_small = small_part("w_small").rearrange("p (k n) -> p k n", k=KT)
        w2 = small_part("w2").rearrange("p (a n) -> p a n", a=2)
        peT = small_part("pe").rearrange("p (a t) -> p a t", a=2)
        taps, gnorm = small_part("taps"), small_part("norm_g")
        ident, ones = C("ident"), C("ones")
        acc = yT[:, 0:MOD_J * DM // SEQ, :].rearrange("p a b -> p (a b)")
        ln_gb = hT[:, 0:2 * DM // SEQ, :].rearrange("p (a b) c -> p a (b c)", a=2)

        bank = [ctx.enter_context(nc.psum_tensor(f"bank{i}", [P, SEQ], F32)) for i in range(8)]
        PJ, SB_, TB, OB, MB = bank[0:2], bank[2:4], bank[4:6], bank[6], bank[7]

        def A(i, parts=P):
            return arena[0:parts, i, :]

        def tiles(ap):
            return ap.rearrange("p (t n) -> p t n", t=TT)

        def over(ap, shape):
            return ap.broadcast_to(shape)

        BIG = (P, TT, P)
        blocks_kv = [arena[:, 2 * i:2 * i + 2, :].rearrange("p a b -> p (a b)") for i in range(2)]
        prob, probT = [A(0), A(1)], [A(2), A(3)]
        kS, kW, vS, vW = A(4), A(5), A(6), A(7)
        qT, szq, z_raw, z_tanh = [A(8), A(9)], [A(10), A(11)], A(12), A(13)
        v_raw = [A(14), A(15)]
        rope_a, rope_b = A(16, 32), A(17, 32)
        cmp_s = A(18)[:, 0:TT * N_CMP].rearrange("p (t n) -> p t n", t=TT)
        cmp_p = A(18)[:, 256:256 + TT * N_CMP].rearrange("p (t n) -> p t n", t=TT)
        cmp_pT = A(19, N_CMP)

        semaphores = {}

        def S(name):
            if name not in semaphores:
                semaphores[name] = ctx.enter_context(nc.semaphore(name))
            return semaphores[name]

        CREDITS = {"mod_used": NS, "load_used": NS, "p_copied": 1, "rot_used": 1, "exp_done": 1,
                   "pt_ready": 1, "pv_done": 1, "y_ready": 1, "sz_ready": 1, "layer_done": 1,
                   "o_used": 8, "rec_vn": 1, "rec_state": 1, "gdn_lv_y": 1, "lb_ready": 1,
                   "sb_exp": 1, "sb_pv": 1}
        for i in range(LOT):
            CREDITS[f"raw_used{i}"] = 1

        def after(name, n):
            return n + CREDITS.get(name, 0)

        for name in CREDITS:
            S(name)
        for name in ["const_in", "x_in", "small_in", "ln_in", "slot_in0", "slot_in1", "slot_in2", "slot_in3"]:
            S(name)

        block = ctx.enter_context(nc.Block())

        REC = 5 + 2 * len(LEVELS) + 1
        GDN_STEPS = REC + 2 * (SEQ // CHUNK) + 1
        gdn_fill = [LOT * KT * (s + 1) // GDN_STEPS - LOT * KT * s // GDN_STEPS for s in range(GDN_STEPS)]
        SB_STEPS = TT + 2
        sb_fill = [LOT * KT * (s + 1) // SB_STEPS - LOT * KT * s // SB_STEPS for s in range(SB_STEPS)]
        NSA_STEPS = 11
        nsa_fill = [2 * KT * (s + 1) // NSA_STEPS - 2 * KT * s // NSA_STEPS for s in range(NSA_STEPS)]

        def ended(fill, s):
            return range(sum(fill[:s]) // KT, sum(fill[:s + 1]) // KT)

        def parts(fill, s):
            a, b = sum(fill[:s]), sum(fill[:s + 1])
            spans = [(i, max(a - i * KT, 0), min(b - i * KT, KT)) for i in range(sum(fill) // KT)]
            return [x for x in spans if x[1] < x[2]]

        def tile_of_lot(l, n):
            return l * LAYER_TILES + KVH * GROUP_TILES + n * LOT

        def load_of_lot(l, n):
            return l * PE_LOADS + KVH * GROUP_LOADS + n * LOT

        def turn(l, n4):
            return l * (LAYER_LOADS // NS) + MOD_LOADS // NS + n4

        @block.sync
        def _(sp):
            sp.dma_start(cst[:, :], const).then_inc(S("const_in"), 16)
            sp.dma_start(cact[:, 1, :], c[0].rearrange("(p k) -> p k", k=KT)).then_inc(S("const_in"), 16)
            sp.dma_start(A(0, 32).bitcast(I32), positions.broadcast_to((32, SEQ))).then_inc(S("const_in"), 16)
            sp.dma_start(xres[:, :, :], x[0].rearrange("(t p) n -> p t n", p=P)).then_inc(S("x_in"), 16)

            def load(l, n, slot):
                sp.dma_start(ring[:, slot, :], stream[bass.ds(l, 1), bass.ds(n, 1)].rearrange(
                    "a b p n -> (a b p) n")).then_inc(S(f"slot_in{slot}"), 16)

            with sp.Fori(0, layers) as l:
                sp.wait_ge(S("layer_done"), after("layer_done", l))
                one = bass.ds(l, 1)
                sp.dma_start(sm_all[:, :], small[one].rearrange("a p n -> (a p) n")).then_inc(S("small_in"), 16)
                sp.wait_ge(S("acc_zero"), l + 1)
                sp.dma_start(acc[0:1, :], b_mod[one, :]).then_inc(S("bmod_in"), 16)
                with sp.Fori(0, MOD_LOADS // NS) as n4:
                    for i in range(NS):
                        sp.wait_ge(S("mod_used"), l * MOD_LOADS + n4 * NS + i + 1)
                        load(l, n4 * NS + i, i)
                with sp.Fori(0, PE_LOADS // NS) as n4:
                    sp.wait_ge(S("mod_used"), after("mod_used", l * MOD_LOADS + MOD_LOADS))
                    for i in range(NS):
                        sp.wait_ge(S("load_used"), l * PE_LOADS + n4 * NS + i + 1)
                        load(l, n4 * NS + (MOD_LOADS + i), i)
                sp.wait_ge(S("load_used"), after("load_used", l * PE_LOADS + COL_LOADS))
                sp.dma_start(ln_gb[:, :, :].rearrange("p a n -> p (a n)"),
                             lns[one, :].broadcast_to((P, 2 * DM))).then_inc(S("ln_in"), 16)
            sp.wait_ge(S("layer_done"), after("layer_done", layers))
            sp.dma_start(out[0].rearrange("(t p) n -> p t n", p=P), xres[:, :, :]).then_inc(S("out_in"), 16)
            sp.wait_ge(S("out_in"), 16)

        @block.tensor
        def _(pe):
            mm, tr = pe.matmul, pe.transpose

            def each_tile(dst, lhs, rhs):
                for t in range(TT):
                    at = slice(t * P, (t + 1) * P)
                    last = mm(dst[:, at], lhs[:, at], rhs[:, at], start=True, stop=True)
                return last

            def transposes(dst, src):
                for t in range(TT):
                    at = slice(t * P, (t + 1) * P)
                    last = tr(dst[:, at], src[:, at], ident)
                return last

            def column_tile(tile, slot_turn, slot, b, k0, k1):
                for k in range(k0, k1):
                    if k == 0:
                        pe.wait_ge(S("p_copied"), tile)
                        pe.wait_ge(S(f"slot_in{slot}"), slot_turn * 16 + 16)
                    last = mm(PJ[b][:, :], ring[:, slot, k * P:(k + 1) * P], hT[:, k, :],
                              start=(k == 0), stop=(k == KT - 1))
                if k1 == KT:
                    last.then_inc(S("load_used"), 1)

            def lot_products(l, n, fill, s):
                for i, k0, k1 in parts(fill, s):
                    column_tile(tile_of_lot(l, n) + i, turn(l, KVH * GROUP_LOADS // NS + n), i, i % 2, k0, k1)

            pe.wait_ge(S("const_in"), 48)
            pe.wait_ge(S("x_in"), 16)
            with pe.Fori(0, layers) as l:
                pe.wait_ge(S("mod_sum"), l + 1)
                for k in range(2 * KT):
                    last = mm(MB[:, k:k + 1], acc[:, k * P:(k + 1) * P], ones[:, 0:1], start=True, stop=True)
                last.then_inc(S("mod_done"), 1)
                for n in range(TT):
                    last = mm(bank[n][:, :], ones, acc[:, 2 * DM + n * SEQ:2 * DM + (n + 1) * SEQ],
                              start=True, stop=True)
                last.then_inc(S("gate_done"), 1)
                pe.wait_ge(S("layer_done"), after("layer_done", l))
                for k in range(KT):
                    if k >= 2:
                        pe.wait_ge(S(("h_even", "h_odd")[k % 2]), l * (KT // 2) + k // 2)
                    for t in range(TT):
                        last = tr(TB[k % 2][:, t * P:(t + 1) * P], xres[:, t, k * P:(k + 1) * P], ident)
                    last.then_inc(S("xT_done"), 1)
                pe.wait_ge(S("h_even"), l * (KT // 2) + KT // 2)
                pe.wait_ge(S("h_odd"), l * (KT // 2) + KT // 2)
                pe.wait_ge(S("small_in"), l * 16 + 16)
                for k in range(KT):
                    last = mm(OB[0:N_SMALL, :], w_small[:, k, :], hT[:, k, :], start=(k == 0), stop=(k == KT - 1))
                last.then_inc(S("small_done"), 1)
                pe.wait_ge(S("mod_ready"), l + 1)
                pe.wait_ge(S("small_copied"), l + 1)
                for t in range(TT):
                    last = mm(MB[:, t * 32:t * 32 + N_SMALL], A(0, N_SMALL)[:, t * P:(t + 1) * P],
                              ident[0:N_SMALL, 0:N_SMALL], start=True, stop=True)
                last.then_inc(S("smallT_done"), 1)
                pe.wait_ge(S("g_ready"), l + 1)
                pe.wait_ge(S("gate_ready"), l + 1)
                g_all = coef[:, 0, :, :].rearrange("p t h -> p (t h)")
                mm(SB_[0][:, 0:24], C("cumul"), g_all, start=True, stop=True)
                mm(SB_[0][:, 24:48], C("chunk"), g_all, start=True, stop=True).then_inc(S("gc_done"), 1)

                with pe.Fori(0, KVH) as g:
                    G = l * KVH + g

                    def load_tile(load, tile, k0=0, k1=KT):
                        column_tile(l * LAYER_TILES + g * GROUP_TILES + tile,
                                    turn(l, g * (GROUP_LOADS // NS) + load // NS), load % NS, tile % 2, k0, k1)

                    def copied(tile):
                        pe.wait_ge(S("p_copied"), after("p_copied", l * LAYER_TILES + g * GROUP_TILES + tile + 1))

                    def compress(which):
                        pe.wait_ge(S("blocks_ready"), G * 2 + which + 1)
                        for half in range(2):
                            load = 2 + 2 * which + half
                            pe.wait_ge(S(f"slot_in{load % NS}"),
                                       turn(l, g * (GROUP_LOADS // NS) + load // NS) * 16 + 16)
                            for i in range(CMP_LEN // 2):
                                t = half * (CMP_LEN // 2) + i
                                last = mm(TB[which][:, 0:N_CMP], ring[:, load % NS, i * HD:(i + 1) * HD],
                                          blocks_kv[which][:, t * N_CMP:(t + 1) * N_CMP],
                                          start=(t == 0), stop=(t == CMP_LEN - 1))
                            last.then_inc(S("load_used"), 1)

                    def rotate(j, x):
                        pe.wait_ge(S("rot_used"), after("rot_used", G * 6 + j))
                        mm(MB[0:32, 0:x.shape[1]], C("rot"), x, start=True, stop=True)\
                            .then_inc(S("rot_done"), 1)

                    load_tile(0, 0)
                    load_tile(1, 1)
                    compress(0)
                    compress(1)
                    load_tile(6, 2)
                    pe.wait_ge(S("hid_ready"), G * 2 + 2)
                    mm(SB_[0][:, 0:N_CMP], w2[:, 0, :], cmpb[:, 2, 0:N_CMP], start=True, stop=True)
                    mm(SB_[1][0:N_CMP, 0:HD], cmpb[:, 3, 0:N_CMP], w2[:, 1, :],
                       start=True, stop=True).then_inc(S("cmp_done"), 1)
                    load_tile(7, 3)
                    pe.wait_ge(S("cmp_copied"), G + 1)
                    rotate(0, cmpb[:, 0, 0:N_CMP])
                    rotate(1, kS)
                    load_tile(8, 4)
                    copied(3)
                    transposes(TB[0], v_raw[0]).then_inc(S("vT_done"), 1)
                    load_tile(9, 5)
                    copied(4)
                    rotate(2, kW)
                    load_tile(10, 6)
                    copied(5)
                    transposes(TB[1], v_raw[1]).then_inc(S("vT_done"), 1)
                    load_tile(11, 7)
                    copied(6)
                    rotate(3, qT[0])
                    for r in range(GROUP):
                        H = G * GROUP + r
                        q = qT[r % 2]
                        for s in range(NSA_STEPS):
                            if r < GROUP - 1:
                                for i, k0, k1 in parts(nsa_fill, s):
                                    load_tile(12 + 2 * r + i, 8 + 2 * r + i, k0, k1)
                                if s == 8:
                                    copied(8 + 2 * r)
                                    rotate(4 + r, qT[(r + 1) % 2])
                            if s == 0:
                                pe.wait_ge(S("roped"), G * 6 + 4 + r)
                                pe.wait_ge(S("exp_done"), after("exp_done", H * 8))
                                for i in range(TT):
                                    last = mm(SB_[0][:, i * 32:i * 32 + N_CMP], q[:, i * P:(i + 1) * P],
                                              cmpb[:, 0, 0:N_CMP], start=True, stop=True)
                                last.then_inc(S("cmp_scores"), 1)
                            if 1 <= s <= 8:
                                u = s - 1
                                i, keys, w = u % TT, (kS, kW)[u // TT], (u % TT + 1) * P
                                if u == 1:
                                    pe.wait_ge(S("cmp_scored"), H + 1)
                                pe.wait_ge(S("exp_done"), after("exp_done", H * 8 + max(u - 1, 0)))
                                mm(SB_[(u + 1) % 2][:, 0:w], q[:, w - P:w], keys[:, 0:w], start=True, stop=False)
                                mm(SB_[(u + 1) % 2][:, w - P:w], ident, C("causal"),
                                   start=False, stop=True).then_inc(S("scores"), 1)
                            if s == 1:
                                pe.wait_ge(S("cmp_probs"), H + 1)
                                pe.wait_ge(S("pt_ready"), after("pt_ready", H * 8))
                                pe.wait_ge(S("v_ready"), G * 2 + 2)
                                for i in range(TT):
                                    last = tr(TB[0][0:N_CMP, i * P:(i + 1) * P], cmp_p[:, i, :], ident)
                                last.then_inc(S("cmp_pT"), 1)
                            if s == 2:
                                pe.wait_ge(S("cmp_pT_ready"), H + 1)
                                pe.wait_ge(S("y_ready"), after("y_ready", l * 16 + g * GROUP + r))
                                mm(OB[:, :], vcmp[0:N_CMP, :], cmp_pT, start=True, stop=False,
                                   skip_group_check=True)
                            if 2 <= s <= 9:
                                u = s - 2
                                pe.wait_ge(S("pt_ready"), after("pt_ready", H * 8 + max(u - 1, 0)))
                                pe.wait_ge(S("probs"), H * 8 + u + 1)
                                for j in range(u % TT + 1):
                                    last = tr(TB[(u + 1) % 2][:, j * P:(j + 1) * P],
                                              prob[u % 2][:, j * P:(j + 1) * P], ident)
                                last.then_inc(S("pt_done"), 1)
                            if 3 <= s <= 10:
                                u = s - 3
                                i, vals = u % TT, (vS, vW)[u // TT]
                                pe.wait_ge(S("pt_ready"), after("pt_ready", H * 8 + u + 1))
                                for j in range(i + 1):
                                    last = mm(OB[:, i * P:(i + 1) * P], vals[:, j * P:(j + 1) * P],
                                              probT[u % 2][:, j * P:(j + 1) * P], start=False,
                                              stop=(j == i), skip_group_check=True)
                                last.then_inc(S("pv_done"), 1)

                for s in range(LOT):
                    lot_products(l, 0, [KT] * LOT, s)

                with pe.Fori(0, GDN_H) as h:
                    D = l * GDN_H + h
                    n = D + 1

                    def ready(name):
                        pe.wait_ge(S(name), n)

                    for s in range(GDN_STEPS):
                        lot_products(l, h + 1, gdn_fill, s)
                        if s == 0:
                            ready("gdn_gsel")
                            pe.wait_ge(S("y_ready"), after("y_ready", l * 16 + NSA_H + h))
                            mm(MB[:, :], ones, A(3), start=True, stop=True).then_inc(S("gdn_gcb"), 1)
                        if s == 1:
                            ready("gdn_sqk")
                            mm(SB_[0][:, :], ones, A(1), start=True, stop=True).then_inc(S("gdn_nk"), 1)
                            ready("gdn_sqq")
                            mm(SB_[1][:, :], ones, A(9), start=True, stop=True).then_inc(S("gdn_nq"), 1)
                        if s == 2:
                            ready("gdn_k")
                            transposes(TB[0], A(0)).then_inc(S("gdn_kT"), 1)
                            each_tile(TB[1], A(0), A(0)).then_inc(S("gdn_kk"), 1)
                        if s == 3:
                            ready("gdn_q")
                            each_tile(SB_[0], A(6), A(0)).then_inc(S("gdn_qk"), 1)
                            ready("gdn_v")
                            transposes(SB_[1], A(8)).then_inc(S("gdn_vT"), 1)
                            ready("gdn_lower")
                            transposes(TB[0], A(3)).then_inc(S("gdn_lT"), 1)
                        if s == 4:
                            ready("gdn_intra")
                            transposes(MB, A(10)).then_inc(S("gdn_iT"), 1)
                        for v in range(len(LEVELS)):
                            if s == 5 + 2 * v:
                                pe.wait_ge(S("gdn_ct"), D * 6 + v + 2)
                                pe.wait_ge(S("gdn_T"), D * 5 + v + 1)
                                if v == 0:
                                    ready("gdn_lT_copied")
                                each_tile(TB[0], A(15 - v % 2), A(11)).then_inc(S("gdn_CT"), 1)
                            if s == 6 + 2 * v:
                                pe.wait_ge(S("gdn_lv_y"), after("gdn_lv_y", D * 5 + v + 1))
                                if v == 0:
                                    ready("gdn_bv")
                                if v < len(LEVELS) - 1:
                                    each_tile(SB_[0], A(13), A(17))
                                each_tile(SB_[1], A(17), A(13)).then_inc(S("gdn_TCT"), 1)
                        if s == REC - 1:
                            pe.wait_ge(S("gdn_T"), D * 5 + 5)
                            pe.wait_ge(S("gdn_Tt"), n)
                            each_tile(TB[1], A(1), A(13)).then_inc(S("gdn_w"), 1)
                        if REC <= s < GDN_STEPS - 1:
                            i, second = (s - REC) // 2, (s - REC) % 2
                            t, half = i // 2, i % 2
                            at = slice(i * CHUNK, (i + 1) * CHUNK)
                            rows = slice(half * CHUNK, (half + 1) * CHUNK)
                            if not second:
                                if i == 0:
                                    ready("gdn_w_copied")
                                    ready("gdn_qh")
                                    ready("gdn_i_copied")
                                pe.wait_ge(S("rec_state"), after("rec_state", D * 9 + i + 1))
                                mm(SB_[half][rows, 0:HD], A(13)[:, at], A(8)[:, t * P:(t + 1) * P],
                                   start=True, stop=False)
                                mm(SB_[half][rows, 0:HD], A(18)[:, at], state[:, :],
                                   start=False, stop=True).then_inc(S("rec_v"), 1)
                                mm(OB[:, at], state[:, :], A(6)[:, at], start=True, stop=False)
                            else:
                                pe.wait_ge(S("rec_vn"), after("rec_vn", D * 8 + i + 1))
                                mm(TB[half][:, 0:HD], A(9)[:, t * P:(t + 1) * P], vnew[:, half, :],
                                   start=True, stop=True).then_inc(S("rec_kv"), 1)
                                last = mm(OB[:, at], vnew[:, half, :], A(16)[:, at], start=False, stop=True)
                                if i == SEQ // CHUNK - 1:
                                    last.then_inc(S("gdn_o"), 1)
                        if s == GDN_STEPS - 1:
                            ready("gdn_osq")
                            mm(SB_[0][:, :], ones, A(14), start=True, stop=True).then_inc(S("gdn_no"), 1)

                def stick(h, lot):
                    B = l * SB_H + h
                    for s in range(SB_STEPS):
                        if lot is not None:
                            lot_products(l, lot, sb_fill, s)
                        if s == 0:
                            pe.wait_ge(S("y_ready"), after("y_ready", l * 16 + NSA_H + GDN_H + h))
                            pe.wait_ge(S("p_copied"), after("p_copied", tile_of_lot(l, GDN_H + h) + 3))
                            transposes(MB, raw[:, 2, TAPS - 1:]).then_inc(S("sb_vT"), 1)
                            pe.wait_ge(S("sb_qk"), B + 1)
                        if s < TT:
                            j = TT - 1 - s
                            w = SEQ - j * P
                            pe.wait_ge(S("lb_ready"), after("lb_ready", B * TT + max(s - 1, 0)))
                            mm(SB_[s % 2][:, 0:w], A(0)[:, j * P:(j + 1) * P], A(1)[:, j * P:],
                               start=True, stop=True).then_inc(S("sb_z"), 1)
                        if 1 <= s <= TT:
                            j = TT - s
                            w = SEQ - j * P
                            pe.wait_ge(S("spm_ready"), B * TT + s)
                            b = TB[(s - 1) % 2]
                            mm(b[:, 0:w], C("after"), A(9 + j)[:, 0:w], start=True, stop=(s == 1))
                            for m in range(j + 1, TT):
                                last = mm(b[:, (m - j) * P:w], ones, A(9 + m)[:, 0:SEQ - m * P],
                                          start=False, stop=(m == TT - 1))
                            if s == 1:
                                last = None
                            if last is None:
                                pe.drain().then_inc(S("sb_acc"), 1)
                            else:
                                last.then_inc(S("sb_acc"), 1)
                        if 2 <= s <= TT + 1:
                            j = TT + 1 - s
                            pe.wait_ge(S("sb_a"), B * TT + s - 1)
                            if s == 2:
                                pe.wait_ge(S("sb_v"), B + 1)
                            last = mm(OB[:, j * P:], A(2)[:, j * P:(j + 1) * P], A(15 + s % 2)[:, 0:SEQ - j * P],
                                      start=(s == 2), stop=(s == TT + 1), skip_group_check=True)
                            last.then_inc(S("sb_pv"), 1)

                with pe.Fori(0, SB_H - 1) as h:
                    stick(h, h + (GDN_H + 1))
                stick(SB_H - 1, None)

                with pe.Fori(0, TT // 2) as n2:
                    pe.wait_ge(S("y_ready"), after("y_ready", l * 16 + 16))
                    for e in range(2):
                        outs = (bank[2:6], [bank[0], bank[1], bank[6], bank[7]])[e]
                        for k4 in range(NS):
                            pe.wait_ge(S(f"slot_in{k4}"), turn(l, COL_LOADS // NS + n2 * 2 + e) * 16 + 16)
                            for t in range(TT):
                                if k4 == 0:
                                    pe.wait_ge(S("o_used"), l * 16 + n2 * 8 + (e * 4 + t + 1))
                                for k in range(4):
                                    kk = k4 * 4 + k
                                    last = mm(outs[t][:, :], yT[:, kk, t * P:(t + 1) * P],
                                              ring[:, k4, k * SEQ:(k + 1) * SEQ],
                                              start=(kk == 0), stop=(kk == KT - 1))
                                if k4 == NS - 1 and t < TT - 1:
                                    last.then_inc(S("o_done"), 1)
                            if k4 == NS - 1:
                                last.then_inc(S("load_used"), 1)
                            else:
                                last.then_inc(S("load_used"), 1)

        @block.scalar
        def _(act):
            def fn(*args, **kw):
                made = act.activation(*args, **kw)
                act.drain()
                return made

            def copy_tile(l_load, dst, b):
                act.wait_ge(S("load_used"), after("load_used", l_load + 1))
                fn(dst, PJ[b][:, :], ACT.Copy).then_inc(S("p_copied"), 1)

            def copy_lot(l, n, i):
                act.wait_ge(S(f"raw_used{i}"), after(f"raw_used{i}", l * (GDN_H + SB_H) + n))
                copy_tile(load_of_lot(l, n) + i, raw[:, i, TAPS - 1:], i % 2)

            act.wait_ge(S("const_in"), 48)
            fn(cact[:, 0, :], cact[:, 1, :], ACT.Tanh, scale=0.5).then_inc(S("c_tanh"), 1)
            act.wait_ge(S("angles"), 1)
            fn(rope_cs[:, :, :], arena[0:32, 4:6, :], ACT.Sin).then_inc(S("rope_ready"), 1)
            with act.Fori(0, layers) as l:
                for k in range(1, KT, 2):
                    if k == 1:
                        act.wait_ge(S("mod_ready"), l + 1)
                    act.wait_ge(S("xT_done"), l * KT + k + 1)
                    fn(hT[:, k, :], TB[1][:, :], ACT.Identity, scale=modT[:, 1, k:k + 1],
                       bias=modT[:, 0, k:k + 1]).then_inc(S("h_odd"), 1)
                act.wait_ge(S("small_done"), l + 1)
                fn(A(0, N_SMALL), OB[0:N_SMALL, :], ACT.Copy).then_inc(S("small_copied"), 1)
                act.wait_ge(S("smallT_done"), l + 1)
                small = MB[:, 0:TT * 32].rearrange("p (t n) -> p t n", t=TT)
                th = A(1)[:, 0:TT * 24].rearrange("p (t n) -> p t n", t=TT)
                fn(th, small[:, :, 0:24], ACT.Tanh, scale=0.5).then_inc(S("gates_tanh"), 1)
                act.wait_ge(S("ga_ready"), l + 1)
                fn(A(2)[:, 32:56], A(2)[:, 0:24], ACT.Abs)
                fn(ea[:, :], small_part("a_log"), ACT.Exp)
                fn(A(2)[:, 64:88], A(2)[:, 32:56], ACT.Exp, scale=-1.0)
                fn(A(2)[:, 96:120], A(2)[:, 64:88], ACT.Ln, bias=1.0).then_inc(S("ga_ln"), 1)
                act.wait_ge(S("gc_ready"), l + 1)
                fn(A(2)[:, 128:152], coef[:, 3, :, :].rearrange("p t h -> p (t h)"), ACT.Exp)
                fn(coef[:, 5, :, :].rearrange("p t h -> p (t h)"), A(2)[:, 160:184], ACT.Exp)\
                    .then_inc(S("gc_exp"), 1)
                act.wait_ge(S("coef_ready"), l + 1)

                with act.Fori(0, KVH) as g:
                    G = l * KVH + g

                    def copy_group(load, dst, b):
                        copy_tile(l * PE_LOADS + g * GROUP_LOADS + load, dst, b)

                    def copy_z(load, H):
                        act.wait_ge(S("load_used"), after("load_used", l * PE_LOADS + g * GROUP_LOADS + load + 1))
                        act.wait_ge(S("sz_ready"), after("sz_ready", H))
                        fn(z_raw, PJ[1][:, :], ACT.Copy)
                        fn(z_tanh, PJ[1][:, :], ACT.Tanh, scale=0.5)
                        act.drain().then_inc(S("p_copied"), 1)
                        act.sem_inc(S("z_tanh"), 1)

                    copy_group(0, v_raw[0], 0)
                    copy_group(1, v_raw[1], 1)
                    for which in range(2):
                        act.wait_ge(S("load_used"), after("load_used", l * PE_LOADS + g * GROUP_LOADS + 4 + 2 * which))
                        fn(cmpb[:, 4 + which, 0:N_CMP], TB[which][:, 0:N_CMP], ACT.Tanh, scale=0.5)\
                            .then_inc(S("cmp_tanh"), 1)
                    copy_group(6, kS, 0)
                    act.wait_ge(S("cmp_done"), G + 1)
                    fn(cmpb[:, 0, 0:N_CMP], SB_[0][:, 0:N_CMP], ACT.Copy)
                    fn(vcmp[0:N_CMP, :], SB_[1][0:N_CMP, 0:HD], ACT.Copy)
                    act.drain().then_inc(S("cmp_copied"), 1)
                    copy_group(7, v_raw[0], 1)
                    copy_group(8, kW, 0)
                    act.wait_ge(S("vT_done"), G * 2 + 1)
                    fn(vS, TB[0][:, :], ACT.Copy).then_inc(S("v_ready"), 1)
                    copy_group(9, v_raw[1], 1)
                    copy_group(10, qT[0], 0)
                    act.wait_ge(S("vT_done"), G * 2 + 2)
                    fn(vW, TB[1][:, :], ACT.Copy).then_inc(S("v_ready"), 1)
                    copy_z(11, G * GROUP)
                    for r in range(GROUP):
                        H = G * GROUP + r
                        for s in range(NSA_STEPS):
                            if r < GROUP - 1:
                                for i in ended(nsa_fill, s):
                                    if i == 0:
                                        copy_group(12 + 2 * r, qT[(r + 1) % 2], 0)
                                    else:
                                        copy_z(13 + 2 * r, H + 1)
                            if s == 0:
                                act.wait_ge(S("cmp_scored2"), H + 1)
                                fn(cmp_s, cmp_s, ACT.Exp).then_inc(S("cmp_exp"), 1)
                            if 1 <= s <= 8:
                                u = s - 1
                                w = (u % TT + 1) * P
                                act.wait_ge(S("max_ready"), H * 8 + u + 1)
                                fn(prob[u % 2][:, 0:w], SB_[(u + 1) % 2][:, 0:w], ACT.Exp, scale=SCALE,
                                   bias=tiny[:, u:u + 1], accum_out=tiny[:, 8 + u:9 + u]).then_inc(S("exp_done"), 1)
                            if 2 <= s <= 9:
                                u = s - 2
                                w = (u % TT + 1) * P
                                act.wait_ge(S("pt_done"), H * 8 + u + 1)
                                act.wait_ge(S("pv_done"), after("pv_done", H * 8 + max(u - 1, 0)))
                                fn(probT[u % 2][:, 0:w], TB[(u + 1) % 2][:, 0:w], ACT.Copy)\
                                    .then_inc(S("pt_ready"), 1)

                for i in range(LOT):
                    copy_lot(l, 0, i)

                with act.Fori(0, GDN_H) as h:
                    D = l * GDN_H + h
                    n = D + 1

                    def ready(name):
                        act.wait_ge(S(name), n)

                    for s in range(GDN_STEPS):
                        for i in ended(gdn_fill, s):
                            copy_lot(l, h + 1, i)
                        if s == 0:
                            for i, th in enumerate((1, 9, 10)):
                                act.wait_ge(S("gdn_conv"), D * 3 + i + 1)
                                fn(A(th), A((0, 6, 8)[i]), ACT.Tanh, scale=0.5).then_inc(S("gdn_tanh"), 1)
                            fn(A(11), raw[:, 3, TAPS - 1:], ACT.Tanh, scale=0.5).then_inc(S("gdn_ztanh"), 1)
                            ready("gdn_d")
                            fn(A(4), MB[:, :], ACT.Exp).then_inc(S("gdn_egb"), 1)
                            fn(A(5), A(5), ACT.Exp, scale=-1.0).then_inc(S("gdn_decay"), 1)
                            act.wait_ge(S("gdn_silu"), D * 3 + 1)
                            fn(A(1), A(0), ACT.Square).then_inc(S("gdn_sqk"), 1)
                            act.wait_ge(S("gdn_silu"), D * 3 + 2)
                            fn(A(9), A(6), ACT.Square).then_inc(S("gdn_sqq"), 1)
                        if s == 1:
                            ready("gdn_nk")
                            fn(A(2), SB_[0][:, :], ACT.Ln, scale=0.25, bias=tiny[:, 32:33])
                            ready("gdn_nq")
                            fn(A(7), SB_[1][:, :], ACT.Ln, scale=0.25, bias=tiny[:, 32:33])
                            fn(A(2), A(2), ACT.Exp, scale=-0.5, bias=tiny[:, 34:35]).then_inc(S("gdn_rk"), 1)
                            fn(A(7), A(7), ACT.Exp, scale=-0.5, bias=tiny[:, 35:36]).then_inc(S("gdn_rq"), 1)
                        if s == 3:
                            ready("gdn_lT")
                            fn(A(12), TB[0][:, :], ACT.Copy).then_inc(S("gdn_lT_copied"), 1)
                        if s == 4:
                            ready("gdn_iT")
                            fn(A(16), MB[:, :], ACT.Copy).then_inc(S("gdn_i_copied"), 1)
                        for v in range(len(LEVELS)):
                            if s == 5 + 2 * v:
                                act.wait_ge(S("gdn_CT"), D * 5 + v + 1)
                                fn(A(17), TB[0][:, :], ACT.Copy).then_inc(S("gdn_lv_y"), 1)
                        if s == REC - 1:
                            ready("gdn_w")
                            fn(A(18), TB[1][:, :], ACT.Copy, scale=-1.0).then_inc(S("gdn_w_copied"), 1)
                        if REC <= s < GDN_STEPS - 1 and (s - REC) % 2 == 0:
                            i = (s - REC) // 2
                            rows = slice(i % 2 * CHUNK, (i % 2 + 1) * CHUNK)
                            act.wait_ge(S("rec_v"), D * 8 + i + 1)
                            fn(vnew[rows, i % 2, :], SB_[i % 2][rows, 0:HD], ACT.Copy).then_inc(S("rec_vn"), 1)
                        if s == GDN_STEPS - 1:
                            ready("gdn_o")
                            fn(A(14), OB[:, :], ACT.Square).then_inc(S("gdn_osq"), 1)
                            ready("gdn_no")
                            fn(A(15), SB_[0][:, :], ACT.Ln, scale=1.0 / HD, bias=tiny[:, 32:33])
                            fn(A(15), A(15), ACT.Exp, scale=-0.5, bias=tiny[:, 34:35]).then_inc(S("gdn_ro"), 1)

                def stick(h, lot):
                    B = l * SB_H + h
                    for s in range(SB_STEPS):
                        if lot is not None:
                            for i in ended(sb_fill, s):
                                copy_lot(l, lot, i)
                        if s == 0:
                            act.wait_ge(S("y_ready"), after("y_ready", l * 16 + NSA_H + GDN_H + h))
                            fn(A(4), raw[:, 3, TAPS - 1:], ACT.Tanh, scale=0.5).then_inc(S("sb_ztanh"), 1)
                        if s < TT:
                            w = (s + 1) * P
                            act.wait_ge(S("sb_z"), B * TT + s + 1)
                            e = A(5 + s % 2)[:, 0:w]
                            fn(e, SB_[s % 2][:, 0:w], ACT.Abs)
                            fn(e, e, ACT.Exp, scale=-1.0)
                            fn(e, e, ACT.Ln, bias=1.0).then_inc(S("sb_ln"), 1)
                        if 1 <= s <= TT:
                            w = s * P
                            act.wait_ge(S("sb_arg"), B * TT + s)
                            act.wait_ge(S("sb_pv"), after("sb_pv", B * TT + max(s - 2, 0)))
                            fn(A(16 - s % 2)[:, 0:w], A(13 + (s - 1) % 2)[:, 0:w], ACT.Exp).then_inc(S("sb_exp"), 1)

                with act.Fori(0, SB_H - 1) as h:
                    stick(h, h + (GDN_H + 1))
                stick(SB_H - 1, None)
                act.wait_ge(S("var_ready"), l + 1)
                fn(tiny[:, 16:20], meanvar[:, :, 1], ACT.Ln, bias=tiny[:, 33:34])
                fn(tiny[:, 20:24], tiny[:, 16:20], ACT.Exp, scale=-0.5).then_inc(S("rstd_ready"), 1)

        @block.gpsimd
        def _(pool):
            for name, n in CREDITS.items():
                pool.sem_inc(S(name), n)
            pool.memset(raw[:, :, 0:TAPS - 1], 0.0)
            pool.memset(vnew[:, :, :], 0.0)
            for i, v in enumerate((RMS_EPS, LN_EPS, float(np.log(0.5)), float(np.log(0.5 * SCALE)))):
                pool.memset(tiny[:, 32 + i:33 + i], v)
            pool.drain().then_inc(S("pool_ready"), 1)
            pool.wait_ge(S("const_in"), 48)
            with pool.Fori(0, layers) as l:
                with pool.Fori(0, GDN_H) as h:
                    D = l * GDN_H + h
                    pool.wait_ge(S("gdn_lT_copied"), D + 1)
                    for v, m in enumerate((1,) + LEVELS):
                        if v >= 2:
                            pool.wait_ge(S("gdn_T" if v == 2 else "gdn_CT"), D * 5 + (1 if v == 2 else v - 2))
                        pool.tensor_tensor(tiles(A(14 + v % 2)), tiles(A(12)),
                                           over(C(f"mergeT{m}").unsqueeze(1), BIG), ALU.mult)\
                            .then_inc(S("gdn_ct"), 1)

        @block.vector
        def _(dve):
            def drained(op):
                def run(*args, **kw):
                    made = op(*args, **kw)
                    dve.drain()
                    return made
                return run

            tt, ts, stt, cp, reduce, reciprocal, bn_stats, bn_aggr, fill = map(drained, (
                dve.tensor_tensor, dve.tensor_scalar, dve.scalar_tensor_tensor, dve.tensor_copy,
                dve.tensor_reduce, dve.reciprocal, dve.bn_stats, dve.bn_aggr, dve.memset))
            M, Ad, Su, Mx = ALU.mult, ALU.add, ALU.subtract, ALU.max
            sync = dve.drain

            dve.wait_ge(S("const_in"), 48)
            dve.wait_ge(S("pool_ready"), 1)
            cp(A(1, 32), A(0, 32).bitcast(I32))
            ts(A(2, 32), A(1, 32), C("misc", 32)[:, 0:1], None, M)
            two_pi = 2 * np.pi
            c1 = 6.28125
            c2 = float(np.float32(two_pi - c1))
            c3 = float(two_pi - c1 - c2)
            for i, phase in enumerate((np.pi / 2, 0.0)):
                n, r = A(3, 32), A(4 + i, 32)
                ts(n, A(2, 32), float(1 / two_pi), float(phase / two_pi), M, Ad)
                ts(n, n, 12582912.0, None, Ad)
                ts(n, n, 12582912.0, None, Su)
                stt(r, n, -c1, A(2, 32), M, Ad)
                stt(r, n, -c2, r, M, Ad)
                stt(r, n, -c3, r, M, Ad)
                ts(r, r, float(phase), None, Ad)
                ts(r, r, 3.1415925, -3.1415925, ALU.min, Mx)
            sync().then_inc(S("angles"), 1)
            dve.wait_ge(S("c_tanh"), 1)
            stt(cact[:, 1, :], cact[:, 0, :], 1.0, cact[:, 1, :], Ad, M)
            ts(cact[:, 1, :], cact[:, 1, :], 0.5, None, M)

            def rope(j_count, x32, n, at):
                dve.wait_ge(S("rot_done"), j_count + 1)
                tt(rope_a[:, 0:n], MB[0:32, 0:n], rope_cs[:, 1, at], M).then_inc(S("rot_used"), 1)
                tt(rope_b[:, 0:n], x32, rope_cs[:, 0, at], M)
                tt(x32, rope_a[:, 0:n], rope_b[:, 0:n], Ad).then_inc(S("roped"), 1)

            with dve.Fori(0, layers) as l:
                dve.wait_ge(S("load_used"), after("load_used", l * PE_LOADS))
                fill(acc, 0.0).then_inc(S("acc_zero"), 1)
                with dve.Fori(0, KT // 4) as k4:
                    dve.wait_ge(S("bmod_in"), l * 16 + 16)
                    for i in range(4 * MOD_J):
                        j, dk = i % MOD_J, i // MOD_J
                        part = acc[:, j * DM:(j + 1) * DM]
                        dve.wait_ge(S(f"slot_in{i % NS}"),
                                    (l * (LAYER_LOADS // NS) + k4 * MOD_J + (i // NS + 1)) * 16)
                        stt(part, ring[:, i % NS, :], cact[:, 1, bass.ds(k4 * 4 + dk, 1)], part, M, Ad)\
                            .then_inc(S("mod_used"), 1)
                sync().then_inc(S("mod_sum"), 1)
                dve.wait_ge(S("mod_done"), l + 1)
                cp(modT[:, 0, :], MB[:, 0:KT])
                ts(modT[:, 1, :], MB[:, KT:2 * KT], 1.0, None, Ad)
                sync().then_inc(S("mod_ready"), 1)
                dve.wait_ge(S("gate_done"), l + 1)
                for n in range(TT):
                    ts(gateb[:, n * SEQ:(n + 1) * SEQ], bank[n][:, :], 1.0, None, Ad)
                sync().then_inc(S("gate_ready"), 1)
                for k in range(0, KT, 2):
                    dve.wait_ge(S("xT_done"), l * KT + k + 1)
                    ts(hT[:, k, :], TB[0][:, :], modT[:, 1, k:k + 1], modT[:, 0, k:k + 1], M, Ad)\
                        .then_inc(S("h_even"), 1)
                dve.wait_ge(S("gates_tanh"), l + 1)
                small = MB[:, 0:TT * 32].rearrange("p (t n) -> p t n", t=TT)
                th = A(1)[:, 0:TT * 24].rearrange("p (t n) -> p t n", t=TT)
                ga = A(2)[:, 0:24].rearrange("p (t h) -> p t h", t=TT)
                small_shape = (P, TT, GDN_H)
                tt(ga, small[:, :, 24:30], over(small_part("dt_bias").unsqueeze(1), small_shape), Ad).then_inc(S("ga_ready"), 1)
                ts(gates[:, :, :], th[:, :, 0:18], 0.5, 0.5, M, Ad)
                ts(coef[:, 1, :, :], th[:, :, 18:24], 0.5, 0.5, M, Ad)
                dve.wait_ge(S("ga_ln"), l + 1)
                ln = A(2)[:, 96:120].rearrange("p (t h) -> p t h", t=TT)
                sp_ = A(2)[:, 192:216].rearrange("p (t h) -> p t h", t=TT)
                stt(sp_, ga, 0.0, ln, Mx, Ad)
                ts(coef[:, 2, :, :], coef[:, 1, :, :], 0.5, None, M)
                stt(coef[:, 0, :, :], sp_, -1.0, over(ea[:, :].unsqueeze(1), small_shape), M, M).then_inc(S("g_ready"), 1)
                dve.wait_ge(S("gc_done"), l + 1)
                gc = coef[:, 3, :, :].rearrange("p t h -> p (t h)")
                cp(gc, SB_[0][:, 0:24])
                tt(A(2)[:, 160:184], SB_[0][:, 24:48], gc, Su)
                sync().then_inc(S("gc_ready"), 1)
                dve.wait_ge(S("gc_exp"), l + 1)
                tt(coef[:, 4, :, :].rearrange("p t h -> p (t h)"), coef[:, 1, :, :].rearrange("p t h -> p (t h)"),
                   A(2)[:, 128:152], M)
                sync().then_inc(S("coef_ready"), 1)
                dve.wait_ge(S("rope_ready"), 1)

                with dve.Fori(0, KVH) as g:
                    G = l * KVH + g
                    cp(gate_g[:, :, :], gates[:, :, bass.ds(g * 9, 9)])
                    for which in range(2):
                        dve.wait_ge(S("p_copied"), after("p_copied", l * LAYER_TILES + g * GROUP_TILES + which + 1))
                        src = v_raw[which]
                        windows = bass.AP(src.tensor, src.offset, [src.ap[0], [1, CMP_LEN], [CMP_STRIDE, N_CMP]])
                        tt(blocks_kv[which][:, 0:CMP_LEN * N_CMP].rearrange("p (t n) -> p t n", n=N_CMP), windows,
                           over(peT[:, which, :].unsqueeze(2), (P, CMP_LEN, N_CMP)), Ad).then_inc(S("blocks_ready"), 1)
                    for which in range(2):
                        dve.wait_ge(S("cmp_tanh"), G * 2 + which + 1)
                        hid = cmpb[:, 2 + which, 0:N_CMP]
                        stt(hid, cmpb[:, 4 + which, 0:N_CMP], 1.0, TB[which][:, 0:N_CMP], Ad, M)
                        ts(hid, hid, 0.5, None, M).then_inc(S("hid_ready"), 1)
                    first = CMP_LEN - 1
                    rope(G * 6, cmpb[0:32, 0, 0:N_CMP], N_CMP, slice(first, first + (N_CMP - 1) * CMP_STRIDE + 1, CMP_STRIDE))
                    rope(G * 6 + 1, kS[0:32, :], SEQ, slice(0, SEQ))
                    rope(G * 6 + 2, kW[0:32, :], SEQ, slice(0, SEQ))
                    rope(G * 6 + 3, qT[0][0:32, :], SEQ, slice(0, SEQ))

                    def silu_z(H, dst):
                        dve.wait_ge(S("z_tanh"), H + 1)
                        stt(dst, z_tanh, 1.0, z_raw, Ad, M).then_inc(S("sz_ready"), 1)

                    silu_z(G * GROUP, szq[0])
                    for r in range(GROUP):
                        H = G * GROUP + r
                        for s in range(NSA_STEPS):
                            if s == 0:
                                dve.wait_ge(S("cmp_scores"), H + 1)
                                shape = (P, TT, N_CMP)
                                mx, sm = tiny[:, 24:28], tiny[:, 28:32]
                                scores = SB_[0][:, 0:TT * 32].rearrange("p (t n) -> p t n", t=TT)[:, :, 0:N_CMP]
                                stt(cmp_s, scores, SCALE, C("cmp_add").rearrange("p (t n) -> p t n", t=TT), M, Ad)\
                                    .then_inc(S("cmp_scored"), 1)
                                reduce(mx, cmp_s, AX, Mx)
                                tt(cmp_s, cmp_s, over(mx.unsqueeze(2), shape), Su).then_inc(S("cmp_scored2"), 1)
                                dve.wait_ge(S("cmp_exp"), H + 1)
                                tt(cmp_s, cmp_s, C("cmp_mul").rearrange("p (t n) -> p t n", t=TT), M)
                                reduce(sm, cmp_s, AX, Ad)
                                ts(sm, sm, 1e-30, None, Mx)
                                reciprocal(sm, sm)
                                tt(sm, sm, gate_g[:, :, 3 * r], M)
                                tt(cmp_p, cmp_s, over(sm.unsqueeze(2), shape), M).then_inc(S("cmp_probs"), 1)
                            if 1 <= s <= 8:
                                u = s - 1
                                i, w, b = u % TT, (u % TT + 1) * P, SB_[(u + 1) % 2]
                                dve.wait_ge(S("scores"), H * 8 + u + 1)
                                reduce(tiny[:, 30:31], b[:, 0:w], AX, Mx)
                                ts(tiny[:, u:u + 1], tiny[:, 30:31], -SCALE, None, M).then_inc(S("max_ready"), 1)
                                if s == 1:
                                    dve.wait_ge(S("cmp_pT"), H + 1)
                                    cp(cmp_pT, TB[0][0:N_CMP, :]).then_inc(S("cmp_pT_ready"), 1)
                                dve.wait_ge(S("exp_done"), after("exp_done", H * 8 + u + 1))
                                reciprocal(tiny[:, 31:32], tiny[:, 8 + u:9 + u])
                                ts(prob[u % 2][:, 0:w], prob[u % 2][:, 0:w], tiny[:, 31:32],
                                   gate_g[:, i, 3 * r + 1 + u // TT:3 * r + 2 + u // TT], M, M).then_inc(S("probs"), 1)
                            if s == 8 and r < GROUP - 1:
                                rope(G * 6 + 4 + r, qT[(r + 1) % 2][0:32, :], SEQ, slice(0, SEQ))
                        if r < GROUP - 1:
                            silu_z(H + 1, szq[(r + 1) % 2])
                        dve.wait_ge(S("pv_done"), after("pv_done", H * 8 + 8))
                        stt(yT[:, bass.ds(g * GROUP + r, 1), :].rearrange("p a n -> p (a n)"), OB[:, :], 0.5,
                            szq[r % 2], M, M).then_inc(S("y_ready"), 1)

                with dve.Fori(0, GDN_H) as h:
                    D = l * GDN_H + h

                    def ready(name):
                        dve.wait_ge(S(name), D + 1)

                    cp(coef_h[:, :, :], coef[:, :, :, bass.ds(h, 1)].rearrange("p a t h -> p (a t) h").rearrange(
                        "p (a t) h -> p a (t h)", t=TT))
                    conv_heads = taps.rearrange("p (k h) -> p k h", h=GDN_H)
                    cp(conv_h[:, :, :].rearrange("p t x -> p (t x)"),
                       conv_heads[:, :, bass.ds(h, 1)].rearrange("p k h -> p (k h)"))
                    fill(state[:, :], 0.0)
                    sync().then_inc(S("rec_state"), 1)
                    per_token = lambda i: over(coef_h[:, i, :].unsqueeze(2), BIG)
                    tt(tiles(A(3)), over(C("cumul").unsqueeze(1), BIG), per_token(0), M).then_inc(S("gdn_gsel"), 1)
                    for i, (src, dst, part) in enumerate(((0, 0, 1), (1, 6, 0), (2, 8, 2))):
                        dve.wait_ge(S("p_copied"), after("p_copied", tile_of_lot(l, h) + src + 1))
                        for k in range(TAPS):
                            tap, x_ = conv_h[:, k, part:part + 1], raw[:, src, k:k + SEQ]
                            if k == 0:
                                ts(A(dst), x_, tap, None, M)
                            else:
                                stt(A(dst), x_, tap, A(dst), M, Ad)
                        sync().then_inc(S("gdn_conv"), 1)
                        dve.sem_inc(S(f"raw_used{src}"), 1)
                    for i, (x_, th) in enumerate(((0, 1), (6, 9), (8, 10))):
                        dve.wait_ge(S("gdn_tanh"), D * 3 + i + 1)
                        stt(A(x_), A(th), 1.0, A(x_), Ad, M).then_inc(S("gdn_silu"), 1)
                    sync().then_inc(S("gdn_v"), 1)
                    ready("gdn_gcb")
                    tt(tiles(A(5)), tiles(MB[:, :]), per_token(3), Su)
                    ts(A(5), A(5), 0.0, None, Mx).then_inc(S("gdn_d"), 1)
                    ready("gdn_ztanh")
                    stt(A(19), A(11), 1.0, raw[:, 3, TAPS - 1:], Ad, M).then_inc(S("raw_used3"), 1)
                    ready("gdn_rk")
                    tt(A(0), A(0), A(2), M).then_inc(S("gdn_k"), 1)
                    ready("gdn_rq")
                    tt(A(6), A(6), A(7), M).then_inc(S("gdn_q"), 1)
                    ready("gdn_decay")
                    tt(tiles(A(2)), tiles(A(5)), per_token(1), M)
                    tt(tiles(A(10)), tiles(A(5)), over(C("incl").unsqueeze(1), BIG), M)
                    ready("gdn_kT")
                    tt(tiles(A(1)), tiles(TB[0][:, :]), per_token(4), M)
                    tt(tiles(A(9)), tiles(TB[0][:, :]), per_token(5), M)
                    ready("gdn_kk")
                    tt(A(3), TB[1][:, :], A(2), M).then_inc(S("gdn_lower"), 1)
                    ready("gdn_qk")
                    tt(A(10), SB_[0][:, :], A(10), M).then_inc(S("gdn_intra"), 1)
                    ready("gdn_egb")
                    tt(A(6), A(6), A(4), M).then_inc(S("gdn_qh"), 1)
                    tt(tiles(A(11)), tiles(A(3)), over(C("merge1").unsqueeze(1), BIG), M)
                    ready("gdn_vT")
                    tt(tiles(A(8)), tiles(SB_[1][:, :]), per_token(2), M).then_inc(S("gdn_bv"), 1)
                    tt(tiles(A(11)), over(ident.unsqueeze(1), BIG), tiles(A(11)), Su)
                    dve.wait_ge(S("gdn_ct"), D * 6 + 1)
                    tt(tiles(A(13)), over(ident.unsqueeze(1), BIG), tiles(A(14)), Su)
                    sync().then_inc(S("gdn_T"), 1)
                    for v in range(len(LEVELS)):
                        dve.wait_ge(S("gdn_TCT"), D * 5 + v + 1)
                        if v < len(LEVELS) - 1:
                            tt(A(11), A(11), SB_[0][:, :], Su)
                        tt(A(13), A(13), SB_[1][:, :], Su)
                        sync().then_inc(S("gdn_T" if v < len(LEVELS) - 1 else "gdn_Tt"), 1)
                    for i in range(SEQ // CHUNK):
                        dve.wait_ge(S("rec_kv"), D * 8 + i + 1)
                        end = (i + 1) * CHUNK - 1
                        stt(state[:, :], state[:, :], A(4)[:, end:end + 1], TB[i % 2][:, 0:HD], M, Ad)\
                            .then_inc(S("rec_state"), 1)
                    ready("gdn_ro")
                    tt(A(14), OB[:, :], A(15), M)
                    stt(yT[:, bass.ds(h + NSA_H, 1), :].rearrange("p a n -> p (a n)"), A(14), gnorm,
                        A(19), M, M).then_inc(S("y_ready"), 1)

                def stick(h):
                    B = l * SB_H + h
                    for i in range(2):
                        dve.wait_ge(S("p_copied"), after("p_copied", tile_of_lot(l, GDN_H + h) + i + 1))
                        ts(A(i), raw[:, i, TAPS - 1:], (1.0, SCALE)[i], None, M).then_inc(S(f"raw_used{i}"), 1)
                    sync().then_inc(S("sb_qk"), 1)
                    dve.wait_ge(S("sb_vT"), B + 1)
                    cp(A(2), MB[:, :]).then_inc(S("sb_v"), 1)
                    dve.sem_inc(S("raw_used2"), 1)
                    dve.wait_ge(S("sb_ztanh"), B + 1)
                    stt(A(3), A(4), 1.0, raw[:, 3, TAPS - 1:], Ad, M).then_inc(S("raw_used3"), 1)
                    for s in range(TT + 1):
                        if s < TT:
                            j, w = TT - 1 - s, (s + 1) * P
                            dve.wait_ge(S("sb_ln"), B * TT + s + 1)
                            stt(A(9 + j)[:, 0:w], SB_[s % 2][:, 0:w], 0.0, A(5 + s % 2)[:, 0:w], Mx, Ad)
                            tt(A(13 + s % 2)[:, 0:w], SB_[s % 2][:, 0:w], A(9 + j)[:, 0:w], Su)\
                                .then_inc(S("lb_ready"), 1)
                            tt(A(9 + j)[:, 0:P], A(9 + j)[:, 0:P], C("past"), M)
                            sync().then_inc(S("spm_ready"), 1)
                        if s >= 1:
                            w = s * P
                            lb = A(13 + (s - 1) % 2)[:, 0:w]
                            dve.wait_ge(S("sb_acc"), B * TT + s)
                            tt(lb, lb, TB[(s - 1) % 2][:, 0:w], Su).then_inc(S("sb_arg"), 1)
                            a = A(16 - s % 2)[:, 0:P]
                            dve.wait_ge(S("sb_exp"), after("sb_exp", B * TT + s))
                            tt(a, a, C("past"), M).then_inc(S("sb_a"), 1)
                    dve.wait_ge(S("sb_pv"), after("sb_pv", B * TT + TT))
                    at = yT[:, MIX_T - 1, :] if isinstance(h, int) else \
                        yT[:, bass.ds(h + (NSA_H + GDN_H), 1), :].rearrange("p a n -> p (a n)")
                    stt(at, OB[:, :], 0.5, A(3), M, M).then_inc(S("y_ready"), 1)

                with dve.Fori(0, SB_H - 1) as h:
                    stick(h)
                stick(SB_H - 1)

                with dve.Fori(0, TT // 2) as n2:
                    for e in range(2):
                        outs = (bank[2:6], [bank[0], bank[1], bank[6], bank[7]])[e]
                        cols = bass.ds(n2 * (2 * SEQ) + e * SEQ, SEQ)
                        dve.wait_ge(S("load_used"), after("load_used", l * PE_LOADS + n2 * 8 + (COL_LOADS + e * 4 + 4)))
                        for t in range(TT):
                            tmp = A(t)
                            tt(tmp, outs[t][:, :], gateb[:, cols], M).then_inc(S("o_used"), 1)
                        for t in range(TT):
                            x_ = xres[:, t, cols]
                            stt(x_, x_, ALPHA, A(t), M, Ad)
                for t in range(TT):
                    for n in range(4):
                        bn_stats(stats[:, t, n, :], xres[:, t, n * SEQ:(n + 1) * SEQ])
                for t in range(TT):
                    bn_aggr(meanvar[:, t, :], stats[:, t, :, :])
                sync().then_inc(S("var_ready"), 1)
                dve.wait_ge(S("rstd_ready"), l + 1)
                dve.wait_ge(S("ln_in"), l * 16 + 16)
                for t in range(TT):
                    x_ = xres[:, t, :]
                    ts(x_, x_, meanvar[:, t, 0:1], tiny[:, 20 + t:21 + t], Su, M)
                    tt(x_, x_, ln_gb[:, 0, :], M)
                    tt(x_, x_, ln_gb[:, 1, :], Ad)
                sync().then_inc(S("layer_done"), 1)


def by_row_tiles(w):
    *lead, rows, n = w.shape
    return w.reshape(*lead, rows // P, P, n).swapaxes(-3, -2).reshape(*lead, P, rows // P * n)


def columns(w_in, start, i):
    return by_row_tiles(w_in[:, :, start + i * P:start + (i + 1) * P])


def weight_stream(w_mod, w_in, w1_k, w1_v, w_out):
    loads = []
    for k in range(KT):
        for j in range(MOD_J):
            loads.append(w_mod[:, k::KT, j * DM:(j + 1) * DM])
    for g in range(KVH):
        loads += [columns(w_in, C_KC, g), columns(w_in, C_VC, g)]
        for w1 in (w1_k, w1_v):
            loads += [by_row_tiles(w1[:, :DM]), by_row_tiles(w1[:, DM:])]
        loads += [columns(w_in, start, g) for start in (C_KS, C_VS, C_KW, C_VW)]
        for r in range(GROUP):
            loads += [columns(w_in, C_NQ, g * GROUP + r), columns(w_in, C_NZ, g * GROUP + r)]
    for heads, starts in ((GDN_H, (C_GK, C_GQ, C_GV, C_GZ)), (SB_H, (C_SK, C_SQ, C_SV, C_SZ))):
        for h in range(heads):
            loads += [columns(w_in, start, h) for start in starts]
    for n in range(TT):
        for k in range(NS):
            loads.append(by_row_tiles(w_out[:, k * SEQ:(k + 1) * SEQ, n * SEQ:(n + 1) * SEQ]))
    return np.stack(loads, 1)


def small_weights(w_in, w2_k, w2_v, conv_w, norm_g, pe_k, pe_v, dt_bias, a_log):
    few = np.concatenate([w_in[:, :, C_NG:C_NG + 18], w_in[:, :, C_GB:C_GB + 2 * GDN_H]], 2)
    taps = conv_w.reshape(DEPTH, TAPS * 18, P).swapaxes(1, 2)
    rows = [np.broadcast_to(v[:, None, :], (DEPTH, P, GDN_H)) for v in (dt_bias, a_log)]
    return np.concatenate([by_row_tiles(few), w2_k, w2_v, taps, norm_g[:, :, None],
                           pe_k.swapaxes(1, 2), pe_v.swapaxes(1, 2), *rows], 2)


def kernel(x, c, positions, w_mod, b_mod, w_in, w_out, ln_g, ln_b, cmp_pe_k, cmp_pe_v, cmp_w1_k,
           cmp_w2_k, cmp_w1_v, cmp_w2_v, gdn_conv_w, gdn_a_log, gdn_dt_bias, gdn_norm_g):
    import concourse.bacc as _bacc
    from concourse.bass_utils import run_bass_kernel_spmd as _run

    nc = _bacc.Bacc("TRN2", target_bir_lowering=False, num_devices=1)
    const, where = constants()
    arrays = {
        "x": x, "positions": positions, "c": c, "b_mod": b_mod,
        "stream": weight_stream(w_mod, w_in, cmp_w1_k, cmp_w1_v, w_out),
        "small": small_weights(w_in, cmp_w2_k, cmp_w2_v, gdn_conv_w, gdn_norm_g, cmp_pe_k, cmp_pe_v,
                               gdn_dt_bias, gdn_a_log),
        "lns": np.concatenate([ln_g, ln_b], 1),
        "const": const,
    }
    arrays = {f"in_{name}": np.ascontiguousarray(a) for name, a in arrays.items()}
    args = [nc.dram_tensor(n, a.shape, mybir.dt.from_np(a.dtype), kind="ExternalInput").ap()
            for n, a in arrays.items()]
    out = nc.dram_tensor("out_0", (1, SEQ, DM), F32, kind="ExternalOutput").ap()
    build(nc, *args, out, where)
    r = _run(nc, [arrays], core_ids=[0])
    return r.results[0]["out_0"]
```

```python
from contextlib import ExitStack

import numpy as np

import concourse.bass as bass
from concourse import mybir

F32 = mybir.dt.float32
F32R = mybir.dt.float32r
I32 = mybir.dt.int32
ALU = mybir.AluOpType
ACT = mybir.ActivationFunctionType
AX = mybir.AxisListType.X

P = 128
DEPTH, SEQ, DM, HD = 2, 512, 2048, 128
ROPE_HALF, ROPE_THETA = 16, 500000.0
KVH, GROUP, CMP_LEN, CMP_STRIDE = 2, 3, 32, 16
GDN_H, TAPS, CHUNK = 6, 4, 64
SB_H = 4
NSA_H = KVH * GROUP
NSA_W, KV_W, GDN_W, SB_W = 6 * HD, 2 * HD, 6 * HD, 4 * HD
N_CMP = (SEQ - CMP_LEN) // CMP_STRIDE + 1
SCALE = HD ** -0.5
ALPHA = (2 * DEPTH) ** 0.25
LN_EPS, RMS_EPS, NEG = 1e-5, 1e-6, -1e30
WIDTHS = (NSA_W, KV_W, KV_W, KV_W, KV_W, KV_W, KV_W, 18, NSA_W, GDN_W, GDN_W, GDN_W, 6, 6, GDN_W,
          SB_W, SB_W, SB_W, SB_W)
STARTS = [0]
for _w in WIDTHS:
    STARTS.append(STARTS[-1] + _w)
(C_NQ, C_KC, C_VC, C_KS, C_VS, C_KW, C_VW, C_NG, C_NZ, C_GQ, C_GK, C_GV, C_GB, C_GA, C_GZ,
 C_SQ, C_SK, C_SV, C_SZ, IN_COLS) = STARTS

KT = DM // P
TT = SEQ // P
NS = 4
HALF = 8 * P
N_SMALL = 30
MIX_T = (NSA_W + GDN_W + SB_W) // P

SMALL_HALVES = 4


def mixed(tiles, m_each, m_first=0):
    items, m = [], m_first
    for i, t in enumerate(tiles):
        for half in range(2):
            items.append(("C", t, half))
            items += [("M", m + j) for j in range(m_each)]
            m += m_each
    return items


def group_items(has_next):
    items = mixed((0, 1), 0) + [("D", i) for i in range(8)] + mixed(range(2, 8), 0)
    if not has_next:
        return items + mixed(range(8, 12), 0)
    return items + mixed((8, 9), 2) + mixed((10, 11), 2, 8) + [("M", i) for i in range(16, 32)]


LOT = 4
PLAIN_LOT, GATE_LOT = mixed(range(LOT), 0), mixed(range(LOT), 1)
N_LOTS = GDN_H + SB_H
GROUP_TILES = 12
LAYER_TILES = KVH * GROUP_TILES + N_LOTS * LOT
OUT_HALVES = 2 * KT
LEVELS = (2, 4, 8, 16, 32)


def layout(has_next):
    group = len(group_items(has_next))
    at, n = {"group": SMALL_HALVES, "group_len": group}, SMALL_HALVES + KVH * group
    at["lot0"] = n
    n += len(GATE_LOT)
    at["gdn"] = n
    n += GDN_H * len(PLAIN_LOT)
    at["sb"] = n
    n += (SB_H - 1) * len(GATE_LOT)
    at["out"] = n
    at["end"] = n + OUT_HALVES
    return at


LAYOUTS = [layout(l < DEPTH - 1) for l in range(DEPTH)]
STREAM_AT = [sum(a["end"] - SMALL_HALVES for a in LAYOUTS[:l]) for l in range(DEPTH)]
HALVES_AT = [sum(a["end"] for a in LAYOUTS[:l]) for l in range(DEPTH)]
SPLITS = SMALL_HALVES + 2 * LAYER_TILES + OUT_HALVES


SMALL = {"w2": 2 * HD, "taps": TAPS * 18, "norm_g": 1, "pe": 2 * CMP_LEN,
         "dt_bias": GDN_H, "a_log": GDN_H, "ln_before": 2 * KT}
SMALL_AT, SMALL_W = {}, 0
for _name, _w in SMALL.items():
    SMALL_AT[_name] = (SMALL_W, _w)
    SMALL_W += _w


def constants():
    r = np.arange(P)
    row, col = r[:, None], r[None, :]
    same = row // CHUNK == col // CHUNK
    blocks = {
        "ident": (row == col),
        "ones": np.ones((P, P)),
        "after": (row > col),
        "causal": np.where(col <= row, 0.0, NEG),
        "past": (row < col),
        "cumul": same & (row <= col),
        "chunk": same,
        "incl": same & (row >= col),
        "merge1": (row // 2 == col // 2) & (row % 2 == 1) & (col % 2 == 0),
    }
    for m in (1,) + LEVELS:
        lower = (row // (2 * m) == col // (2 * m)) & (row % (2 * m) >= m) & (col % (2 * m) < m)
        blocks[f"mergeT{m}"] = lower.T
    t = np.arange(TT)[None, :, None] * P + r[:, None, None]
    seen = (np.arange(N_CMP) * CMP_STRIDE + CMP_LEN - 1)[None, None, :] <= t
    blocks["cmp_add"] = np.where(seen, 0.0, NEG).reshape(P, -1)
    blocks["cmp_mul"] = seen.reshape(P, -1)
    rot = np.zeros((P, 2 * ROPE_HALF))
    for i in range(ROPE_HALF):
        rot[ROPE_HALF + i, i] = -1.0
        rot[i, ROPE_HALF + i] = 1.0
    blocks["rot"] = rot
    inv = np.float32(ROPE_THETA) ** (-np.arange(ROPE_HALF, dtype=np.float32) * np.float32(2.0)
                                     / np.float32(2 * ROPE_HALF))
    misc = np.zeros((P, 2))
    misc[:2 * ROPE_HALF, 0] = np.tile(inv, 2)
    blocks["misc"] = misc
    at, where = 0, {}
    for name, b in blocks.items():
        where[name] = (at, b.shape[1])
        at += b.shape[1]
    return np.concatenate([np.asarray(b, np.float32) for b in blocks.values()], 1), where


def build(nc, x, positions, c, b_mod, mod0, small_cols, stream, small, lns, const, out, where, layers=DEPTH):
    x_norm = nc.dram_tensor("x_norm", (TT, P, DM), F32, kind="Internal").ap()
    ctx = ExitStack()
    with ctx:
        def sb(name, shape, dt=F32):
            return ctx.enter_context(nc.sbuf_tensor(name, shape, dt))

        h_hi = sb("h_hi", [P, KT, SEQ], F32R)
        h_lo = sb("h_lo", [P, KT, SEQ], F32R)
        yT = sb("yT", [P, MIX_T, SEQ])
        ring = sb("ring", [P, NS, HALF])
        w_hi = sb("w_hi", [P, 2, HALF], F32R)
        w_lo = sb("w_lo", [P, 2, HALF], F32R)
        acc = sb("acc", [P, DM])
        cst = sb("cst", [P, const.shape[1]])
        rope_cs = sb("rope_cs", [2 * ROPE_HALF, 2, SEQ])
        raw = sb("raw", [P, LOT, TAPS - 1 + SEQ])
        arena = sb("arena", [P, 20, SEQ])
        state = sb("state", [P, HD])
        vnew = sb("vnew", [P, 2, HD])
        sm_all = sb("sm_all", [P, SMALL_W])
        cact = sb("cact", [P, 2, KT])
        modT = sb("modT", [P, 2, KT])
        h_mod = sb("h_mod", [P, 2, KT])
        ea = sb("ea", [P, GDN_H])
        gates = sb("gates", [P, TT, 18])
        gate_g = sb("gate_g", [P, TT, 9])
        coef = sb("coef", [P, 6, TT, GDN_H])
        coef_h = sb("coef_h", [P, 6, TT])
        conv_h = sb("conv_h", [P, TAPS, 3])
        tiny = sb("tiny", [P, 40])
        stats = sb("stats", [P, TT, 4, 6])
        meanvar = sb("meanvar", [P, TT, 2])
        cmpb = sb("cmpb", [P, 6, 32])
        vcmp = sb("vcmp", [P, HD])

        def C(name, parts=P):
            at, n = where[name]
            return cst[0:parts, at:at + n]

        def small_part(name):
            at, n = SMALL_AT[name]
            return sm_all[:, at:at + n]

        w2 = small_part("w2").rearrange("p (a n) -> p a n", a=2)
        peT = small_part("pe").rearrange("p (a t) -> p a t", a=2)
        taps, gnorm = small_part("taps"), small_part("norm_g")
        ident, ones = C("ident"), C("ones")
        ln_before = small_part("ln_before").rearrange("p (a k) -> p a k", a=2)
        xres = arena[:, 0:16, :].rearrange("p (t a) b -> p t (a b)", t=TT)
        gateb = yT[:, 0:4, :].rearrange("p a b -> p (a b)")
        ln_gb = yT[:, 4:12, :].rearrange("p (a b) c -> p a (b c)", a=2)
        acc0 = [acc[:, :], arena[:, 16:20, :].rearrange("p a b -> p (a b)")]
        mod_ring = yT[:, :, :].rearrange("p (a b) c -> p a (b c)", a=NS)

        bank = [ctx.enter_context(nc.psum_tensor(f"bank{i}", [P, SEQ], F32)) for i in range(8)]
        PJ, SB_, TB, OB, MB = bank[0:2], bank[2:4], bank[4:6], bank[6], bank[7]
        ODD = [bank[0], bank[1], bank[6], bank[7]]

        def A(i, parts=P):
            return arena[0:parts, i, :]

        def tiles(ap):
            return ap.rearrange("p (t n) -> p t n", t=TT)

        def over(ap, shape):
            return ap.broadcast_to(shape)

        BIG = (P, TT, P)
        blocks_kv = [arena[:, 2 * i:2 * i + 2, :].rearrange("p a b -> p (a b)") for i in range(2)]
        prob, probT = [A(0), A(1)], [A(2), A(3)]
        kS, kW, vS, vW = A(4), A(5), A(6), A(7)
        qT, szq, z_raw, z_tanh = [A(8), A(9)], [A(10), A(11)], A(12), A(13)
        v_raw = [A(14), A(15)]
        rope_a, rope_b = A(16, 32), A(17, 32)
        cmp_s = A(18)[:, 0:TT * N_CMP].rearrange("p (t n) -> p t n", t=TT)
        cmp_p = A(18)[:, 256:256 + TT * N_CMP].rearrange("p (t n) -> p t n", t=TT)
        cmp_pT = A(19, N_CMP)

        semaphores = {}

        def S(name):
            if name not in semaphores:
                semaphores[name] = ctx.enter_context(nc.semaphore(name))
            return semaphores[name]

        CREDITS = {"mod_used": NS, "split_used": 2, "p_copied": 1, "rot_used": 1, "exp_done": 1,
                   "pt_ready": 1, "pv_done": 1, "y_ready": 1, "sz_ready": 1,
                   "o_used": 8, "rec_vn": 1, "rec_state": 1, "gdn_lv_y": 1, "lb_ready": 1,
                   "sb_exp": 1, "sb_pv": 1}
        for i in range(NS):
            CREDITS[f"raw_free{i}"] = 1
        for i in range(LOT):
            CREDITS[f"raw_used{i}"] = 1

        def after(name, n):
            return n + CREDITS.get(name, 0)

        for name in CREDITS:
            S(name)
        for name in ["const_in", "x_in", "small_in", "ln_in", "x_stored", "bmod_in", "slot_in0", "slot_in1", "slot_in2", "slot_in3"]:
            S(name)

        block = ctx.enter_context(nc.Block())

        REC = 5 + 2 * len(LEVELS) + 1
        GDN_STEPS = REC + 2 * (SEQ // CHUNK) + 1
        gdn_fill = [LOT * KT * (s + 1) // GDN_STEPS - LOT * KT * s // GDN_STEPS for s in range(GDN_STEPS)]
        SB_STEPS = TT + 2
        sb_fill = [LOT * KT * (s + 1) // SB_STEPS - LOT * KT * s // SB_STEPS for s in range(SB_STEPS)]
        NSA_STEPS = 11
        nsa_fill = [2 * KT * (s + 1) // NSA_STEPS - 2 * KT * s // NSA_STEPS for s in range(NSA_STEPS)]

        MOD_STEPS = [{s: (s, s + 1) for s in range(8)}, {s: (8 + s, 9 + s) for s in range(8)},
                     {s: (16 + 2 * s, 18 + 2 * s) for s in range(8)}]

        def ended(fill, s):
            return range(sum(fill[:s]) // KT, sum(fill[:s + 1]) // KT)

        def parts(fill, s):
            a, b = sum(fill[:s]), sum(fill[:s + 1])
            spans = [(i, max(a - i * KT, 0), min(b - i * KT, KT)) for i in range(sum(fill) // KT)]
            return [x for x in spans if x[1] < x[2]]

        def tile_of_lot(l, n):
            return l * LAYER_TILES + KVH * GROUP_TILES + n * LOT

        def split_of_group(l, g):
            return l * SPLITS + SMALL_HALVES + g * (2 * GROUP_TILES)

        def split_of_lot(l, n):
            return l * SPLITS + SMALL_HALVES + 2 * KVH * GROUP_TILES + n * (2 * LOT)

        def turn_of_group(l, g):
            return (HALVES_AT[l] + LAYOUTS[l]["group"]) // NS + g * (LAYOUTS[l]["group_len"] // NS)

        def turn_of_lot(l, n):
            at = {key: (HALVES_AT[l] + LAYOUTS[l][key]) // NS for key in ("lot0", "gdn", "sb")}
            if isinstance(n, int) and n == 0:
                return at["lot0"]
            kind, first = n
            return at[kind] + first * (len(GATE_LOT if kind == "sb" else PLAIN_LOT) // NS)

        turn_of_out = [(HALVES_AT[l] + LAYOUTS[l]["out"]) // NS for l in range(DEPTH)]
        sums_before = [2 + l + 2 * min(l, DEPTH - 1) for l in range(DEPTH)]

        @block.sync
        def _(sp):
            sp.dma_start(cst[:, :], const).then_inc(S("const_in"), 16)
            sp.dma_start(cact[:, 1, :], c[0].rearrange("(p k) -> p k", k=KT)).then_inc(S("const_in"), 16)
            sp.dma_start(raw[0:32, 0, TAPS - 1:].bitcast(I32), positions.broadcast_to((32, SEQ)))\
                .then_inc(S("const_in"), 16)
            with sp.Fori(0, 2 * KT // NS) as n4:
                for i in range(NS):
                    sp.wait_ge(S("mod_used"), n4 * NS + i + 1)
                    sp.dma_start(mod_ring[:, i, :], mod0[bass.ds(n4 * NS + i, 1)].rearrange("a p n -> (a p) n"))\
                        .then_inc(S(f"mod_in{i}"), 16)

            for l in range(layers):
                if l == 0:
                    sp.dma_start(sm_all[:, :], small[0]).then_inc(S("small_in"), 16)
                    sp.dma_start(xres, x[0].rearrange("(t p) n -> p t n", p=P)).then_inc(S("x_in"), 16)
                for i in range(SMALL_HALVES):
                    sp.wait_ge(S(f"raw_free{i}"), HALVES_AT[l] // NS + 1)
                    sp.dma_start(ring[:, i, 0:4 * N_SMALL], small_cols[l, i]).then_inc(S(f"slot_in{i}"), 16)

                def load(first, n):
                    with sp.Fori(0, n // NS) as n4:
                        for i in range(NS):
                            sp.wait_ge(S(f"raw_free{i}"), n4 + ((HALVES_AT[l] + first) // NS + 1))
                            sp.dma_start(ring[:, i, :], stream[bass.ds(
                                n4 * NS + (STREAM_AT[l] + first - SMALL_HALVES + i), 1)].rearrange(
                                    "a p n -> (a p) n")).then_inc(S(f"slot_in{i}"), 16)

                at = LAYOUTS[l]
                load(SMALL_HALVES, at["out"] - SMALL_HALVES)
                if l < layers - 1:
                    sp.wait_ge(S("y_ready"), after("y_ready", l * 16 + NSA_H + GDN_H))
                    sp.dma_start(sm_all[:, :], small[l + 1]).then_inc(S("small_in"), 16)
                load(at["out"], OUT_HALVES)
            for t in range(TT):
                if t < 2:
                    sp.wait_ge(S("pool_out"), t + 1)
                else:
                    sp.wait_ge(S("dve_out"), t - 1)
                sp.dma_start(out[0, t * P:(t + 1) * P, :], xres[:, t, :]).then_inc(S("out_in"), 16)
            sp.wait_ge(S("out_in"), TT * 16)

        @block.tensor
        def _(pe):
            mm, tr = pe.matmul, pe.transpose

            def each_tile(dst, lhs, rhs):
                for t in range(TT):
                    at = slice(t * P, (t + 1) * P)
                    last = mm(dst[:, at], lhs[:, at], rhs[:, at], start=True, stop=True)
                return last

            def transposes(dst, src):
                for t in range(TT):
                    at = slice(t * P, (t + 1) * P)
                    last = tr(dst[:, at], src[:, at], ident)
                return last

            def column_tile(tile, split, b, k0, k1):
                for k in range(k0, k1):
                    half, i = divmod(k, KT // 2)
                    if k == 0:
                        pe.wait_ge(S("p_copied"), tile)
                    if i == 0 or k == k0:
                        pe.wait_ge(S("split_ready"), split + half + 1)
                    hi, lo = (w[:, half, i * P:(i + 1) * P] for w in (w_hi, w_lo))
                    mm(PJ[b][:, :], hi, h_hi[:, k, :], start=(k == 0), stop=False)
                    mm(PJ[b][:, :], hi, h_lo[:, k, :], start=False, stop=False)
                    last = mm(PJ[b][:, :], lo, h_hi[:, k, :], start=False, stop=(k == KT - 1))
                    if i == KT // 2 - 1:
                        last.then_inc(S("split_used"), 1)

            def lot_products(l, n, fill, s):
                for i, k0, k1 in parts(fill, s):
                    column_tile(tile_of_lot(l, n) + i, split_of_lot(l, n) + 2 * i, i % 2, k0, k1)

            def reduce_mod(sums, n):
                pe.wait_ge(S("mod_sum"), n)
                for k in range(KT):
                    last = mm(MB[:, k:k + 1], sums[:, k * P:(k + 1) * P], ones[:, 0:1], start=True, stop=True)
                last.then_inc(S("mod_done"), 1)

            pe.wait_ge(S("const_in"), 48)
            reduce_mod(acc0[0], 1)
            pe.wait_ge(S("mod_copied"), 1)
            reduce_mod(acc0[1], 2)
            for l in range(layers):
                if l == 0:
                    pe.wait_ge(S("x_in"), 16)
                else:
                    pe.wait_ge(S("norm_act"), 2 * l)
                    pe.wait_ge(S("norm_dve"), 2 * l)
                for k in range(KT + 2):
                    if k < KT:
                        if k >= 2:
                            pe.wait_ge(S("h_read"), l * KT + k - 1)
                        for t in range(TT):
                            last = tr(TB[k % 2][:, t * P:(t + 1) * P], xres[:, t, k * P:(k + 1) * P], ident)
                        last.then_inc(S("xT_done"), 1)
                    if k >= 2:
                        j = k - 2
                        pe.wait_ge(S("h_ready"), l * KT + j + 1)
                        piece, i = divmod(j, KT // SMALL_HALVES)
                        if i == 0:
                            pe.wait_ge(S("split_ready"), l * SPLITS + piece + 1)
                        hi, lo = (w[:, piece % 2, i * N_SMALL:(i + 1) * N_SMALL] for w in (w_hi, w_lo))
                        o = OB[0:N_SMALL, :]
                        mm(o, hi, h_hi[:, j, :], start=(j == 0), stop=False)
                        mm(o, hi, h_lo[:, j, :], start=False, stop=False)
                        last = mm(o, lo, h_hi[:, j, :], start=False, stop=(j == KT - 1))
                        if i == KT // SMALL_HALVES - 1:
                            last.then_inc(S("split_used"), 1)
                if l == 0:
                    pe.wait_ge(S("mod_copied"), 2)
                pe.wait_ge(S("small_copied"), l + 1)
                for t in range(TT):
                    last = mm(MB[:, t * 32:t * 32 + N_SMALL], A(16, N_SMALL)[:, t * P:(t + 1) * P],
                              ident[0:N_SMALL, 0:N_SMALL], start=True, stop=True)
                last.then_inc(S("smallT_done"), 1)
                pe.wait_ge(S("g_ready"), l + 1)
                g_all = coef[:, 0, :, :].rearrange("p t h -> p (t h)")
                mm(SB_[0][:, 0:24], C("cumul"), g_all, start=True, stop=True)
                mm(SB_[0][:, 24:48], C("chunk"), g_all, start=True, stop=True).then_inc(S("gc_done"), 1)

                with pe.Fori(0, KVH) as g:
                    G = l * KVH + g

                    def load_tile(tile, k0=0, k1=KT):
                        column_tile(l * LAYER_TILES + g * GROUP_TILES + tile,
                                    split_of_group(l, g) + 2 * tile, tile % 2, k0, k1)

                    def copied(tile):
                        pe.wait_ge(S("p_copied"), after("p_copied", l * LAYER_TILES + g * GROUP_TILES + tile + 1))

                    def compress(which):
                        pe.wait_ge(S("blocks_ready"), G * 2 + which + 1)
                        for q4 in range(4):
                            pe.wait_ge(S(f"slot_in{q4}"), (turn_of_group(l, g) + (which + 2)) * 16)
                            for i in range(CMP_LEN // 4):
                                t = q4 * (CMP_LEN // 4) + i
                                last = mm(TB[which][:, 0:N_CMP], ring[:, q4, i * HD:(i + 1) * HD],
                                          blocks_kv[which][:, t * N_CMP:(t + 1) * N_CMP],
                                          start=(t == 0), stop=(t == CMP_LEN - 1))
                            last.then_inc(S(f"raw_free{q4}"), 1)

                    def rotate(j, x):
                        pe.wait_ge(S("rot_used"), after("rot_used", G * 6 + j))
                        mm(MB[0:32, 0:x.shape[1]], C("rot"), x, start=True, stop=True)\
                            .then_inc(S("rot_done"), 1)

                    load_tile(0)
                    load_tile(1)
                    compress(0)
                    compress(1)
                    load_tile(2)
                    pe.wait_ge(S("hid_ready"), G * 2 + 2)
                    mm(SB_[0][:, 0:N_CMP], w2[:, 0, :], cmpb[:, 2, 0:N_CMP], start=True, stop=True)
                    mm(SB_[1][0:N_CMP, 0:HD], cmpb[:, 3, 0:N_CMP], w2[:, 1, :],
                       start=True, stop=True).then_inc(S("cmp_done"), 1)
                    load_tile(3)
                    pe.wait_ge(S("cmp_copied"), G + 1)
                    rotate(0, cmpb[:, 0, 0:N_CMP])
                    rotate(1, kS)
                    load_tile(4)
                    copied(3)
                    transposes(TB[0], v_raw[0]).then_inc(S("vT_done"), 1)
                    load_tile(5)
                    copied(4)
                    rotate(2, kW)
                    load_tile(6)
                    copied(5)
                    transposes(TB[1], v_raw[1]).then_inc(S("vT_done"), 1)
                    load_tile(7)
                    copied(6)
                    rotate(3, qT[0])
                    for r in range(GROUP):
                        H = G * GROUP + r
                        q = qT[r % 2]
                        for s in range(NSA_STEPS):
                            if r < GROUP - 1:
                                for i, k0, k1 in parts(nsa_fill, s):
                                    load_tile(8 + 2 * r + i, k0, k1)
                                if s == 8:
                                    copied(8 + 2 * r)
                                    rotate(4 + r, qT[(r + 1) % 2])
                            if s == 0:
                                pe.wait_ge(S("roped"), G * 6 + 4 + r)
                                pe.wait_ge(S("exp_done"), after("exp_done", H * 8))
                                for i in range(TT):
                                    last = mm(SB_[0][:, i * 32:i * 32 + N_CMP], q[:, i * P:(i + 1) * P],
                                              cmpb[:, 0, 0:N_CMP], start=True, stop=True)
                                last.then_inc(S("cmp_scores"), 1)
                            if 1 <= s <= 8:
                                u = s - 1
                                i, keys, w = u % TT, (kS, kW)[u // TT], (u % TT + 1) * P
                                if u == 1:
                                    pe.wait_ge(S("cmp_scored"), H + 1)
                                pe.wait_ge(S("exp_done"), after("exp_done", H * 8 + max(u - 1, 0)))
                                mm(SB_[(u + 1) % 2][:, 0:w], q[:, w - P:w], keys[:, 0:w], start=True, stop=False)
                                mm(SB_[(u + 1) % 2][:, w - P:w], ident, C("causal"),
                                   start=False, stop=True).then_inc(S("scores"), 1)
                            if s == 1:
                                pe.wait_ge(S("cmp_probs"), H + 1)
                                pe.wait_ge(S("pt_ready"), after("pt_ready", H * 8))
                                pe.wait_ge(S("v_ready"), G * 2 + 2)
                                for i in range(TT):
                                    last = tr(TB[0][0:N_CMP, i * P:(i + 1) * P], cmp_p[:, i, :], ident)
                                last.then_inc(S("cmp_pT"), 1)
                            if s == 2:
                                pe.wait_ge(S("cmp_pT_ready"), H + 1)
                                pe.wait_ge(S("y_ready"), after("y_ready", l * 16 + g * GROUP + r))
                                mm(OB[:, :], vcmp[0:N_CMP, :], cmp_pT, start=True, stop=False,
                                   skip_group_check=True)
                            if 2 <= s <= 9:
                                u = s - 2
                                pe.wait_ge(S("pt_ready"), after("pt_ready", H * 8 + max(u - 1, 0)))
                                pe.wait_ge(S("probs"), H * 8 + u + 1)
                                for j in range(u % TT + 1):
                                    last = tr(TB[(u + 1) % 2][:, j * P:(j + 1) * P],
                                              prob[u % 2][:, j * P:(j + 1) * P], ident)
                                last.then_inc(S("pt_done"), 1)
                            if 3 <= s <= 10:
                                u = s - 3
                                i, vals = u % TT, (vS, vW)[u // TT]
                                pe.wait_ge(S("pt_ready"), after("pt_ready", H * 8 + u + 1))
                                for j in range(i + 1):
                                    last = mm(OB[:, i * P:(i + 1) * P], vals[:, j * P:(j + 1) * P],
                                              probT[u % 2][:, j * P:(j + 1) * P], start=False,
                                              stop=(j == i), skip_group_check=True)
                                last.then_inc(S("pv_done"), 1)
                    if l < DEPTH - 1:
                        reduce_mod(acc, g + (sums_before[l] + 1))

                for s in range(LOT):
                    lot_products(l, 0, [KT] * LOT, s)

                with pe.Fori(0, GDN_H) as h:
                    D = l * GDN_H + h
                    n = D + 1

                    def ready(name):
                        pe.wait_ge(S(name), n)

                    for s in range(GDN_STEPS):
                        lot_products(l, h + 1, gdn_fill, s)
                        if s == 0:
                            ready("gdn_gsel")
                            pe.wait_ge(S("y_ready"), after("y_ready", l * 16 + NSA_H + h))
                            mm(MB[:, :], ones, A(3), start=True, stop=True).then_inc(S("gdn_gcb"), 1)
                        if s == 1:
                            ready("gdn_sqk")
                            mm(SB_[0][:, :], ones, A(1), start=True, stop=True).then_inc(S("gdn_nk"), 1)
                            ready("gdn_sqq")
                            mm(SB_[1][:, :], ones, A(9), start=True, stop=True).then_inc(S("gdn_nq"), 1)
                        if s == 2:
                            ready("gdn_k")
                            transposes(TB[0], A(0)).then_inc(S("gdn_kT"), 1)
                            each_tile(TB[1], A(0), A(0)).then_inc(S("gdn_kk"), 1)
                        if s == 3:
                            ready("gdn_q")
                            each_tile(SB_[0], A(6), A(0)).then_inc(S("gdn_qk"), 1)
                            ready("gdn_v")
                            transposes(SB_[1], A(8)).then_inc(S("gdn_vT"), 1)
                            ready("gdn_lower")
                            transposes(TB[0], A(3)).then_inc(S("gdn_lT"), 1)
                        if s == 4:
                            ready("gdn_intra")
                            transposes(MB, A(10)).then_inc(S("gdn_iT"), 1)
                        for v in range(len(LEVELS)):
                            if s == 5 + 2 * v:
                                pe.wait_ge(S("gdn_ct"), D * 6 + v + 2)
                                pe.wait_ge(S("gdn_T"), D * 5 + v + 1)
                                if v == 0:
                                    ready("gdn_lT_copied")
                                each_tile(TB[0], A(15 - v % 2), A(11)).then_inc(S("gdn_CT"), 1)
                            if s == 6 + 2 * v:
                                pe.wait_ge(S("gdn_lv_y"), after("gdn_lv_y", D * 5 + v + 1))
                                if v == 0:
                                    ready("gdn_bv")
                                if v < len(LEVELS) - 1:
                                    each_tile(SB_[0], A(13), A(17))
                                each_tile(SB_[1], A(17), A(13)).then_inc(S("gdn_TCT"), 1)
                        if s == REC - 1:
                            pe.wait_ge(S("gdn_T"), D * 5 + 5)
                            pe.wait_ge(S("gdn_Tt"), n)
                            each_tile(TB[1], A(1), A(13)).then_inc(S("gdn_w"), 1)
                        if REC <= s < GDN_STEPS - 1:
                            i, second = (s - REC) // 2, (s - REC) % 2
                            t, half = i // 2, i % 2
                            at = slice(i * CHUNK, (i + 1) * CHUNK)
                            rows = slice(half * CHUNK, (half + 1) * CHUNK)
                            if not second:
                                if i == 0:
                                    ready("gdn_w_copied")
                                    ready("gdn_qh")
                                    ready("gdn_i_copied")
                                pe.wait_ge(S("rec_state"), after("rec_state", D * 9 + i + 1))
                                mm(SB_[half][rows, 0:HD], A(13)[:, at], A(8)[:, t * P:(t + 1) * P],
                                   start=True, stop=False)
                                mm(SB_[half][rows, 0:HD], A(18)[:, at], state[:, :],
                                   start=False, stop=True).then_inc(S("rec_v"), 1)
                                mm(OB[:, at], state[:, :], A(6)[:, at], start=True, stop=False)
                            else:
                                pe.wait_ge(S("rec_vn"), after("rec_vn", D * 8 + i + 1))
                                mm(TB[half][:, 0:HD], A(9)[:, t * P:(t + 1) * P], vnew[:, half, :],
                                   start=True, stop=True).then_inc(S("rec_kv"), 1)
                                last = mm(OB[:, at], vnew[:, half, :], A(16)[:, at], start=False, stop=True)
                                if i == SEQ // CHUNK - 1:
                                    last.then_inc(S("gdn_o"), 1)
                        if s == GDN_STEPS - 1:
                            ready("gdn_osq")
                            mm(SB_[0][:, :], ones, A(14), start=True, stop=True).then_inc(S("gdn_no"), 1)

                def stick(h, lot):
                    B = l * SB_H + h
                    for s in range(SB_STEPS):
                        if lot is not None:
                            lot_products(l, lot, sb_fill, s)
                        if s == 0:
                            pe.wait_ge(S("y_ready"), after("y_ready", l * 16 + NSA_H + GDN_H + h))
                            pe.wait_ge(S("p_copied"), after("p_copied", tile_of_lot(l, GDN_H + h) + 3))
                            transposes(MB, raw[:, 2, TAPS - 1:]).then_inc(S("sb_vT"), 1)
                            pe.wait_ge(S("sb_qk"), B + 1)
                        if s < TT:
                            j = TT - 1 - s
                            w = SEQ - j * P
                            pe.wait_ge(S("lb_ready"), after("lb_ready", B * TT + max(s - 1, 0)))
                            mm(SB_[s % 2][:, 0:w], A(0)[:, j * P:(j + 1) * P], A(1)[:, j * P:],
                               start=True, stop=True).then_inc(S("sb_z"), 1)
                        if 1 <= s <= TT:
                            j = TT - s
                            w = SEQ - j * P
                            pe.wait_ge(S("spm_ready"), B * TT + s)
                            b = TB[(s - 1) % 2]
                            mm(b[:, 0:w], C("after"), A(9 + j)[:, 0:w], start=True, stop=(s == 1))
                            for m in range(j + 1, TT):
                                last = mm(b[:, (m - j) * P:w], ones, A(9 + m)[:, 0:SEQ - m * P],
                                          start=False, stop=(m == TT - 1))
                            if s == 1:
                                last = None
                            if last is None:
                                pe.drain().then_inc(S("sb_acc"), 1)
                            else:
                                last.then_inc(S("sb_acc"), 1)
                        if 2 <= s <= TT + 1:
                            j = TT + 1 - s
                            pe.wait_ge(S("sb_a"), B * TT + s - 1)
                            if s == 2:
                                pe.wait_ge(S("sb_v"), B + 1)
                            last = mm(OB[:, j * P:], A(2)[:, j * P:(j + 1) * P], A(15 + s % 2)[:, 0:SEQ - j * P],
                                      start=(s == 2), stop=(s == TT + 1), skip_group_check=True)
                            last.then_inc(S("sb_pv"), 1)

                with pe.Fori(0, SB_H - 1) as h:
                    stick(h, h + (GDN_H + 1))
                stick(SB_H - 1, None)

                pe.wait_ge(S("y_ready"), after("y_ready", l * 16 + 16))
                pe.wait_ge(S("mod_sum"), sums_before[l] + (3 if l < DEPTH - 1 else 1))
                for n in range(TT):
                    last = mm(ODD[n][:, :], ones, acc[:, n * SEQ:(n + 1) * SEQ], start=True, stop=True)
                last.then_inc(S("gate_done"), 1)
                with pe.Fori(0, TT // 2) as n2:
                    for e in range(2):
                        outs = (bank[2:6], ODD)[e]
                        if e == 1:
                            pe.wait_ge(S("gate_ready"), l + 1)
                        for k2 in range(KT // 2):
                            pe.wait_ge(S("split_ready"), n2 * KT + (
                                l * SPLITS + SMALL_HALVES + 2 * LAYER_TILES + e * (KT // 2) + k2 + 1))
                            pe.wait_ge(S("y_split"), l * 16 + 2 * k2 + 2)
                            for t in range(TT):
                                if k2 == 0:
                                    pe.wait_ge(S("o_used"), l * 16 + n2 * 8 + (e * 4 + t + 1))
                                at = slice(t * P, (t + 1) * P)
                                for i in range(2):
                                    k = k2 * 2 + i
                                    hi, lo = (w[:, k2 % 2, i * SEQ:(i + 1) * SEQ] for w in (w_hi, w_lo))
                                    mm(outs[t][:, :], h_hi[:, k, at], hi, start=(k == 0), stop=False)
                                    mm(outs[t][:, :], h_hi[:, k, at], lo, start=False, stop=False)
                                    last = mm(outs[t][:, :], h_lo[:, k, at], hi, start=False, stop=(k == KT - 1))
                                if k2 == KT // 2 - 1 and t < TT - 1:
                                    last.then_inc(S("o_done"), 1)
                            last.then_inc(S("split_used"), 1)

        @block.scalar
        def _(act):
            def fn(*args, **kw):
                made = act.activation(*args, **kw)
                act.drain()
                return made

            def copy_tile(split, dst, b):
                act.wait_ge(S("split_used"), after("split_used", split))
                fn(dst, PJ[b][:, :], ACT.Copy).then_inc(S("p_copied"), 1)

            def copy_lot(l, n, i):
                act.wait_ge(S(f"raw_used{i}"), after(f"raw_used{i}", l * N_LOTS + n))
                copy_tile(split_of_lot(l, n) + 2 * i + 2, raw[:, i, TAPS - 1:], i % 2)

            def start_sums(n, dst, l, part):
                act.wait_ge(S("acc_zero"), n)
                src = b_mod[l:l + 1, part * DM:(part + 1) * DM] if isinstance(part, int) else \
                    b_mod[l:l + 1, bass.ds(part * DM, DM)]
                act.dma_start(dst, src).then_inc(S("bmod_in"), 16)

            act.wait_ge(S("const_in"), 48)
            fn(cact[:, 0, :], cact[:, 1, :], ACT.Tanh, scale=0.5).then_inc(S("c_tanh"), 1)
            act.wait_ge(S("angles"), 1)
            fn(rope_cs[:, :, :], arena[0:32, 18:20, :], ACT.Sin).then_inc(S("rope_ready"), 1)
            for i in range(2):
                start_sums(i + 1, acc0[i][0:1, :], 0, i)
            for l in range(layers):
                for k in range(KT):
                    act.wait_ge(S("h_tmp"), l * KT + k + 1)
                    if l and k == 0:
                        act.wait_ge(S("split_used"), after("split_used", l * SPLITS))
                    fn(h_hi[:, k, :], A(16 + k % 4), ACT.Copy).then_inc(S("h_hi_ready"), 1)
                act.wait_ge(S("split_used"), after("split_used", l * SPLITS + SMALL_HALVES))
                act.wait_ge(S("h_ready"), l * KT + KT)
                fn(A(16, N_SMALL), OB[0:N_SMALL, :], ACT.Copy).then_inc(S("small_copied"), 1)
                act.wait_ge(S("smallT_done"), l + 1)
                small = MB[:, 0:TT * 32].rearrange("p (t n) -> p t n", t=TT)
                th = A(17)[:, 0:TT * 24].rearrange("p (t n) -> p t n", t=TT)
                fn(th, small[:, :, 0:24], ACT.Tanh, scale=0.5).then_inc(S("gates_tanh"), 1)
                act.wait_ge(S("ga_ready"), l + 1)
                fn(A(18)[:, 32:56], A(18)[:, 0:24], ACT.Abs)
                fn(ea[:, :], small_part("a_log"), ACT.Exp)
                fn(A(18)[:, 64:88], A(18)[:, 32:56], ACT.Exp, scale=-1.0)
                fn(A(18)[:, 96:120], A(18)[:, 64:88], ACT.Ln, bias=1.0).then_inc(S("ga_ln"), 1)
                act.wait_ge(S("gc_ready"), l + 1)
                fn(A(18)[:, 128:152], coef[:, 3, :, :].rearrange("p t h -> p (t h)"), ACT.Exp)
                fn(coef[:, 5, :, :].rearrange("p t h -> p (t h)"), A(18)[:, 160:184], ACT.Exp)\
                    .then_inc(S("gc_exp"), 1)
                act.wait_ge(S("coef_ready"), l + 1)
                if l:
                    act.wait_ge(S("x_stored"), l * TT * 16)

                with act.Fori(0, KVH) as g:
                    G = l * KVH + g
                    if l < DEPTH - 1:
                        start_sums(g + (sums_before[l] + 1), acc[0:1, :], l + 1, g)

                    def copy_group(tile, dst):
                        copy_tile(split_of_group(l, g) + (2 * tile + 2), dst, tile % 2)

                    def copy_z(tile, H):
                        act.wait_ge(S("split_used"), after("split_used", split_of_group(l, g) + (2 * tile + 2)))
                        act.wait_ge(S("sz_ready"), after("sz_ready", H))
                        fn(z_raw, PJ[1][:, :], ACT.Copy)
                        fn(z_tanh, PJ[1][:, :], ACT.Tanh, scale=0.5)
                        act.drain().then_inc(S("p_copied"), 1)
                        act.sem_inc(S("z_tanh"), 1)

                    copy_group(0, v_raw[0])
                    copy_group(1, v_raw[1])
                    for which in range(2):
                        act.wait_ge(S("raw_free3"), after("raw_free3", turn_of_group(l, g) + (which + 2)))
                        fn(cmpb[:, 4 + which, 0:N_CMP], TB[which][:, 0:N_CMP], ACT.Tanh, scale=0.5)\
                            .then_inc(S("cmp_tanh"), 1)
                    copy_group(2, kS)
                    act.wait_ge(S("cmp_done"), G + 1)
                    fn(cmpb[:, 0, 0:N_CMP], SB_[0][:, 0:N_CMP], ACT.Copy)
                    fn(vcmp[0:N_CMP, :], SB_[1][0:N_CMP, 0:HD], ACT.Copy)
                    act.drain().then_inc(S("cmp_copied"), 1)
                    copy_group(3, v_raw[0])
                    copy_group(4, kW)
                    act.wait_ge(S("vT_done"), G * 2 + 1)
                    fn(vS, TB[0][:, :], ACT.Copy).then_inc(S("v_ready"), 1)
                    copy_group(5, v_raw[1])
                    copy_group(6, qT[0])
                    act.wait_ge(S("vT_done"), G * 2 + 2)
                    fn(vW, TB[1][:, :], ACT.Copy).then_inc(S("v_ready"), 1)
                    copy_z(7, G * GROUP)
                    for r in range(GROUP):
                        H = G * GROUP + r
                        for s in range(NSA_STEPS):
                            if r < GROUP - 1:
                                for i in ended(nsa_fill, s):
                                    if i == 0:
                                        copy_group(8 + 2 * r, qT[(r + 1) % 2])
                                    else:
                                        copy_z(9 + 2 * r, H + 1)
                            if s == 0:
                                act.wait_ge(S("cmp_scored2"), H + 1)
                                fn(cmp_s, cmp_s, ACT.Exp).then_inc(S("cmp_exp"), 1)
                            if 1 <= s <= 8:
                                u = s - 1
                                w = (u % TT + 1) * P
                                act.wait_ge(S("max_ready"), H * 8 + u + 1)
                                fn(prob[u % 2][:, 0:w], SB_[(u + 1) % 2][:, 0:w], ACT.Exp, scale=SCALE,
                                   bias=tiny[:, u:u + 1], accum_out=tiny[:, 8 + u:9 + u]).then_inc(S("exp_done"), 1)
                            if 2 <= s <= 9:
                                u = s - 2
                                w = (u % TT + 1) * P
                                act.wait_ge(S("pt_done"), H * 8 + u + 1)
                                act.wait_ge(S("pv_done"), after("pv_done", H * 8 + max(u - 1, 0)))
                                fn(probT[u % 2][:, 0:w], TB[(u + 1) % 2][:, 0:w], ACT.Copy)\
                                    .then_inc(S("pt_ready"), 1)

                start_sums(sums_before[l] + (3 if l < DEPTH - 1 else 1), acc[0:1, :], l, 2)
                for i in range(LOT):
                    copy_lot(l, 0, i)

                with act.Fori(0, GDN_H) as h:
                    D = l * GDN_H + h
                    n = D + 1

                    def ready(name):
                        act.wait_ge(S(name), n)

                    for s in range(GDN_STEPS):
                        for i in ended(gdn_fill, s):
                            copy_lot(l, h + 1, i)
                        if s == 0:
                            for i, th in enumerate((1, 9, 10)):
                                act.wait_ge(S("gdn_conv"), D * 3 + i + 1)
                                fn(A(th), A((0, 6, 8)[i]), ACT.Tanh, scale=0.5).then_inc(S("gdn_tanh"), 1)
                            fn(A(11), raw[:, 3, TAPS - 1:], ACT.Tanh, scale=0.5).then_inc(S("gdn_ztanh"), 1)
                            ready("gdn_d")
                            fn(A(4), MB[:, :], ACT.Exp).then_inc(S("gdn_egb"), 1)
                            fn(A(5), A(5), ACT.Exp, scale=-1.0).then_inc(S("gdn_decay"), 1)
                            act.wait_ge(S("gdn_silu"), D * 3 + 1)
                            fn(A(1), A(0), ACT.Square).then_inc(S("gdn_sqk"), 1)
                            act.wait_ge(S("gdn_silu"), D * 3 + 2)
                            fn(A(9), A(6), ACT.Square).then_inc(S("gdn_sqq"), 1)
                        if s == 1:
                            ready("gdn_nk")
                            fn(A(2), SB_[0][:, :], ACT.Ln, scale=0.25, bias=tiny[:, 32:33])
                            ready("gdn_nq")
                            fn(A(7), SB_[1][:, :], ACT.Ln, scale=0.25, bias=tiny[:, 32:33])
                            fn(A(2), A(2), ACT.Exp, scale=-0.5, bias=tiny[:, 34:35]).then_inc(S("gdn_rk"), 1)
                            fn(A(7), A(7), ACT.Exp, scale=-0.5, bias=tiny[:, 35:36]).then_inc(S("gdn_rq"), 1)
                        if s == 3:
                            ready("gdn_lT")
                            fn(A(12), TB[0][:, :], ACT.Copy).then_inc(S("gdn_lT_copied"), 1)
                        if s == 4:
                            ready("gdn_iT")
                            fn(A(16), MB[:, :], ACT.Copy).then_inc(S("gdn_i_copied"), 1)
                        for v in range(len(LEVELS)):
                            if s == 5 + 2 * v:
                                act.wait_ge(S("gdn_CT"), D * 5 + v + 1)
                                fn(A(17), TB[0][:, :], ACT.Copy).then_inc(S("gdn_lv_y"), 1)
                        if s == REC - 1:
                            ready("gdn_w")
                            fn(A(18), TB[1][:, :], ACT.Copy, scale=-1.0).then_inc(S("gdn_w_copied"), 1)
                        if REC <= s < GDN_STEPS - 1 and (s - REC) % 2 == 0:
                            i = (s - REC) // 2
                            rows = slice(i % 2 * CHUNK, (i % 2 + 1) * CHUNK)
                            act.wait_ge(S("rec_v"), D * 8 + i + 1)
                            fn(vnew[rows, i % 2, :], SB_[i % 2][rows, 0:HD], ACT.Copy).then_inc(S("rec_vn"), 1)
                        if s == GDN_STEPS - 1:
                            ready("gdn_o")
                            fn(A(14), OB[:, :], ACT.Square).then_inc(S("gdn_osq"), 1)
                            ready("gdn_no")
                            fn(A(15), SB_[0][:, :], ACT.Ln, scale=1.0 / HD, bias=tiny[:, 32:33])
                            fn(A(15), A(15), ACT.Exp, scale=-0.5, bias=tiny[:, 34:35]).then_inc(S("gdn_ro"), 1)

                def stick(h, lot):
                    B = l * SB_H + h
                    for s in range(SB_STEPS):
                        if lot is not None:
                            for i in ended(sb_fill, s):
                                copy_lot(l, lot, i)
                        elif s < TT:
                            if s == 0:
                                act.wait_ge(S("split_used"), after("split_used", split_of_lot(l, N_LOTS)))
                                act.wait_ge(S("y_ready"), after("y_ready", l * 16 + MIX_T - 1))
                            for k in range(s * 4, min(s * 4 + 4, MIX_T - 1)):
                                fn(h_hi[:, k, :], yT[:, k, :], ACT.Copy).then_inc(S("y_hi"), 1)
                        if s == 0:
                            act.wait_ge(S("y_ready"), after("y_ready", l * 16 + NSA_H + GDN_H + h))
                            fn(A(4), raw[:, 3, TAPS - 1:], ACT.Tanh, scale=0.5).then_inc(S("sb_ztanh"), 1)
                        if s < TT:
                            w = (s + 1) * P
                            act.wait_ge(S("sb_z"), B * TT + s + 1)
                            e = A(5 + s % 2)[:, 0:w]
                            fn(e, SB_[s % 2][:, 0:w], ACT.Abs)
                            fn(e, e, ACT.Exp, scale=-1.0)
                            fn(e, e, ACT.Ln, bias=1.0).then_inc(S("sb_ln"), 1)
                        if 1 <= s <= TT:
                            w = s * P
                            act.wait_ge(S("sb_arg"), B * TT + s)
                            act.wait_ge(S("sb_pv"), after("sb_pv", B * TT + max(s - 2, 0)))
                            fn(A(16 - s % 2)[:, 0:w], A(13 + (s - 1) % 2)[:, 0:w], ACT.Exp).then_inc(S("sb_exp"), 1)

                with act.Fori(0, SB_H - 1) as h:
                    stick(h, h + (GDN_H + 1))
                stick(SB_H - 1, None)
                act.wait_ge(S("y_ready"), after("y_ready", l * 16 + MIX_T))
                fn(h_hi[:, MIX_T - 1, :], yT[:, MIX_T - 1, :], ACT.Copy).then_inc(S("y_hi"), 1)
                act.wait_ge(S("y_split"), l * 16 + MIX_T)
                for n in range(TT):
                    at = slice(n * SEQ, (n + 1) * SEQ)
                    src = x_norm.rearrange("t p n -> p t n") if l else x[0].rearrange("(t p) n -> p t n", p=P)
                    act.dma_start(xres[:, :, at], src[:, :, at]).then_inc(S(f"xo_in{n}"), 16)
                    if l:
                        if n >= 2:
                            act.wait_ge(S("lnb_used"), (l - 1) * TT + n - 1)
                        for a in range(2):
                            act.dma_start(raw[:, n % 2 * 2 + a, TAPS - 1:],
                                          lns[l - 1:l, a * DM + n * SEQ:a * DM + (n + 1) * SEQ].broadcast_to((P, SEQ)))\
                                .then_inc(S(f"xo_in{n}"), 16)
                if l == layers - 1:
                    act.dma_start(ln_gb.rearrange("p a n -> p (a n)"), lns[l:l + 1, :].broadcast_to((P, 2 * DM)))\
                        .then_inc(S("ln_in"), 16)
                act.wait_ge(S("var_ready"), l + 1)
                fn(tiny[:, 16:20], meanvar[:, :, 1], ACT.Ln, bias=tiny[:, 33:34])
                fn(tiny[:, 20:24], tiny[:, 16:20], ACT.Exp, scale=-0.5).then_inc(S("rstd_ready"), 1)
                act.wait_ge(S("nmr_ready"), l + 1)
                for t in range(2):
                    fn(xres[:, t, :], xres[:, t, :], ACT.Identity, scale=tiny[:, 20 + t:21 + t],
                       bias=tiny[:, 36 + t:37 + t]).then_inc(S("norm_act"), 1)
                if l < layers - 1:
                    for t in range(TT):
                        if t < 2:
                            act.wait_ge(S("norm_act"), 2 * l + t + 1)
                        else:
                            act.wait_ge(S("norm_dve"), 2 * l + t - 1)
                        act.dma_start(x_norm[t], xres[:, t, :]).then_inc(S("x_stored"), 16)

        @block.gpsimd
        def _(pool):
            for name, n in CREDITS.items():
                pool.sem_inc(S(name), n)
            pool.memset(raw[:, :, 0:TAPS - 1], 0.0)
            pool.memset(vnew[:, :, :], 0.0)
            for i, v in enumerate((RMS_EPS, LN_EPS, float(np.log(0.5)), float(np.log(0.5 * SCALE)))):
                pool.memset(tiny[:, 32 + i:33 + i], v)
            pool.drain().then_inc(S("pool_ready"), 1)
            pool.wait_ge(S("const_in"), 48)
            one = ones[:, 0:1]

            def split(slot, turn, n, par, w=HALF):
                pool.wait_ge(S(f"slot_in{slot}"), turn * 16 + 16)
                pool.wait_ge(S("split_used"), n + 1)
                pool.tensor_tensor(w_hi[:, par, 0:w], ring[:, slot, 0:w], one.broadcast_to((P, w)), ALU.mult)
                pool.drain()
                pool.tensor_tensor(w_lo[:, par, 0:w], ring[:, slot, 0:w], w_hi[:, par, 0:w].bitcast(F32), ALU.subtract)
                pool.drain().then_inc(S("split_ready"), 1)
                pool.sem_inc(S(f"raw_free{slot}"), 1)

            def split_items(items, turn, n):
                done = 0
                for p, item in enumerate(items):
                    if item[0] == "C":
                        split(p % NS, turn + p // NS, n + done, done % 2)
                        done += 1

            for l in range(layers):
                for i in range(SMALL_HALVES):
                    split(i, HALVES_AT[l] // NS, l * SPLITS + i, i % 2, 4 * N_SMALL)
                with pool.Fori(0, KVH) as g:
                    split_items(group_items(l < DEPTH - 1), turn_of_group(l, g), split_of_group(l, g))
                split_items(GATE_LOT, turn_of_lot(l, 0), split_of_lot(l, 0))
                with pool.Fori(0, GDN_H) as h:
                    split_items(PLAIN_LOT, turn_of_lot(l, ("gdn", h)), split_of_lot(l, 1) + h * (2 * LOT))
                with pool.Fori(0, SB_H - 1) as h:
                    split_items(GATE_LOT, turn_of_lot(l, ("sb", h)), split_of_lot(l, GDN_H + 1) + h * (2 * LOT))
                with pool.Fori(0, TT) as n:
                    for k2 in range(KT // 2):
                        split(k2 % NS, n * (KT // 2 // NS) + (turn_of_out[l] + k2 // NS),
                              n * (KT // 2) + (split_of_lot(l, N_LOTS) + k2), k2 % 2)
            for t in range(2):
                pool.wait_ge(S("ln_g_done"), t + 1)
                pool.tensor_tensor(xres[:, t, :], xres[:, t, :], ln_gb[:, 1, :], ALU.add).then_inc(S("pool_out"), 1)

        @block.vector
        def _(dve):
            def drained(op):
                def run(*args, **kw):
                    made = op(*args, **kw)
                    dve.drain()
                    return made
                return run

            tt, ts, stt, cp, reduce, reciprocal, bn_stats, bn_aggr, fill = map(drained, (
                dve.tensor_tensor, dve.tensor_scalar, dve.scalar_tensor_tensor, dve.tensor_copy,
                dve.tensor_reduce, dve.reciprocal, dve.bn_stats, dve.bn_aggr, dve.memset))
            M, Ad, Su, Mx = ALU.mult, ALU.add, ALU.subtract, ALU.max
            sync = dve.drain

            dve.wait_ge(S("const_in"), 48)
            dve.wait_ge(S("pool_ready"), 1)
            R = lambda i: raw[0:32, i, TAPS - 1:]
            cp(R(1), R(0).bitcast(I32))
            ts(R(2), R(1), C("misc", 32)[:, 0:1], None, M)
            two_pi = 2 * np.pi
            c1 = 6.28125
            c2 = float(np.float32(two_pi - c1))
            c3 = float(two_pi - c1 - c2)
            for i, phase in enumerate((np.pi / 2, 0.0)):
                n, r = R(3), A(18 + i, 32)
                ts(n, R(2), float(1 / two_pi), float(phase / two_pi), M, Ad)
                ts(n, n, 12582912.0, None, Ad)
                ts(n, n, 12582912.0, None, Su)
                stt(r, n, -c1, R(2), M, Ad)
                stt(r, n, -c2, r, M, Ad)
                stt(r, n, -c3, r, M, Ad)
                ts(r, r, float(phase), None, Ad)
                ts(r, r, 3.1415925, -3.1415925, ALU.min, Mx)
            sync().then_inc(S("angles"), 1)
            dve.wait_ge(S("c_tanh"), 1)
            stt(cact[:, 1, :], cact[:, 0, :], 1.0, cact[:, 1, :], Ad, M)
            ts(cact[:, 1, :], cact[:, 1, :], 0.5, None, M)

            def rope(j_count, x32, n, at):
                dve.wait_ge(S("rot_done"), j_count + 1)
                tt(rope_a[:, 0:n], MB[0:32, 0:n], rope_cs[:, 1, at], M).then_inc(S("rot_used"), 1)
                tt(rope_b[:, 0:n], x32, rope_cs[:, 0, at], M)
                tt(x32, rope_a[:, 0:n], rope_b[:, 0:n], Ad).then_inc(S("roped"), 1)

            fill(acc0[0], 0.0).then_inc(S("acc_zero"), 1)
            for part in range(2):
                if part:
                    dve.wait_ge(S("rope_ready"), 1)
                    fill(acc0[1], 0.0).then_inc(S("acc_zero"), 1)
                dve.wait_ge(S("bmod_in"), part * 16 + 16)
                with dve.Fori(0, KT // NS) as k4:
                    for i in range(NS):
                        dve.wait_ge(S(f"mod_in{i}"), (k4 + (part * (KT // NS) + 1)) * 16)
                        stt(acc0[part], mod_ring[:, i, :], cact[:, 1, bass.ds(k4 * NS + i, 1)], acc0[part], M, Ad)\
                            .then_inc(S("mod_used"), 1)
                sync().then_inc(S("mod_sum"), 1)
            for part in range(2):
                dve.wait_ge(S("mod_done"), part + 1)
                cp(modT[:, part, :], MB[:, 0:KT]).then_inc(S("mod_copied"), 1)

            def add_mod(item, items, turn, k_first=0):
                p, m = items.index(item), item[1]
                part = acc[:, m % 2 * HALF:(m % 2 + 1) * HALF]
                dve.wait_ge(S(f"slot_in{p % NS}"), (turn + (p // NS + 1)) * 16)
                k = m // 2 if isinstance(k_first, int) else bass.ds(k_first + m // 2, 1)
                by = cact[:, 1, m // 2 + k_first:m // 2 + k_first + 1] if isinstance(k_first, int) else cact[:, 1, k]
                stt(part, ring[:, p % NS, :], by, part, M, Ad).then_inc(S(f"raw_free{p % NS}"), 1)

            for l in range(layers):
                has_next = l < DEPTH - 1
                dve.wait_ge(S("small_in"), l * 16 + 16)
                if l == 0:
                    ts(h_mod[:, 0, :], modT[:, 1, :], 1.0, None, Ad)
                    cp(h_mod[:, 1, :], modT[:, 0, :])
                else:
                    stt(h_mod[:, 0, :], modT[:, 1, :], 1.0, ln_before[:, 0, :], Ad, M)
                    stt(h_mod[:, 1, :], modT[:, 1, :], 1.0, ln_before[:, 1, :], Ad, M)
                    tt(h_mod[:, 1, :], h_mod[:, 1, :], modT[:, 0, :], Ad)
                for k in range(KT + 1):
                    if k < KT:
                        dve.wait_ge(S("xT_done"), l * KT + k + 1)
                        ts(A(16 + k % 4), TB[k % 2][:, :], h_mod[:, 0, k:k + 1], h_mod[:, 1, k:k + 1], M, Ad)\
                            .then_inc(S("h_read"), 1)
                        dve.sem_inc(S("h_tmp"), 1)
                    if k >= 1:
                        j = k - 1
                        dve.wait_ge(S("h_hi_ready"), l * KT + j + 1)
                        tt(h_lo[:, j, :], A(16 + j % 4), h_hi[:, j, :].bitcast(F32), Su).then_inc(S("h_ready"), 1)
                dve.wait_ge(S("gates_tanh"), l + 1)
                small = MB[:, 0:TT * 32].rearrange("p (t n) -> p t n", t=TT)
                th = A(17)[:, 0:TT * 24].rearrange("p (t n) -> p t n", t=TT)
                ga = A(18)[:, 0:24].rearrange("p (t h) -> p t h", t=TT)
                small_shape = (P, TT, GDN_H)
                tt(ga, small[:, :, 24:30], over(small_part("dt_bias").unsqueeze(1), small_shape), Ad).then_inc(S("ga_ready"), 1)
                ts(gates[:, :, :], th[:, :, 0:18], 0.5, 0.5, M, Ad)
                ts(coef[:, 1, :, :], th[:, :, 18:24], 0.5, 0.5, M, Ad)
                dve.wait_ge(S("ga_ln"), l + 1)
                ln = A(18)[:, 96:120].rearrange("p (t h) -> p t h", t=TT)
                sp_ = A(18)[:, 192:216].rearrange("p (t h) -> p t h", t=TT)
                stt(sp_, ga, 0.0, ln, Mx, Ad)
                ts(coef[:, 2, :, :], coef[:, 1, :, :], 0.5, None, M)
                stt(coef[:, 0, :, :], sp_, -1.0, over(ea[:, :].unsqueeze(1), small_shape), M, M).then_inc(S("g_ready"), 1)
                dve.wait_ge(S("gc_done"), l + 1)
                gc = coef[:, 3, :, :].rearrange("p t h -> p (t h)")
                cp(gc, SB_[0][:, 0:24])
                tt(A(18)[:, 160:184], SB_[0][:, 24:48], gc, Su)
                sync().then_inc(S("gc_ready"), 1)
                dve.wait_ge(S("gc_exp"), l + 1)
                tt(coef[:, 4, :, :].rearrange("p t h -> p (t h)"), coef[:, 1, :, :].rearrange("p t h -> p (t h)"),
                   A(18)[:, 128:152], M)
                sync().then_inc(S("coef_ready"), 1)
                if l:
                    dve.wait_ge(S("x_stored"), l * TT * 16)

                g_items = group_items(has_next)
                with dve.Fori(0, KVH) as g:
                    G = l * KVH + g
                    if has_next:
                        fill(acc[:, :], 0.0).then_inc(S("acc_zero"), 1)

                    def add_mods(m0, m1):
                        if has_next:
                            if m0 == 0:
                                dve.wait_ge(S("bmod_in"), (g + (sums_before[l] + 1)) * 16)
                            for m in range(m0, m1):
                                add_mod(("M", m), g_items, turn_of_group(l, g))

                    cp(gate_g[:, :, :], gates[:, :, bass.ds(g * 9, 9)])
                    for which in range(2):
                        dve.wait_ge(S("p_copied"), after("p_copied", l * LAYER_TILES + g * GROUP_TILES + which + 1))
                        src = v_raw[which]
                        windows = bass.AP(src.tensor, src.offset, [src.ap[0], [1, CMP_LEN], [CMP_STRIDE, N_CMP]])
                        tt(blocks_kv[which][:, 0:CMP_LEN * N_CMP].rearrange("p (t n) -> p t n", n=N_CMP), windows,
                           over(peT[:, which, :].unsqueeze(2), (P, CMP_LEN, N_CMP)), Ad).then_inc(S("blocks_ready"), 1)
                    for which in range(2):
                        dve.wait_ge(S("cmp_tanh"), G * 2 + which + 1)
                        hid = cmpb[:, 2 + which, 0:N_CMP]
                        stt(hid, cmpb[:, 4 + which, 0:N_CMP], 1.0, TB[which][:, 0:N_CMP], Ad, M)
                        ts(hid, hid, 0.5, None, M).then_inc(S("hid_ready"), 1)
                    first = CMP_LEN - 1
                    rope(G * 6, cmpb[0:32, 0, 0:N_CMP], N_CMP, slice(first, first + (N_CMP - 1) * CMP_STRIDE + 1, CMP_STRIDE))
                    rope(G * 6 + 1, kS[0:32, :], SEQ, slice(0, SEQ))
                    rope(G * 6 + 2, kW[0:32, :], SEQ, slice(0, SEQ))
                    rope(G * 6 + 3, qT[0][0:32, :], SEQ, slice(0, SEQ))

                    def silu_z(H, dst):
                        dve.wait_ge(S("z_tanh"), H + 1)
                        stt(dst, z_tanh, 1.0, z_raw, Ad, M).then_inc(S("sz_ready"), 1)

                    silu_z(G * GROUP, szq[0])
                    for r in range(GROUP):
                        H = G * GROUP + r
                        for s in range(NSA_STEPS):
                            if s in MOD_STEPS[r]:
                                add_mods(*MOD_STEPS[r][s])
                            if s == 0:
                                dve.wait_ge(S("cmp_scores"), H + 1)
                                shape = (P, TT, N_CMP)
                                mx, sm = tiny[:, 24:28], tiny[:, 28:32]
                                scores = SB_[0][:, 0:TT * 32].rearrange("p (t n) -> p t n", t=TT)[:, :, 0:N_CMP]
                                stt(cmp_s, scores, SCALE, C("cmp_add").rearrange("p (t n) -> p t n", t=TT), M, Ad)\
                                    .then_inc(S("cmp_scored"), 1)
                                reduce(mx, cmp_s, AX, Mx)
                                tt(cmp_s, cmp_s, over(mx.unsqueeze(2), shape), Su).then_inc(S("cmp_scored2"), 1)
                                dve.wait_ge(S("cmp_exp"), H + 1)
                                tt(cmp_s, cmp_s, C("cmp_mul").rearrange("p (t n) -> p t n", t=TT), M)
                                reduce(sm, cmp_s, AX, Ad)
                                ts(sm, sm, 1e-30, None, Mx)
                                reciprocal(sm, sm)
                                tt(sm, sm, gate_g[:, :, 3 * r], M)
                                tt(cmp_p, cmp_s, over(sm.unsqueeze(2), shape), M).then_inc(S("cmp_probs"), 1)
                            if 1 <= s <= 8:
                                u = s - 1
                                i, w, b = u % TT, (u % TT + 1) * P, SB_[(u + 1) % 2]
                                dve.wait_ge(S("scores"), H * 8 + u + 1)
                                reduce(tiny[:, 30:31], b[:, 0:w], AX, Mx)
                                ts(tiny[:, u:u + 1], tiny[:, 30:31], -SCALE, None, M).then_inc(S("max_ready"), 1)
                                if s == 1:
                                    dve.wait_ge(S("cmp_pT"), H + 1)
                                    cp(cmp_pT, TB[0][0:N_CMP, :]).then_inc(S("cmp_pT_ready"), 1)
                                dve.wait_ge(S("exp_done"), after("exp_done", H * 8 + u + 1))
                                reciprocal(tiny[:, 31:32], tiny[:, 8 + u:9 + u])
                                ts(prob[u % 2][:, 0:w], prob[u % 2][:, 0:w], tiny[:, 31:32],
                                   gate_g[:, i, 3 * r + 1 + u // TT:3 * r + 2 + u // TT], M, M).then_inc(S("probs"), 1)
                            if s == 8 and r < GROUP - 1:
                                rope(G * 6 + 4 + r, qT[(r + 1) % 2][0:32, :], SEQ, slice(0, SEQ))
                        if r < GROUP - 1:
                            silu_z(H + 1, szq[(r + 1) % 2])
                        dve.wait_ge(S("pv_done"), after("pv_done", H * 8 + 8))
                        stt(yT[:, bass.ds(g * GROUP + r, 1), :].rearrange("p a n -> p (a n)"), OB[:, :], 0.5,
                            szq[r % 2], M, M).then_inc(S("y_ready"), 1)
                    if has_next:
                        sync().then_inc(S("mod_sum"), 1)
                        dve.wait_ge(S("mod_done"), g + (sums_before[l] + 1))
                        cp(modT[:, bass.ds(g, 1), :].rearrange("p a n -> p (a n)"), MB[:, 0:KT])\
                            .then_inc(S("mod_copied"), 1)

                fill(acc[:, :], 0.0).then_inc(S("acc_zero"), 1)
                dve.wait_ge(S("bmod_in"), (sums_before[l] + (3 if has_next else 1)) * 16)
                for m in range(8):
                    add_mod(("M", m), GATE_LOT, turn_of_lot(l, 0))

                with dve.Fori(0, GDN_H) as h:
                    D = l * GDN_H + h

                    def ready(name):
                        dve.wait_ge(S(name), D + 1)

                    cp(coef_h[:, :, :], coef[:, :, :, bass.ds(h, 1)].rearrange("p a t h -> p (a t) h").rearrange(
                        "p (a t) h -> p a (t h)", t=TT))
                    conv_heads = taps.rearrange("p (k h) -> p k h", h=GDN_H)
                    cp(conv_h[:, :, :].rearrange("p t x -> p (t x)"),
                       conv_heads[:, :, bass.ds(h, 1)].rearrange("p k h -> p (k h)"))
                    fill(state[:, :], 0.0)
                    sync().then_inc(S("rec_state"), 1)
                    per_token = lambda i: over(coef_h[:, i, :].unsqueeze(2), BIG)
                    tt(tiles(A(3)), over(C("cumul").unsqueeze(1), BIG), per_token(0), M).then_inc(S("gdn_gsel"), 1)
                    for i, (src, dst, part) in enumerate(((0, 0, 1), (1, 6, 0), (2, 8, 2))):
                        dve.wait_ge(S("p_copied"), after("p_copied", tile_of_lot(l, h) + src + 1))
                        for k in range(TAPS):
                            tap, x_ = conv_h[:, k, part:part + 1], raw[:, src, k:k + SEQ]
                            if k == 0:
                                ts(A(dst), x_, tap, None, M)
                            else:
                                stt(A(dst), x_, tap, A(dst), M, Ad)
                        sync().then_inc(S("gdn_conv"), 1)
                        dve.sem_inc(S(f"raw_used{src}"), 1)
                    for i, (x_, th) in enumerate(((0, 1), (6, 9), (8, 10))):
                        dve.wait_ge(S("gdn_tanh"), D * 3 + i + 1)
                        stt(A(x_), A(th), 1.0, A(x_), Ad, M).then_inc(S("gdn_silu"), 1)
                    sync().then_inc(S("gdn_v"), 1)
                    ready("gdn_gcb")
                    tt(tiles(A(5)), tiles(MB[:, :]), per_token(3), Su)
                    ts(A(5), A(5), 0.0, None, Mx).then_inc(S("gdn_d"), 1)
                    ready("gdn_ztanh")
                    stt(A(19), A(11), 1.0, raw[:, 3, TAPS - 1:], Ad, M).then_inc(S("raw_used3"), 1)
                    ready("gdn_rk")
                    tt(A(0), A(0), A(2), M).then_inc(S("gdn_k"), 1)
                    ready("gdn_rq")
                    tt(A(6), A(6), A(7), M).then_inc(S("gdn_q"), 1)
                    ready("gdn_decay")
                    tt(tiles(A(2)), tiles(A(5)), per_token(1), M)
                    tt(tiles(A(10)), tiles(A(5)), over(C("incl").unsqueeze(1), BIG), M)
                    ready("gdn_kT")
                    tt(tiles(A(1)), tiles(TB[0][:, :]), per_token(4), M)
                    tt(tiles(A(9)), tiles(TB[0][:, :]), per_token(5), M)
                    ready("gdn_kk")
                    tt(A(3), TB[1][:, :], A(2), M).then_inc(S("gdn_lower"), 1)
                    ready("gdn_qk")
                    tt(A(10), SB_[0][:, :], A(10), M).then_inc(S("gdn_intra"), 1)
                    ready("gdn_egb")
                    tt(A(6), A(6), A(4), M).then_inc(S("gdn_qh"), 1)
                    tt(tiles(A(11)), tiles(A(3)), over(C("merge1").unsqueeze(1), BIG), M)
                    ready("gdn_vT")
                    tt(tiles(A(8)), tiles(SB_[1][:, :]), per_token(2), M).then_inc(S("gdn_bv"), 1)

                    def mask(v):
                        m = ((1,) + LEVELS)[v]
                        tt(tiles(A(14 + v % 2)), tiles(A(12)), over(C(f"mergeT{m}").unsqueeze(1), BIG), M)\
                            .then_inc(S("gdn_ct"), 1)

                    ready("gdn_lT_copied")
                    mask(0)
                    tt(tiles(A(11)), over(ident.unsqueeze(1), BIG), tiles(A(11)), Su)
                    tt(tiles(A(13)), over(ident.unsqueeze(1), BIG), tiles(A(14)), Su)
                    sync().then_inc(S("gdn_T"), 1)
                    mask(1)
                    mask(2)
                    for v in range(len(LEVELS)):
                        dve.wait_ge(S("gdn_TCT"), D * 5 + v + 1)
                        if v < len(LEVELS) - 1:
                            tt(A(11), A(11), SB_[0][:, :], Su)
                        tt(A(13), A(13), SB_[1][:, :], Su)
                        sync().then_inc(S("gdn_T" if v < len(LEVELS) - 1 else "gdn_Tt"), 1)
                        if v < len(LEVELS) - 2:
                            mask(v + 3)
                    for i in range(SEQ // CHUNK):
                        dve.wait_ge(S("rec_kv"), D * 8 + i + 1)
                        end = (i + 1) * CHUNK - 1
                        stt(state[:, :], state[:, :], A(4)[:, end:end + 1], TB[i % 2][:, 0:HD], M, Ad)\
                            .then_inc(S("rec_state"), 1)
                    ready("gdn_ro")
                    tt(A(14), OB[:, :], A(15), M)
                    stt(yT[:, bass.ds(h + NSA_H, 1), :].rearrange("p a n -> p (a n)"), A(14), gnorm,
                        A(19), M, M).then_inc(S("y_ready"), 1)

                def split_y(k):
                    dve.wait_ge(S("y_hi"), l * MIX_T + k + 1)
                    tt(h_lo[:, k, :], yT[:, k, :], h_hi[:, k, :].bitcast(F32), Su).then_inc(S("y_split"), 1)

                def stick(h, lot):
                    B = l * SB_H + h
                    for i in range(2):
                        dve.wait_ge(S("p_copied"), after("p_copied", tile_of_lot(l, GDN_H + h) + i + 1))
                        ts(A(i), raw[:, i, TAPS - 1:], (1.0, SCALE)[i], None, M).then_inc(S(f"raw_used{i}"), 1)
                    sync().then_inc(S("sb_qk"), 1)
                    dve.wait_ge(S("sb_vT"), B + 1)
                    cp(A(2), MB[:, :]).then_inc(S("sb_v"), 1)
                    dve.sem_inc(S("raw_used2"), 1)
                    dve.wait_ge(S("sb_ztanh"), B + 1)
                    stt(A(3), A(4), 1.0, raw[:, 3, TAPS - 1:], Ad, M).then_inc(S("raw_used3"), 1)
                    for s in range(TT + 1):
                        if lot is None:
                            if s < TT:
                                for k in range(s * 4, min(s * 4 + 4, MIX_T - 1)):
                                    split_y(k)
                        elif s < TT:
                            for m in (2 * s, 2 * s + 1):
                                add_mod(("M", m), GATE_LOT, turn_of_lot(l, ("sb", h)), h * 4 + 4)
                        if s < TT:
                            j, w = TT - 1 - s, (s + 1) * P
                            dve.wait_ge(S("sb_ln"), B * TT + s + 1)
                            stt(A(9 + j)[:, 0:w], SB_[s % 2][:, 0:w], 0.0, A(5 + s % 2)[:, 0:w], Mx, Ad)
                            tt(A(13 + s % 2)[:, 0:w], SB_[s % 2][:, 0:w], A(9 + j)[:, 0:w], Su)\
                                .then_inc(S("lb_ready"), 1)
                            tt(A(9 + j)[:, 0:P], A(9 + j)[:, 0:P], C("past"), M)
                            sync().then_inc(S("spm_ready"), 1)
                        if s >= 1:
                            w = s * P
                            lb = A(13 + (s - 1) % 2)[:, 0:w]
                            dve.wait_ge(S("sb_acc"), B * TT + s)
                            tt(lb, lb, TB[(s - 1) % 2][:, 0:w], Su).then_inc(S("sb_arg"), 1)
                            a = A(16 - s % 2)[:, 0:P]
                            dve.wait_ge(S("sb_exp"), after("sb_exp", B * TT + s))
                            tt(a, a, C("past"), M).then_inc(S("sb_a"), 1)
                    dve.wait_ge(S("sb_pv"), after("sb_pv", B * TT + TT))
                    at = yT[:, MIX_T - 1, :] if isinstance(h, int) else \
                        yT[:, bass.ds(h + (NSA_H + GDN_H), 1), :].rearrange("p a n -> p (a n)")
                    stt(at, OB[:, :], 0.5, A(3), M, M).then_inc(S("y_ready"), 1)

                with dve.Fori(0, SB_H - 1) as h:
                    stick(h, h)
                sync().then_inc(S("mod_sum"), 1)
                stick(SB_H - 1, None)
                split_y(MIX_T - 1)

                dve.wait_ge(S("gate_done"), l + 1)
                for n in range(TT):
                    ts(gateb[:, n * SEQ:(n + 1) * SEQ], ODD[n][:, :], 1.0, None, Ad)
                sync().then_inc(S("gate_ready"), 1)
                for n in range(TT):
                    outs, cols = (bank[2:6], ODD)[n % 2], slice(n * SEQ, (n + 1) * SEQ)
                    dve.wait_ge(S(f"xo_in{n}"), 16 + l * 48)
                    if l:
                        g_, b_ = (raw[:, n % 2 * 2 + a, TAPS - 1:] for a in range(2))
                        shape = (P, TT, SEQ)
                        tt(xres[:, :, cols], xres[:, :, cols], over(g_.unsqueeze(1), shape), M)
                        tt(xres[:, :, cols], xres[:, :, cols], over(b_.unsqueeze(1), shape), Ad)\
                            .then_inc(S("lnb_used"), 1)
                    for t in range(TT):
                        if t < TT - 1:
                            dve.wait_ge(S("o_done"), (l * TT + n) * (TT - 1) + t + 1)
                        else:
                            dve.wait_ge(S("split_used"), after("split_used", split_of_lot(l, N_LOTS) + (n + 1) * (KT // 2)))
                        tt(A(16 + t), outs[t][:, :], gateb[:, cols], M).then_inc(S("o_used"), 1)
                        x_ = xres[:, t, cols]
                        stt(x_, x_, ALPHA, A(16 + t), M, Ad)
                        bn_stats(stats[:, t, n, :], x_)
                for t in range(TT):
                    bn_aggr(meanvar[:, t, :], stats[:, t, :, :])
                sync().then_inc(S("var_ready"), 1)
                dve.wait_ge(S("rstd_ready"), l + 1)
                stt(tiny[:, 36:40], meanvar[:, :, 0], -1.0, tiny[:, 20:24], M, M).then_inc(S("nmr_ready"), 1)
                for t in (2, 3):
                    x_ = xres[:, t, :]
                    ts(x_, x_, meanvar[:, t, 0:1], tiny[:, 20 + t:21 + t], Su, M).then_inc(S("norm_dve"), 1)
            dve.wait_ge(S("ln_in"), 16)
            for t in range(TT):
                if t < 2:
                    dve.wait_ge(S("norm_act"), 2 * (layers - 1) + t + 1)
                x_ = xres[:, t, :]
                tt(x_, x_, ln_gb[:, 0, :], M).then_inc(S("ln_g_done"), 1)
                if t >= 2:
                    tt(x_, x_, ln_gb[:, 1, :], Ad).then_inc(S("dve_out"), 1)


def by_row_tiles(w):
    *lead, rows, n = w.shape
    return w.reshape(*lead, rows // P, P, n).swapaxes(-3, -2).reshape(*lead, P, rows // P * n)


def columns(w_in, start, i):
    return by_row_tiles(w_in[:, :, start + i * P:start + (i + 1) * P])


def halves(loads):
    return [loads[..., :HALF], loads[..., HALF:]]


def weight_stream(w_mod, w_in, w1_k, w1_v, w_out):
    loads = []

    def mod_half(l, part, m):
        return halves(w_mod[l, m // 2::KT, part * DM:(part + 1) * DM])[m % 2]

    def lot(l, n, items, k_first):
        starts, h = ((C_GK, C_GQ, C_GV, C_GZ), n) if n < GDN_H else ((C_SK, C_SQ, C_SV, C_SZ), n - GDN_H)
        tiles = [halves(columns(w_in, start, h)[l]) for start in starts]
        for item in items:
            loads.append(tiles[item[1]][item[2]] if item[0] == "C" else mod_half(l, 2, item[1] + 2 * k_first))

    for l in range(DEPTH):
        for g in range(KVH):
            tiles = [halves(columns(w_in, start, g)[l]) for start in (C_KC, C_VC, C_KS, C_VS, C_KW, C_VW)]
            for r in range(GROUP):
                tiles += [halves(columns(w_in, start, g * GROUP + r)[l]) for start in (C_NQ, C_NZ)]
            w1 = [h for w in (w1_k, w1_v) for rows in (w[l, :DM], w[l, DM:]) for h in halves(by_row_tiles(rows))]
            for item in group_items(l < DEPTH - 1):
                if item[0] == "C":
                    loads.append(tiles[item[1]][item[2]])
                elif item[0] == "D":
                    loads.append(w1[item[1]])
                else:
                    loads.append(mod_half(l + 1, g, item[1]))
        lot(l, 0, GATE_LOT, 0)
        for n in range(1, GDN_H + 1):
            lot(l, n, PLAIN_LOT, 0)
        for n in range(GDN_H + 1, N_LOTS):
            lot(l, n, GATE_LOT, 4 * (n - GDN_H))
        for n in range(TT):
            for k2 in range(KT // 2):
                loads.append(by_row_tiles(w_out[l, k2 * 2 * P:(k2 + 1) * 2 * P, n * SEQ:(n + 1) * SEQ]))
    return np.stack(loads)


def small_weights(w2_k, w2_v, conv_w, norm_g, pe_k, pe_v, dt_bias, a_log, ln_g, ln_b):
    taps = conv_w.reshape(DEPTH, TAPS * 18, P).swapaxes(1, 2)
    rows = [np.broadcast_to(v[:, None, :], (DEPTH, P, GDN_H)) for v in (dt_bias, a_log)]
    before = [np.roll(v, 1, 0).reshape(DEPTH, KT, P).swapaxes(1, 2) for v in (ln_g, ln_b)]
    return np.concatenate([w2_k, w2_v, taps, norm_g[:, :, None],
                           pe_k.swapaxes(1, 2), pe_v.swapaxes(1, 2), *rows, *before], 2)


def small_columns(w_in):
    few = np.concatenate([w_in[:, :, C_NG:C_NG + 18], w_in[:, :, C_GB:C_GB + 2 * GDN_H]], 2)
    return by_row_tiles(few).reshape(DEPTH, P, SMALL_HALVES, 4 * N_SMALL).swapaxes(1, 2)


def kernel(x, c, positions, w_mod, b_mod, w_in, w_out, ln_g, ln_b, cmp_pe_k, cmp_pe_v, cmp_w1_k,
           cmp_w2_k, cmp_w1_v, cmp_w2_v, gdn_conv_w, gdn_a_log, gdn_dt_bias, gdn_norm_g):
    import concourse.bacc as _bacc
    from concourse.bass_utils import run_bass_kernel_spmd as _run

    nc = _bacc.Bacc("TRN2", target_bir_lowering=False, num_devices=1)
    const, where = constants()
    arrays = {
        "x": x, "positions": positions, "c": c, "b_mod": b_mod,
        "mod0": np.concatenate([w_mod[0].reshape(P, KT, 3, DM)[:, :, part].swapaxes(0, 1) for part in range(2)]),
        "small_cols": small_columns(w_in),
        "stream": weight_stream(w_mod, w_in, cmp_w1_k, cmp_w1_v, w_out),
        "small": small_weights(cmp_w2_k, cmp_w2_v, gdn_conv_w, gdn_norm_g, cmp_pe_k, cmp_pe_v,
                               gdn_dt_bias, gdn_a_log, ln_g, ln_b),
        "lns": np.concatenate([ln_g, ln_b], 1),
        "const": const,
    }
    arrays = {f"in_{name}": np.ascontiguousarray(a) for name, a in arrays.items()}
    args = [nc.dram_tensor(n, a.shape, mybir.dt.from_np(a.dtype), kind="ExternalInput").ap()
            for n, a in arrays.items()]
    out = nc.dram_tensor("out_0", (1, SEQ, DM), F32, kind="ExternalOutput").ap()
    build(nc, *args, out, where)
    r = _run(nc, [arrays], core_ids=[0])
    return r.results[0]["out_0"]
```

```python
from contextlib import ExitStack

import numpy as np

import concourse.bass as bass
from concourse import mybir

F32 = mybir.dt.float32
F32R = mybir.dt.float32r
I32 = mybir.dt.int32
ALU = mybir.AluOpType
ACT = mybir.ActivationFunctionType
AX = mybir.AxisListType.X

P = 128
DEPTH, SEQ, DM, HD = 2, 512, 2048, 128
ROPE_HALF, ROPE_THETA = 16, 500000.0
KVH, GROUP, CMP_LEN, CMP_STRIDE = 2, 3, 32, 16
GDN_H, TAPS, CHUNK = 6, 4, 64
SB_H = 4
NSA_H = KVH * GROUP
NSA_W, KV_W, GDN_W, SB_W = 6 * HD, 2 * HD, 6 * HD, 4 * HD
N_CMP = (SEQ - CMP_LEN) // CMP_STRIDE + 1
SCALE = HD ** -0.5
ALPHA = (2 * DEPTH) ** 0.25
LN_EPS, RMS_EPS, NEG = 1e-5, 1e-6, -1e30
WIDTHS = (NSA_W, KV_W, KV_W, KV_W, KV_W, KV_W, KV_W, 18, NSA_W, GDN_W, GDN_W, GDN_W, 6, 6, GDN_W,
          SB_W, SB_W, SB_W, SB_W)
STARTS = [0]
for _w in WIDTHS:
    STARTS.append(STARTS[-1] + _w)
(C_NQ, C_KC, C_VC, C_KS, C_VS, C_KW, C_VW, C_NG, C_NZ, C_GQ, C_GK, C_GV, C_GB, C_GA, C_GZ,
 C_SQ, C_SK, C_SV, C_SZ, IN_COLS) = STARTS

KT = DM // P
TT = SEQ // P
NS = 4
HALF = 8 * P
N_SMALL = 30
MIX_T = (NSA_W + GDN_W + SB_W) // P

SMALL_HALVES = 4


def mixed(tiles, m_each, m_first=0):
    items, m = [], m_first
    for i, t in enumerate(tiles):
        for half in range(2):
            items.append(("C", t, half))
            items += [("M", m + j) for j in range(m_each)]
            m += m_each
    return items


def group_items(has_next):
    items = mixed((0, 1), 0) + [("D", i) for i in range(8)] + mixed(range(2, 8), 0)
    if not has_next:
        return items + mixed(range(8, 14), 0)
    return items + mixed((8, 9), 2) + mixed((10, 11), 2, 8) + mixed((12, 13), 4, 16)


LOT = 4
N_LOTS = GDN_H + SB_H
FIRST_TILE = mixed([0], 0)
GDN_ITEMS = mixed(range(LOT), 0)
SB_ITEMS = mixed(range(LOT), 1)
SB_2_ITEMS = mixed(range(2), 2)
SB_3_ITEMS = mixed(range(1), 0) + [("M", m) for m in range(8)]
GROUP_TILES = 14
LAYER_TILES = KVH * GROUP_TILES + (N_LOTS - 1) * LOT
OUT_HALVES = 2 * KT
LEVELS = (2, 4, 8, 16, 32)


def layout(has_next):
    group = len(group_items(has_next))
    at, n = {"group": SMALL_HALVES, "group_len": group}, SMALL_HALVES + KVH * group
    at["first"] = n
    n += len(FIRST_TILE)
    at["gdn"] = n
    n += GDN_H * len(GDN_ITEMS)
    at["sb"] = n
    n += (SB_H - 2) * len(SB_ITEMS)
    at["sb_2"] = n
    n += len(SB_2_ITEMS)
    at["sb_3"] = n
    n += len(SB_3_ITEMS)
    at["out"] = n
    at["end"] = n + OUT_HALVES
    return at


LAYOUTS = [layout(l < DEPTH - 1) for l in range(DEPTH)]
STREAM_AT = [sum(a["end"] - SMALL_HALVES for a in LAYOUTS[:l]) for l in range(DEPTH)]
HALVES_AT = [sum(a["end"] for a in LAYOUTS[:l]) for l in range(DEPTH)]
SPLITS = SMALL_HALVES + 2 * LAYER_TILES + OUT_HALVES


SMALL = {"w2": 2 * HD, "taps": TAPS * 18, "norm_g": 1, "pe": 2 * CMP_LEN,
         "dt_bias": GDN_H, "a_log": GDN_H, "ln_before": 2 * KT}
SMALL_AT, SMALL_W = {}, 0
for _name, _w in SMALL.items():
    SMALL_AT[_name] = (SMALL_W, _w)
    SMALL_W += _w


def constants():
    r = np.arange(P)
    row, col = r[:, None], r[None, :]
    same = row // CHUNK == col // CHUNK
    blocks = {
        "ident": (row == col),
        "ones": np.ones((P, P)),
        "after": (row > col),
        "causal": np.where(col <= row, 0.0, NEG),
        "past": (row < col),
        "cumul": same & (row <= col),
        "chunk": same,
        "incl": same & (row >= col),
        "ident_c": (row % CHUNK == col[:, :CHUNK]),
        "merge1_c": (row % CHUNK // 2 == col[:, :CHUNK] // 2) & (row % 2 == 1) & (col[:, :CHUNK] % 2 == 0),
    }
    for m in (1,) + LEVELS:
        lower = (row // (2 * m) == col // (2 * m)) & (row % (2 * m) >= m) & (col % (2 * m) < m)
        blocks[f"mergeT{m}"] = lower.T
    t = np.arange(TT)[None, :, None] * P + r[:, None, None]
    seen = (np.arange(N_CMP) * CMP_STRIDE + CMP_LEN - 1)[None, None, :] <= t
    blocks["cmp_add"] = np.where(seen, 0.0, NEG).reshape(P, -1)
    blocks["cmp_mul"] = seen.reshape(P, -1)
    rot = np.zeros((P, 2 * ROPE_HALF))
    for i in range(ROPE_HALF):
        rot[ROPE_HALF + i, i] = -1.0
        rot[i, ROPE_HALF + i] = 1.0
    blocks["rot"] = rot
    inv = np.float32(ROPE_THETA) ** (-np.arange(ROPE_HALF, dtype=np.float32) * np.float32(2.0)
                                     / np.float32(2 * ROPE_HALF))
    misc = np.zeros((P, 2))
    misc[:2 * ROPE_HALF, 0] = np.tile(inv, 2)
    blocks["misc"] = misc
    at, where = 0, {}
    for name, b in blocks.items():
        where[name] = (at, b.shape[1])
        at += b.shape[1]
    return np.concatenate([np.asarray(b, np.float32) for b in blocks.values()], 1), where


def build(nc, x, positions, c, b_mod, mod0, small_cols, stream, small, lns, const, out, where, layers=DEPTH):
    x_norm = nc.dram_tensor("x_norm", (TT, P, DM), F32, kind="Internal").ap()
    ctx = ExitStack()
    with ctx:
        def sb(name, shape, dt=F32):
            return ctx.enter_context(nc.sbuf_tensor(name, shape, dt))

        h_hi = sb("h_hi", [P, KT, SEQ], F32R)
        h_lo = sb("h_lo", [P, KT, SEQ], F32R)
        yT = sb("yT", [P, MIX_T, SEQ])
        ring = sb("ring", [P, NS, HALF])
        w_hi = sb("w_hi", [P, 2, HALF], F32R)
        w_lo = sb("w_lo", [P, 2, HALF], F32R)
        acc = sb("acc", [P, DM])
        cst = sb("cst", [P, const.shape[1]])
        rope_cs = sb("rope_cs", [2 * ROPE_HALF, 2, SEQ])
        raw = sb("raw", [P, LOT, TAPS - 1 + SEQ])
        arena = sb("arena", [P, 20, SEQ])
        state = sb("state", [P, HD])
        vnew = sb("vnew", [P, 2, HD])
        sm_all = sb("sm_all", [P, SMALL_W])
        cact = sb("cact", [P, 2, KT])
        modT = sb("modT", [P, 2, KT])
        ident_r = sb("ident_r", [P, P], F32R)
        causal_r = sb("causal_r", [P, P], F32R)
        h_mod = sb("h_mod", [P, 2, KT])
        ea = sb("ea", [P, GDN_H])
        gates = sb("gates", [P, TT, 18])
        gate_g = sb("gate_g", [P, TT, 9])
        coef = sb("coef", [P, 6, TT, GDN_H])
        coef_h = sb("coef_h", [P, 6, TT])
        conv_h = sb("conv_h", [P, TAPS, 3])
        tiny = sb("tiny", [P, 40])
        stats = sb("stats", [P, TT, 4, 6])
        meanvar = sb("meanvar", [P, TT, 2])
        cmpb = sb("cmpb", [P, 6, 32])
        vcmp = sb("vcmp", [P, HD])
        hidden = sb("hidden", [N_CMP, 2, HD])

        def C(name, parts=P):
            at, n = where[name]
            return cst[0:parts, at:at + n]

        def small_part(name):
            at, n = SMALL_AT[name]
            return sm_all[:, at:at + n]

        w2 = small_part("w2").rearrange("p (a n) -> p a n", a=2)
        peT = small_part("pe").rearrange("p (a t) -> p a t", a=2)
        taps, gnorm = small_part("taps"), small_part("norm_g")
        ident, ones = C("ident"), C("ones")
        ln_before = small_part("ln_before").rearrange("p (a k) -> p a k", a=2)
        xres = arena[:, 0:16, :].rearrange("p (t a) b -> p t (a b)", t=TT)
        gateb = yT[:, 0:4, :].rearrange("p a b -> p (a b)")
        ln_gb = yT[:, 4:12, :].rearrange("p (a b) c -> p a (b c)", a=2)
        acc0 = [acc[:, :], arena[:, 16:20, :].rearrange("p a b -> p (a b)")]
        mod_ring = yT[:, :, :].rearrange("p (a b) c -> p a (b c)", a=NS)

        bank = [ctx.enter_context(nc.psum_tensor(f"bank{i}", [P, SEQ], F32)) for i in range(8)]
        PJ, SB_, TB, OB, MB = bank[0:2], bank[2:4], bank[4:6], bank[6], bank[7]
        XT = [bank[4], bank[5], bank[2], bank[3]]
        ODD = [bank[0], bank[1], bank[6], bank[7]]

        def A(i, parts=P):
            return arena[0:parts, i, :]

        def tiles(ap):
            return ap.rearrange("p (t n) -> p t n", t=TT)

        def over(ap, shape):
            return ap.broadcast_to(shape)

        BIG, NARROW = (P, TT, P), (P, TT, CHUNK)

        def narrow(ap):
            return ap[:, 0:TT * CHUNK].rearrange("p (t n) -> p t n", t=TT)

        def own(ap, half):
            at = slice(half * CHUNK, (half + 1) * CHUNK)
            return tiles(ap)[at, :, at]

        blocks_kv = [arena[:, 2 * i:2 * i + 2, :].rearrange("p a b -> p (a b)") for i in range(2)]
        prob, probT = [A(0), A(1)], [A(2), A(3)]
        kS, kW, vS, vW = A(4), A(5), A(6), A(7)
        qT, szq, z_raw, z_tanh = [A(8), A(9)], [A(10), A(11)], A(12), A(13)
        v_raw = [A(14), A(15)]
        rope_a, rope_b = A(16, 32), A(17, 32)
        cmp_s = A(18)[:, 0:TT * N_CMP].rearrange("p (t n) -> p t n", t=TT)
        cmp_p = A(18)[:, 256:256 + TT * N_CMP].rearrange("p (t n) -> p t n", t=TT)
        cmp_pT = A(19, N_CMP)

        semaphores = {}

        def S(name):
            if name not in semaphores:
                semaphores[name] = ctx.enter_context(nc.semaphore(name))
            return semaphores[name]

        lv_buf = A(11)[:, TT * CHUNK:]
        lv_n = narrow(lv_buf)
        hid_tanh = A(16, N_CMP)[:, 0:2 * HD].rearrange("p (a n) -> p a n", a=2)

        CREDITS = {"mod_used": NS, "split_used": 2, "p_copied": 1, "rot_used": 1, "exp_done": 1,
                   "pt_ready": 1, "pv_done": 1, "y_ready": 1, "sz_ready": 1,
                   "o_used": 8, "rec_vn": 1, "rec_state": 1, "gdn_lv_y": 1, "lb_ready": 1,
                   "sb_exp": 1, "sb_pv": 1}
        for i in range(NS):
            CREDITS[f"raw_free{i}"] = 1
        for i in range(LOT):
            CREDITS[f"raw_used{i}"] = 1

        def after(name, n):
            return n + CREDITS.get(name, 0)

        for name in CREDITS:
            S(name)
        for name in ["const_in", "x_in", "small_in", "ln_in", "x_stored", "bmod_in", "slot_in0", "slot_in1", "slot_in2", "slot_in3"]:
            S(name)

        block = ctx.enter_context(nc.Block())

        def spread(n, weights):
            at = [round(n * sum(weights[:s]) / sum(weights)) for s in range(len(weights) + 1)]
            return [b - a for a, b in zip(at, at[1:])]

        REC = 3 + 2 * len(LEVELS) + 1
        GDN_STEPS = REC + 2 * (SEQ // CHUNK) + 1
        gdn_weights = [3] * 3 + [1.2] * (REC - 3) + [1] * (GDN_STEPS - REC)
        gdn_fill = spread(LOT * KT, gdn_weights)
        SB_STEPS = TT + 2
        sb_fill = spread(LOT * KT, [1, 1, 1, 1, 1.3, 1.3])
        sb_2_fill = spread(2 * KT, [1] * SB_STEPS)
        sb_3_fill = spread(KT, [1, 1, 1] + [0] * (SB_STEPS - 3))
        NSA_STEPS = 11
        nsa_fill = spread(2 * KT, [1, 2] + [1] * (NSA_STEPS - 2))

        MOD_STEPS = [{s: (s, s + 1) for s in range(8)}, {s: (8 + s, 9 + s) for s in range(8)},
                     {s: (16 + 2 * s, 18 + 2 * s) for s in range(8)}]

        def ended(fill, s):
            return range(sum(fill[:s]) // KT, sum(fill[:s + 1]) // KT)

        def parts(fill, s):
            a, b = sum(fill[:s]), sum(fill[:s + 1])
            spans = [(i, max(a - i * KT, 0), min(b - i * KT, KT)) for i in range(sum(fill) // KT)]
            return [x for x in spans if x[1] < x[2]]

        def tile_of_lot(l, n):
            return l * LAYER_TILES + KVH * GROUP_TILES + (n - 1) * LOT

        def split_of_group(l, g):
            return l * SPLITS + SMALL_HALVES + g * (2 * GROUP_TILES)

        def split_of_lot(l, n):
            return l * SPLITS + SMALL_HALVES + 2 * KVH * GROUP_TILES + (n - 1) * (2 * LOT)

        def turn_of_group(l, g):
            return (HALVES_AT[l] + LAYOUTS[l]["group"]) // NS + g * (LAYOUTS[l]["group_len"] // NS)

        def place(l, kind, p, more=0):
            at = HALVES_AT[l] + LAYOUTS[l][kind] + p
            return at % NS, at // NS + more

        turn_of_out = [(HALVES_AT[l] + LAYOUTS[l]["out"]) // NS for l in range(DEPTH)]
        sums_before = [2 + l + 2 * min(l, DEPTH - 1) for l in range(DEPTH)]

        @block.sync
        def _(sp):
            sp.dma_start(cst[:, :], const).then_inc(S("const_in"), 16)
            sp.dma_start(cact[:, 1, :], c[0].rearrange("(p k) -> p k", k=KT)).then_inc(S("const_in"), 16)
            sp.dma_start(raw[0:32, 0, TAPS - 1:].bitcast(I32), positions.broadcast_to((32, SEQ)))\
                .then_inc(S("const_in"), 16)
            with sp.Fori(0, 2 * KT // NS) as n4:
                for i in range(NS):
                    sp.wait_ge(S("mod_used"), n4 * NS + i + 1)
                    sp.dma_start(mod_ring[:, i, :], mod0[bass.ds(n4 * NS + i, 1)].rearrange("a p n -> (a p) n"))\
                        .then_inc(S(f"mod_in{i}"), 16)

            for l in range(layers):
                if l == 0:
                    sp.wait_ge(S("rope_ready"), 1)
                    sp.dma_start(xres, x[0].rearrange("(t p) n -> p t n", p=P)).then_inc(S("x_in"), 16)
                    sp.dma_start(sm_all[:, :], small[0]).then_inc(S("small_in"), 16)
                for i in range(SMALL_HALVES):
                    sp.wait_ge(S(f"raw_free{i}"), HALVES_AT[l] // NS + 1)
                    sp.dma_start(ring[:, i, 0:4 * N_SMALL], small_cols[l, i]).then_inc(S(f"slot_in{i}"), 16)

                def load(first, n):
                    with sp.Fori(0, n // NS) as n4:
                        for i in range(NS):
                            sp.wait_ge(S(f"raw_free{i}"), n4 + ((HALVES_AT[l] + first) // NS + 1))
                            sp.dma_start(ring[:, i, :], stream[bass.ds(
                                n4 * NS + (STREAM_AT[l] + first - SMALL_HALVES + i), 1)].rearrange(
                                    "a p n -> (a p) n")).then_inc(S(f"slot_in{i}"), 16)

                at = LAYOUTS[l]
                load(SMALL_HALVES, at["out"] - SMALL_HALVES)
                if l < layers - 1:
                    sp.wait_ge(S("y_ready"), after("y_ready", l * 16 + NSA_H + GDN_H))
                    sp.dma_start(sm_all[:, :], small[l + 1]).then_inc(S("small_in"), 16)
                load(at["out"], OUT_HALVES)
            for t in (1, 0, 2, 3):
                if t == 0:
                    sp.wait_ge(S("pool_out"), 1)
                else:
                    sp.wait_ge(S("dve_out"), t)
                sp.dma_start(out[0, t * P:(t + 1) * P, :], xres[:, t, :]).then_inc(S("out_in"), 16)
            sp.wait_ge(S("out_in"), TT * 16)

        @block.tensor
        def _(pe):
            mm, tr = pe.matmul, pe.transpose

            def each_tile(dst, lhs, rhs):
                for t in range(TT):
                    at = slice(t * P, (t + 1) * P)
                    last = mm(dst[:, at], lhs[:, at], rhs[:, at], start=True, stop=True)
                return last

            def each_narrow(dst, lhs, rhs):
                for t in range(TT):
                    last = mm(narrow(dst)[:, t, :], lhs[:, t * P:(t + 1) * P], narrow(rhs)[:, t, :],
                              start=True, stop=True)
                return last

            def transposes(dst, src):
                for t in range(TT):
                    at = slice(t * P, (t + 1) * P)
                    last = tr(dst[:, at], src[:, at], ident)
                return last

            def column_tile(tile, split, b, k0, k1):
                for k in range(k0, k1):
                    half, i = divmod(k, KT // 2)
                    if k == 0:
                        pe.wait_ge(S("p_copied"), tile)
                    if i == 0 or k == k0:
                        pe.wait_ge(S("split_ready"), split + half + 1)
                    hi, lo = (w[:, half, i * P:(i + 1) * P] for w in (w_hi, w_lo))
                    mm(PJ[b][:, :], hi, h_hi[:, k, :], start=(k == 0), stop=False)
                    mm(PJ[b][:, :], hi, h_lo[:, k, :], start=False, stop=False)
                    last = mm(PJ[b][:, :], lo, h_hi[:, k, :], start=False, stop=(k == KT - 1))
                    if i == KT // 2 - 1:
                        last.then_inc(S("split_used"), 1)

            def lot_products(l, h, fill, s):
                for i, k0, k1 in parts(fill, s):
                    column_tile(tile_of_lot(l, 1) + h * LOT + (i + 1), split_of_lot(l, 1) + h * (2 * LOT) + 2 * (i + 1),
                                (i + 1) % 2, k0, k1)

            def reduce_mod(sums, n):
                pe.wait_ge(S("mod_sum"), n)
                for k in range(KT):
                    last = mm(MB[:, k:k + 1], sums[:, k * P:(k + 1) * P], ones[:, 0:1], start=True, stop=True)
                last.then_inc(S("mod_done"), 1)

            pe.wait_ge(S("const_in"), 48)
            reduce_mod(acc0[0], 1)
            pe.wait_ge(S("mod_copied"), 1)
            reduce_mod(acc0[1], 2)
            for l in range(layers):
                if l == 0:
                    pe.wait_ge(S("x_in"), 16)
                else:
                    pe.wait_ge(S("norm_act"), 2 * l)
                    pe.wait_ge(S("norm_dve"), 2 * l)
                for k in range(KT + 3):
                    if k < KT:
                        if k >= 4:
                            pe.wait_ge(S(("h_even", "h_odd")[k % 2]), l * (KT // 2) + k // 2 - 1)
                        for t in range(TT):
                            last = tr(XT[k % 4][:, t * P:(t + 1) * P], xres[:, t, k * P:(k + 1) * P], ident)
                        last.then_inc(S("xT_done"), 1)
                    if k >= 3:
                        j = k - 3
                        pe.wait_ge(S("h_ready"), l * KT + j + 1)
                        piece, i = divmod(j, KT // SMALL_HALVES)
                        if i == 0:
                            pe.wait_ge(S("split_ready"), l * SPLITS + piece + 1)
                        hi, lo = (w[:, piece % 2, i * N_SMALL:(i + 1) * N_SMALL] for w in (w_hi, w_lo))
                        o = OB[0:N_SMALL, :]
                        mm(o, hi, h_hi[:, j, :], start=(j == 0), stop=False)
                        mm(o, hi, h_lo[:, j, :], start=False, stop=False)
                        last = mm(o, lo, h_hi[:, j, :], start=False, stop=(j == KT - 1))
                        if i == KT // SMALL_HALVES - 1:
                            last.then_inc(S("split_used"), 1)
                if l == 0:
                    pe.wait_ge(S("mod_copied"), 2)
                pe.wait_ge(S("small_copied"), l + 1)
                for t in range(TT):
                    last = mm(MB[:, t * 32:t * 32 + N_SMALL], A(16, N_SMALL)[:, t * P:(t + 1) * P],
                              ident[0:N_SMALL, 0:N_SMALL], start=True, stop=True)
                last.then_inc(S("smallT_done"), 1)
                pe.wait_ge(S("g_ready"), l + 1)
                g_all = coef[:, 0, :, :].rearrange("p t h -> p (t h)")
                mm(SB_[0][:, 0:24], C("cumul"), g_all, start=True, stop=True)
                mm(SB_[0][:, 24:48], C("chunk"), g_all, start=True, stop=True).then_inc(S("gc_done"), 1)

                with pe.Fori(0, KVH) as g:
                    G = l * KVH + g

                    def load_tile(tile, k0=0, k1=KT):
                        column_tile(l * LAYER_TILES + g * GROUP_TILES + tile,
                                    split_of_group(l, g) + 2 * tile, tile % 2, k0, k1)

                    def copied(tile):
                        pe.wait_ge(S("p_copied"), after("p_copied", l * LAYER_TILES + g * GROUP_TILES + tile + 1))

                    def compress(which):
                        pe.wait_ge(S("blocks_ready"), G * 2 + which + 1)
                        for q4 in range(4):
                            pe.wait_ge(S(f"slot_in{q4}"), (turn_of_group(l, g) + (which + 2)) * 16)
                            for i in range(CMP_LEN // 4):
                                t = q4 * (CMP_LEN // 4) + i
                                last = mm(TB[which][0:N_CMP, 0:HD], blocks_kv[which][:, t * N_CMP:(t + 1) * N_CMP],
                                          ring[:, q4, i * HD:(i + 1) * HD],
                                          start=(t == 0), stop=(t == CMP_LEN - 1))
                            last.then_inc(S(f"raw_free{q4}"), 1)

                    def rotate(j, x):
                        pe.wait_ge(S("rot_used"), after("rot_used", G * 6 + j))
                        mm(MB[0:32, 0:x.shape[1]], C("rot"), x, start=True, stop=True)\
                            .then_inc(S("rot_done"), 1)

                    load_tile(0)
                    load_tile(1)
                    compress(0)
                    compress(1)
                    load_tile(2)
                    pe.wait_ge(S("hid_ready"), G * 2 + 2)
                    for which in range(2):
                        last = mm(SB_[which][:, 0:N_CMP], hidden[:, which, :], ident[0:N_CMP, 0:N_CMP],
                                  start=True, stop=True)
                    last.then_inc(S("hidT_done"), 1)
                    load_tile(3)
                    pe.wait_ge(S("hidT_ready"), G + 1)
                    mm(SB_[0][:, 0:N_CMP], w2[:, 0, :], cmpb[:, 2, 0:N_CMP], start=True, stop=True)
                    mm(SB_[1][0:N_CMP, 0:HD], cmpb[:, 3, 0:N_CMP], w2[:, 1, :],
                       start=True, stop=True).then_inc(S("cmp_done"), 1)
                    load_tile(4)
                    pe.wait_ge(S("cmp_copied"), G + 1)
                    rotate(0, cmpb[:, 0, 0:N_CMP])
                    rotate(1, kS)
                    copied(3)
                    transposes(TB[0], v_raw[0]).then_inc(S("vT_done"), 1)
                    load_tile(5)
                    copied(4)
                    rotate(2, kW)
                    load_tile(6)
                    copied(5)
                    transposes(TB[1], v_raw[1]).then_inc(S("vT_done"), 1)
                    load_tile(7)
                    copied(6)
                    rotate(3, qT[0])
                    for r in range(GROUP):
                        H = G * GROUP + r
                        q = qT[r % 2]
                        for s in range(NSA_STEPS):
                            for i, k0, k1 in parts(nsa_fill, s):
                                load_tile(8 + 2 * r + i, k0, k1)
                            if r < GROUP - 1:
                                if s == 8:
                                    copied(8 + 2 * r)
                                    rotate(4 + r, qT[(r + 1) % 2])
                            if s == 0:
                                pe.wait_ge(S("roped"), G * 6 + 4 + r)
                                pe.wait_ge(S("exp_done"), after("exp_done", H * 8))
                                for i in range(TT):
                                    last = mm(SB_[0][:, i * 32:i * 32 + N_CMP], q[:, i * P:(i + 1) * P],
                                              cmpb[:, 0, 0:N_CMP], start=True, stop=True)
                                last.then_inc(S("cmp_scores"), 1)
                            if 1 <= s <= 8:
                                u = s - 1
                                i, keys, w = u % TT, (kS, kW)[u // TT], (u % TT + 1) * P
                                if u == 1:
                                    pe.wait_ge(S("cmp_scored"), H + 1)
                                pe.wait_ge(S("exp_done"), after("exp_done", H * 8 + max(u - 1, 0)))
                                mm(SB_[(u + 1) % 2][:, 0:w], q[:, w - P:w], keys[:, 0:w], start=True, stop=False)
                                mm(SB_[(u + 1) % 2][:, w - P:w], ident_r[:, :], causal_r[:, :],
                                   start=False, stop=True).then_inc(S("scores"), 1)
                            if s == 1:
                                pe.wait_ge(S("cmp_probs"), H + 1)
                                pe.wait_ge(S("pt_ready"), after("pt_ready", H * 8))
                                pe.wait_ge(S("v_ready"), G * 2 + 2)
                                for i in range(TT):
                                    last = tr(TB[0][0:N_CMP, i * P:(i + 1) * P], cmp_p[:, i, :], ident)
                                last.then_inc(S("cmp_pT"), 1)
                            if s == 2:
                                pe.wait_ge(S("cmp_pT_ready"), H + 1)
                                pe.wait_ge(S("y_ready"), after("y_ready", l * 16 + g * GROUP + r))
                                mm(OB[:, :], vcmp[0:N_CMP, :], cmp_pT, start=True, stop=False,
                                   skip_group_check=True)
                            if 2 <= s <= 9:
                                u = s - 2
                                pe.wait_ge(S("pt_ready"), after("pt_ready", H * 8 + max(u - 1, 0)))
                                pe.wait_ge(S("probs"), H * 8 + u + 1)
                                for j in range(u % TT + 1):
                                    last = tr(TB[(u + 1) % 2][:, j * P:(j + 1) * P],
                                              prob[u % 2][:, j * P:(j + 1) * P], ident)
                                last.then_inc(S("pt_done"), 1)
                            if 3 <= s <= 10:
                                u = s - 3
                                i, vals = u % TT, (vS, vW)[u // TT]
                                pe.wait_ge(S("pt_ready"), after("pt_ready", H * 8 + u + 1))
                                for j in range(i + 1):
                                    last = mm(OB[:, i * P:(i + 1) * P], vals[:, j * P:(j + 1) * P],
                                              probT[u % 2][:, j * P:(j + 1) * P], start=False,
                                              stop=(j == i), skip_group_check=True)
                                last.then_inc(S("pv_done"), 1)
                    if l < DEPTH - 1:
                        reduce_mod(acc, g + (sums_before[l] + 1))

                def front(h, part):
                    F = l * GDN_H + h
                    if part == 2:
                        pe.wait_ge(S("gdn_sq"), F * 2 + 1)
                        mm(MB[:, :], ones, A(2), start=True, stop=True).then_inc(S("gdn_norm"), 1)
                    if part == 5:
                        pe.wait_ge(S("gdn_sq"), F * 2 + 2)
                        pe.wait_ge(S("gdn_rsqrt"), F * 2 + 1)
                        mm(MB[:, :], ones, A(3), start=True, stop=True).then_inc(S("gdn_norm"), 1)
                    if part == 7:
                        pe.wait_ge(S("gdn_gsel"), F + 1)
                        pe.wait_ge(S("gdn_rsqrt"), F * 2 + 2)
                        mm(MB[:, :], ones, A(12), start=True, stop=True).then_inc(S("gdn_gcb"), 1)

                def delta(h, pipelined):
                    D = l * GDN_H + h

                    def ready(name):
                        pe.wait_ge(S(name), D + 1)

                    for s in range(GDN_STEPS):
                        lot_products(l, h, gdn_fill, s)
                        if s == 0:
                            ready("gdn_k")
                            pe.wait_ge(S("rec_state"), after("rec_state", D * 9))
                            each_tile(TB[1], A(0), A(0)).then_inc(S("gdn_kk"), 1)
                            ready("gdn_q")
                            each_tile(SB_[0], A(7), A(0)).then_inc(S("gdn_qk"), 1)
                            transposes(TB[0], A(0)).then_inc(S("gdn_kT"), 1)
                        if s == 1:
                            ready("gdn_egb")
                            ready("gdn_lower")
                            transposes(MB, A(3)).then_inc(S("gdn_lT"), 1)
                        if s == 2:
                            ready("gdn_lT_copied")
                            ready("gdn_intra")
                            transposes(MB, A(17)).then_inc(S("gdn_iT"), 1)
                        for v in range(len(LEVELS)):
                            if s == 3 + 2 * v:
                                pe.wait_ge(S("gdn_ct"), D * 5 + v + 1)
                                pe.wait_ge(S("gdn_T"), D * 5 + v + 1)
                                each_narrow(TB[1], A(15 - v % 2), A(11)).then_inc(S("gdn_CT"), 1)
                            if s == 4 + 2 * v:
                                if v == 0:
                                    pe.wait_ge(S("y_ready"), after("y_ready", l * 16 + NSA_H + h))
                                if v < len(LEVELS) - 1:
                                    pe.wait_ge(S("gdn_lv_n"), D * 4 + v + 1)
                                    each_narrow(SB_[0], A(13), lv_buf).then_inc(S("gdn_TCTn"), 1)
                                pe.wait_ge(S("gdn_lv_y"), after("gdn_lv_y", D * 5 + v + 1))
                                each_tile(SB_[1], A(17), A(13)).then_inc(S("gdn_TCT"), 1)
                                if v == 1:
                                    ready("gdn_v")
                                    transposes(OB, A(10)).then_inc(S("gdn_vT"), 1)
                        if s == REC - 1:
                            pe.wait_ge(S("gdn_T"), D * 5 + 5)
                            ready("gdn_Tt")
                            each_tile(TB[0], A(1), A(13)).then_inc(S("gdn_w"), 1)
                        if REC <= s < GDN_STEPS - 1:
                            i, second = (s - REC) // 2, (s - REC) % 2
                            t, half = i // 2, i % 2
                            at = slice(i * CHUNK, (i + 1) * CHUNK)
                            rows = slice(half * CHUNK, (half + 1) * CHUNK)
                            if not second:
                                if i == 0:
                                    ready("gdn_w_copied")
                                    ready("gdn_qh")
                                    ready("gdn_i_copied")
                                pe.wait_ge(S("rec_state"), after("rec_state", D * 9 + i + 1))
                                mm(SB_[half][rows, 0:HD], A(13)[:, at], A(8)[:, t * P:(t + 1) * P],
                                   start=True, stop=False)
                                mm(SB_[half][rows, 0:HD], A(18)[:, at], state[:, :],
                                   start=False, stop=True).then_inc(S("rec_v"), 1)
                                mm(OB[:, at], state[:, :], A(6)[:, at], start=True, stop=False)
                                if pipelined:
                                    front(h + 1, i)
                            else:
                                pe.wait_ge(S("rec_vn"), after("rec_vn", D * 8 + i + 1))
                                mm(TB[half][:, 0:HD], A(9)[:, t * P:(t + 1) * P], vnew[:, half, :],
                                   start=True, stop=True).then_inc(S("rec_kv"), 1)
                                last = mm(OB[:, at], vnew[:, half, :], A(16)[:, at], start=False, stop=True)
                                if i == SEQ // CHUNK - 1:
                                    last.then_inc(S("gdn_o"), 1)
                        if s == GDN_STEPS - 1:
                            ready("gdn_osq")
                            mm(SB_[1][:, :], ones, A(14), start=True, stop=True).then_inc(S("gdn_no"), 1)

                pe.wait_ge(S("y_ready"), after("y_ready", l * 16 + NSA_H))
                if l < DEPTH - 1:
                    pe.wait_ge(S("mod_copied"), 2 * l + 4)
                for part, k in ((2, 0), (5, 6), (7, 12)):
                    column_tile(tile_of_lot(l, 1), split_of_lot(l, 1), 0, k, min(k + 6, KT))
                    front(0, part)
                with pe.Fori(0, GDN_H - 1) as h:
                    delta(h, True)
                delta(GDN_H - 1, False)

                def stick(h, fill):
                    B = l * SB_H + h
                    for s in range(SB_STEPS):
                        if fill is sb_3_fill:
                            for i, k0, k1 in parts(fill, s):
                                column_tile(tile_of_lot(l, N_LOTS) - 1, split_of_lot(l, N_LOTS) - 2, 1, k0, k1)
                        else:
                            lot_products(l, h + GDN_H, fill, s)
                        if s == 0:
                            pe.wait_ge(S("y_ready"), after("y_ready", l * 16 + NSA_H + GDN_H + h))
                            pe.wait_ge(S("p_copied"), after("p_copied", tile_of_lot(l, GDN_H + h) + 3))
                            transposes(MB, raw[:, 2, TAPS - 1:]).then_inc(S("sb_vT"), 1)
                            pe.wait_ge(S("sb_qk"), B + 1)
                        if s < TT:
                            j = TT - 1 - s
                            w = SEQ - j * P
                            pe.wait_ge(S("lb_ready"), after("lb_ready", B * TT + max(s - 1, 0)))
                            mm(SB_[s % 2][:, 0:w], A(0)[:, j * P:(j + 1) * P], A(1)[:, j * P:],
                               start=True, stop=True).then_inc(S("sb_z"), 1)
                        if 1 <= s <= TT:
                            j = TT - s
                            w = SEQ - j * P
                            pe.wait_ge(S("spm_ready"), B * TT + s)
                            b = TB[(s - 1) % 2]
                            mm(b[:, 0:w], C("after"), A(9 + j)[:, 0:w], start=True, stop=(s == 1))
                            for m in range(j + 1, TT):
                                last = mm(b[:, (m - j) * P:w], ones, A(9 + m)[:, 0:SEQ - m * P],
                                          start=False, stop=(m == TT - 1))
                            if s == 1:
                                last = None
                            if last is None:
                                pe.drain().then_inc(S("sb_acc"), 1)
                            else:
                                last.then_inc(S("sb_acc"), 1)
                        if 2 <= s <= TT + 1:
                            j = TT + 1 - s
                            pe.wait_ge(S("sb_a"), B * TT + s - 1)
                            if s == 2:
                                pe.wait_ge(S("sb_v"), B + 1)
                            last = mm(OB[:, j * P:], A(2)[:, j * P:(j + 1) * P], A(15 + s % 2)[:, 0:SEQ - j * P],
                                      start=(s == 2), stop=(s == TT + 1), skip_group_check=True)
                            last.then_inc(S("sb_pv"), 1)

                with pe.Fori(0, SB_H - 2) as h:
                    stick(h, sb_fill)
                stick(SB_H - 2, sb_2_fill)
                stick(SB_H - 1, sb_3_fill)

                def gate(first, end):
                    for n in range(first, end):
                        last = mm(ODD[n][:, :], ones, acc[:, n * SEQ:(n + 1) * SEQ], start=True, stop=True)
                    last.then_inc(S("gate_done"), 1)

                pe.wait_ge(S("mod_sum"), sums_before[l] + (3 if l < DEPTH - 1 else 1))
                gate(0, 2)
                for n in range(TT):
                    outs = (bank[2:6], ODD)[n % 2]
                    for k2 in range(KT // 2):
                        if n == 0 and k2 == 3:
                            pe.wait_ge(S("y_ready"), after("y_ready", l * 16 + 16))
                            gate(2, 4)
                        if n == 1 and k2 == 0:
                            pe.wait_ge(S("gate_ready"), l + 1)
                        pe.wait_ge(S("split_ready"), split_of_lot(l, N_LOTS) + n * (KT // 2) + k2 + 1)
                        if n == 0:
                            pe.wait_ge(S("y_split"), l * 16 + 2 * k2 + 2)
                        for t in range(TT):
                            if k2 == 0:
                                pe.wait_ge(S("o_used"), l * 16 + n * TT + t + 1)
                            at = slice(t * P, (t + 1) * P)
                            for i in range(2):
                                k = k2 * 2 + i
                                hi, lo = (w[:, k2 % 2, i * SEQ:(i + 1) * SEQ] for w in (w_hi, w_lo))
                                mm(outs[t][:, :], h_hi[:, k, at], hi, start=(k == 0), stop=False)
                                mm(outs[t][:, :], h_hi[:, k, at], lo, start=False, stop=False)
                                last = mm(outs[t][:, :], h_lo[:, k, at], hi, start=False, stop=(k == KT - 1))
                            if k2 == KT // 2 - 1 and t < TT - 1:
                                last.then_inc(S("o_done"), 1)
                        last.then_inc(S("split_used"), 1)

        @block.scalar
        def _(act):
            def fn(*args, **kw):
                made = act.activation(*args, **kw)
                act.drain()
                return made

            def copy_tile(split, dst, b):
                act.wait_ge(S("split_used"), after("split_used", split))
                fn(dst, PJ[b][:, :], ACT.Copy).then_inc(S("p_copied"), 1)

            def copy_lot(l, n, i):
                act.wait_ge(S(f"raw_used{i}"), after(f"raw_used{i}", l * N_LOTS + n))
                copy_tile(split_of_lot(l, n) + 2 * i + 2, raw[:, i, TAPS - 1:], i % 2)

            def copy_ended(l, h, fill, s):
                for i in ended(fill, s):
                    copy_lot(l, h + (1 if i < LOT - 1 else 2), (i + 1) % LOT)

            def start_sums(n, dst, l, part):
                act.wait_ge(S("acc_zero"), n)
                src = b_mod[l:l + 1, part * DM:(part + 1) * DM] if isinstance(part, int) else \
                    b_mod[l:l + 1, bass.ds(part * DM, DM)]
                act.dma_start(dst, src).then_inc(S("bmod_in"), 16)

            act.wait_ge(S("const_in"), 48)
            fn(cact[:, 0, :], cact[:, 1, :], ACT.Tanh, scale=0.5).then_inc(S("c_tanh"), 1)
            for part in range(2):
                start_sums(2, acc0[part][0:1, :], 0, part)
            act.wait_ge(S("angles"), 1)
            fn(rope_cs[:, :, :], arena[0:32, 14:16, :], ACT.Sin).then_inc(S("rope_ready"), 1)
            for l in range(layers):
                for k in range(KT):
                    if k % 2 == 0 or k == 1:
                        act.wait_ge(S("h_even"), l * (KT // 2) + k // 2 + 1)
                    if k % 2:
                        act.wait_ge(S("xT_done"), l * KT + k + 1)
                        if k >= 4:
                            act.wait_ge(S("h_ready"), l * KT + k - 3)
                        fn(A(16 + k % 4), XT[k % 4][:, :], ACT.Identity, scale=h_mod[:, 0, k:k + 1],
                           bias=h_mod[:, 1, k:k + 1]).then_inc(S("h_odd"), 1)
                    if l and k == 0:
                        act.wait_ge(S("split_used"), after("split_used", l * SPLITS))
                    fn(h_hi[:, k, :], A(16 + k % 4), ACT.Copy).then_inc(S("h_hi_ready"), 1)
                act.wait_ge(S("split_used"), after("split_used", l * SPLITS + SMALL_HALVES))
                act.wait_ge(S("h_ready"), l * KT + KT)
                fn(A(16, N_SMALL), OB[0:N_SMALL, :], ACT.Copy).then_inc(S("small_copied"), 1)
                act.wait_ge(S("smallT_done"), l + 1)
                small = MB[:, 0:TT * 32].rearrange("p (t n) -> p t n", t=TT)
                th = A(17)[:, 0:TT * 24].rearrange("p (t n) -> p t n", t=TT)
                fn(th, small[:, :, 0:24], ACT.Tanh, scale=0.5).then_inc(S("gates_tanh"), 1)
                act.wait_ge(S("ga_ready"), l + 1)
                fn(A(18)[:, 32:56], A(18)[:, 0:24], ACT.Abs)
                fn(ea[:, :], small_part("a_log"), ACT.Exp)
                fn(A(18)[:, 64:88], A(18)[:, 32:56], ACT.Exp, scale=-1.0)
                fn(A(18)[:, 96:120], A(18)[:, 64:88], ACT.Ln, bias=1.0).then_inc(S("ga_ln"), 1)
                act.wait_ge(S("gc_ready"), l + 1)
                fn(A(18)[:, 128:152], coef[:, 3, :, :].rearrange("p t h -> p (t h)"), ACT.Exp)
                fn(coef[:, 5, :, :].rearrange("p t h -> p (t h)"), A(18)[:, 160:184], ACT.Exp)\
                    .then_inc(S("gc_exp"), 1)
                act.wait_ge(S("coef_ready"), l + 1)
                if l:
                    act.wait_ge(S("x_stored"), l * TT * 16)
                if l >= 2:
                    act.wait_ge(S("lnb_used"), (l - 1) * TT)

                with act.Fori(0, KVH) as g:
                    G = l * KVH + g
                    if l < DEPTH - 1:
                        start_sums(g + (sums_before[l] + 1), acc[0:1, :], l + 1, g)

                    def copy_group(tile, dst):
                        copy_tile(split_of_group(l, g) + (2 * tile + 2), dst, tile % 2)

                    def copy_z(tile, H):
                        act.wait_ge(S("split_used"), after("split_used", split_of_group(l, g) + (2 * tile + 2)))
                        act.wait_ge(S("sz_ready"), after("sz_ready", H))
                        fn(z_raw, PJ[1][:, :], ACT.Copy)
                        fn(z_tanh, PJ[1][:, :], ACT.Tanh, scale=0.5)
                        act.drain().then_inc(S("p_copied"), 1)
                        act.sem_inc(S("z_tanh"), 1)

                    copy_group(0, v_raw[0])
                    copy_group(1, v_raw[1])
                    for which in range(2):
                        act.wait_ge(S("raw_free3"), after("raw_free3", turn_of_group(l, g) + (which + 2)))
                        fn(hid_tanh[:, which, :], TB[which][0:N_CMP, 0:HD], ACT.Tanh, scale=0.5)\
                            .then_inc(S("cmp_tanh"), 1)
                    copy_group(2, kS)
                    copy_group(3, v_raw[0])
                    act.wait_ge(S("cmp_done"), G + 1)
                    fn(cmpb[:, 0, 0:N_CMP], SB_[0][:, 0:N_CMP], ACT.Copy)
                    fn(vcmp[0:N_CMP, :], SB_[1][0:N_CMP, 0:HD], ACT.Copy)
                    act.drain().then_inc(S("cmp_copied"), 1)
                    copy_group(4, kW)
                    act.wait_ge(S("vT_done"), G * 2 + 1)
                    fn(vS, TB[0][:, :], ACT.Copy).then_inc(S("v_ready"), 1)
                    copy_group(5, v_raw[1])
                    copy_group(6, qT[0])
                    act.wait_ge(S("vT_done"), G * 2 + 2)
                    fn(vW, TB[1][:, :], ACT.Copy).then_inc(S("v_ready"), 1)
                    copy_z(7, G * GROUP)
                    for r in range(GROUP):
                        H = G * GROUP + r
                        for s in range(NSA_STEPS):
                            for i in ended(nsa_fill, s):
                                if r == GROUP - 1:
                                    copy_tile(split_of_group(l, g) + (26 + 2 * i), raw[
                                        :, bass.ds(g * 2 + i, 1), TAPS - 1:].rearrange("p a n -> p (a n)"), i)
                                else:
                                    if i == 0:
                                        copy_group(8 + 2 * r, qT[(r + 1) % 2])
                                    else:
                                        copy_z(9 + 2 * r, H + 1)
                            if s == 0:
                                act.wait_ge(S("cmp_scored2"), H + 1)
                                fn(cmp_s, cmp_s, ACT.Exp).then_inc(S("cmp_exp"), 1)
                            if 1 <= s <= 8:
                                u = s - 1
                                w = (u % TT + 1) * P
                                act.wait_ge(S("max_ready"), H * 8 + u + 1)
                                fn(prob[u % 2][:, 0:w], SB_[(u + 1) % 2][:, 0:w], ACT.Exp, scale=SCALE,
                                   bias=tiny[:, u:u + 1], accum_out=tiny[:, 8 + u:9 + u]).then_inc(S("exp_done"), 1)
                            if 2 <= s <= 9:
                                u = s - 2
                                w = (u % TT + 1) * P
                                act.wait_ge(S("pt_done"), H * 8 + u + 1)
                                act.wait_ge(S("pv_done"), after("pv_done", H * 8 + max(u - 1, 0)))
                                fn(probT[u % 2][:, 0:w], TB[(u + 1) % 2][:, 0:w], ACT.Copy)\
                                    .then_inc(S("pt_ready"), 1)

                start_sums(sums_before[l] + (3 if l < DEPTH - 1 else 1), acc[0:1, :], l, 2)

                def front(h, part):
                    F = l * GDN_H + h
                    if part == -1:
                        act.wait_ge(S("gdn_conv"), F * 3 + 1)
                        fn(A(2), A(0), ACT.Tanh, scale=0.5).then_inc(S("gdn_tanh"), 1)
                    if part == 1:
                        act.wait_ge(S("gdn_silu"), F * 2 + 1)
                        fn(A(2), A(0), ACT.Square).then_inc(S("gdn_sq"), 1)
                    if part == 2:
                        act.wait_ge(S("gdn_conv"), F * 3 + 2)
                        fn(A(3), A(7), ACT.Tanh, scale=0.5).then_inc(S("gdn_tanh"), 1)
                    if part == 3:
                        act.wait_ge(S("gdn_silu"), F * 2 + 2)
                        fn(A(3), A(7), ACT.Square).then_inc(S("gdn_sq"), 1)
                        act.wait_ge(S("gdn_norm"), F * 2 + 1)
                        fn(A(2), MB[:, :], ACT.Ln, scale=0.25, bias=tiny[:, 32:33])
                        fn(A(2), A(2), ACT.Exp, scale=-0.5, bias=tiny[:, 34:35]).then_inc(S("gdn_rsqrt"), 1)
                    if part == 5:
                        act.wait_ge(S("gdn_norm"), F * 2 + 2)
                        fn(A(3), MB[:, :], ACT.Ln, scale=0.25, bias=tiny[:, 32:33])
                        fn(A(3), A(3), ACT.Exp, scale=-0.5, bias=tiny[:, 35:36]).then_inc(S("gdn_rsqrt"), 1)
                    if part == 8:
                        act.wait_ge(S("gdn_d"), F + 1)
                        fn(A(5), A(5), ACT.Exp, scale=-1.0).then_inc(S("gdn_decay"), 1)

                def delta(h, pipelined):
                    D = l * GDN_H + h

                    def ready(name):
                        act.wait_ge(S(name), D + 1)

                    for s in range(GDN_STEPS):
                        if s < GDN_STEPS - 1:
                            copy_ended(l, h, gdn_fill, s)
                        if s == 0:
                            ready("gdn_gcb")
                            act.wait_ge(S("rec_state"), after("rec_state", D * 9))
                            fn(A(4), MB[:, :], ACT.Exp).then_inc(S("gdn_egb"), 1)
                        if s == 1:
                            ready("gdn_lT")
                            fn(A(12), MB[:, :], ACT.Copy).then_inc(S("gdn_lT_copied"), 1)
                        if s == 2:
                            ready("gdn_iT")
                            fn(A(16), MB[:, :], ACT.Copy).then_inc(S("gdn_i_copied"), 1)
                            act.wait_ge(S("gdn_conv"), D * 3 + 3)
                            fn(A(5), A(10), ACT.Tanh, scale=0.5).then_inc(S("gdn_vtanh"), 1)
                            fn(A(18), raw[:, 3, TAPS - 1:], ACT.Tanh, scale=0.5).then_inc(S("gdn_ztanh"), 1)
                        for v in range(len(LEVELS)):
                            if s == 3 + 2 * v:
                                act.wait_ge(S("gdn_CT"), D * 5 + v + 1)
                                if v < len(LEVELS) - 1:
                                    fn(lv_n, narrow(TB[1]), ACT.Copy).then_inc(S("gdn_lv_n"), 1)
                                for half in range(2):
                                    rows = slice(half * CHUNK, (half + 1) * CHUNK)
                                    act.activation(own(A(17), half), narrow(TB[1])[rows], ACT.Copy)
                                act.drain().then_inc(S("gdn_lv_y"), 1)
                                if v == len(LEVELS) - 1 and pipelined:
                                    front(h + 1, -1)
                        if s == REC - 1:
                            ready("gdn_w")
                            fn(A(18), TB[0][:, :], ACT.Copy, scale=-1.0).then_inc(S("gdn_w_copied"), 1)
                        if REC <= s < GDN_STEPS - 1 and (s - REC) % 2 == 0:
                            i = (s - REC) // 2
                            rows = slice(i % 2 * CHUNK, (i % 2 + 1) * CHUNK)
                            act.wait_ge(S("rec_v"), D * 8 + i + 1)
                            fn(vnew[rows, i % 2, :], SB_[i % 2][rows, 0:HD], ACT.Copy).then_inc(S("rec_vn"), 1)
                            if pipelined:
                                front(h + 1, i)
                        if s == GDN_STEPS - 1:
                            ready("gdn_o")
                            fn(A(14), OB[:, :], ACT.Square).then_inc(S("gdn_osq"), 1)
                            if pipelined:
                                front(h + 1, 8)
                            ready("gdn_no")
                            fn(A(15), SB_[1][:, :], ACT.Ln, scale=1.0 / HD, bias=tiny[:, 32:33])
                            fn(A(15), A(15), ACT.Exp, scale=-0.5, bias=tiny[:, 34:35]).then_inc(S("gdn_ro"), 1)
                            copy_ended(l, h, gdn_fill, s)

                for part in range(-1, 9):
                    front(0, part)
                copy_lot(l, 1, 0)
                with act.Fori(0, GDN_H - 1) as h:
                    delta(h, True)
                delta(GDN_H - 1, False)

                def stick(h, fill):
                    B = l * SB_H + h
                    last = fill is sb_3_fill
                    for s in range(SB_STEPS):
                        if not last:
                            copy_ended(l, h + GDN_H, fill, s)
                        elif ended(fill, s):
                            copy_lot(l, N_LOTS - 1, LOT - 1)
                        if s == 0:
                            act.wait_ge(S("y_ready"), after("y_ready", l * 16 + NSA_H + GDN_H + h))
                        if s == (3 if last else 0):
                            fn(A(4), raw[:, 3, TAPS - 1:], ACT.Tanh, scale=0.5).then_inc(S("sb_ztanh"), 1)
                        if s < TT:
                            w = (s + 1) * P
                            act.wait_ge(S("sb_z"), B * TT + s + 1)
                            e = A(5 + s % 2)[:, 0:w]
                            fn(e, SB_[s % 2][:, 0:w], ACT.Abs)
                            fn(e, e, ACT.Exp, scale=-1.0)
                            fn(e, e, ACT.Ln, bias=1.0).then_inc(S("sb_ln"), 1)
                        if 1 <= s <= TT:
                            w = s * P
                            act.wait_ge(S("sb_arg"), B * TT + s)
                            act.wait_ge(S("sb_pv"), after("sb_pv", B * TT + max(s - 2, 0)))
                            fn(A(16 - s % 2)[:, 0:w], A(13 + (s - 1) % 2)[:, 0:w], ACT.Exp).then_inc(S("sb_exp"), 1)
                        if last and s >= 3:
                            for k in range((s - 3) * 5, (s - 2) * 5):
                                fn(h_hi[:, k, :], yT[:, k, :], ACT.Copy).then_inc(S("y_hi"), 1)

                with act.Fori(0, SB_H - 2) as h:
                    stick(h, sb_fill)
                stick(SB_H - 2, sb_2_fill)
                stick(SB_H - 1, sb_3_fill)
                act.wait_ge(S("y_ready"), after("y_ready", l * 16 + MIX_T))
                fn(h_hi[:, MIX_T - 1, :], yT[:, MIX_T - 1, :], ACT.Copy).then_inc(S("y_hi"), 1)
                act.wait_ge(S("y_split"), l * 16 + MIX_T)
                for n in range(TT):
                    at = slice(n * SEQ, (n + 1) * SEQ)
                    src = x_norm.rearrange("t p n -> p t n") if l else x[0].rearrange("(t p) n -> p t n", p=P)
                    act.dma_start(xres[:, :, at], src[:, :, at]).then_inc(S(f"xo_in{n}"), 16)
                    if l:
                        if n >= 2:
                            act.wait_ge(S("lnb_used"), (l - 1) * TT + n - 1)
                        for a in range(2):
                            act.dma_start(raw[:, n % 2 * 2 + a, TAPS - 1:],
                                          lns[l - 1:l, a * DM + n * SEQ:a * DM + (n + 1) * SEQ].broadcast_to((P, SEQ)))\
                                .then_inc(S(f"xo_in{n}"), 16)
                if l == layers - 1:
                    act.dma_start(ln_gb.rearrange("p a n -> p (a n)"), lns[l:l + 1, :].broadcast_to((P, 2 * DM)))\
                        .then_inc(S("ln_in"), 16)
                act.wait_ge(S("var_ready"), l + 1)
                fn(tiny[:, 16:20], meanvar[:, :, 1], ACT.Ln, bias=tiny[:, 33:34])
                fn(tiny[:, 20:24], tiny[:, 16:20], ACT.Exp, scale=-0.5).then_inc(S("rstd_ready"), 1)
                act.wait_ge(S("nmr_ready"), l + 1)
                for t in range(2 if l < layers - 1 else 1):
                    fn(xres[:, t, :], xres[:, t, :], ACT.Identity, scale=tiny[:, 20 + t:21 + t],
                       bias=tiny[:, 36 + t:37 + t]).then_inc(S("norm_act"), 1)
                if l < layers - 1:
                    for t in range(TT):
                        if t < 2:
                            act.wait_ge(S("norm_act"), 2 * l + t + 1)
                        else:
                            act.wait_ge(S("norm_dve"), 2 * l + t - 1)
                        act.dma_start(x_norm[t], xres[:, t, :]).then_inc(S("x_stored"), 16)

        @block.gpsimd
        def _(pool):
            for name, n in CREDITS.items():
                pool.sem_inc(S(name), n)
            pool.memset(raw[:, :, 0:TAPS - 1], 0.0)
            pool.memset(vnew[:, :, :], 0.0)
            for i, v in enumerate((RMS_EPS, LN_EPS, float(np.log(0.5)), float(np.log(0.5 * SCALE)))):
                pool.memset(tiny[:, 32 + i:33 + i], v)
            pool.drain().then_inc(S("pool_ready"), 1)
            pool.wait_ge(S("const_in"), 48)
            two_pi = 2 * np.pi
            c1 = 6.28125
            c2 = float(np.float32(two_pi - c1))
            c3 = float(two_pi - c1 - c2)
            pos, angle, n, part = (raw[0:32, i, TAPS - 1:] for i in range(LOT))
            M, Ad = ALU.mult, ALU.add

            def ts(*args):
                pool.tensor_scalar(*args)
                pool.drain()

            pool.tensor_copy(n, pos.bitcast(I32))
            pool.drain()
            ts(angle, n, C("misc", 32)[:, 0:1], None, M)
            for i, phase in enumerate((np.pi / 2, 0.0)):
                r = A(14 + i, 32)
                ts(n, angle, float(1 / two_pi), float(phase / two_pi), M, Ad)
                ts(n, n, 12582912.0, None, Ad)
                ts(n, n, 12582912.0, None, ALU.subtract)
                for step, c_ in enumerate((c1, c2, c3)):
                    ts(part, n, -c_, None, M)
                    pool.tensor_tensor(r, part, angle if step == 0 else r, Ad)
                    pool.drain()
                ts(r, r, float(phase), None, Ad)
                ts(r, r, 3.1415925, -3.1415925, ALU.min, ALU.max)
            pool.sem_inc(S("angles"), 1)
            one = ones[:, 0:1]

            def split(slot, turn, n, par, w=HALF):
                pool.wait_ge(S(f"slot_in{slot}"), turn * 16 + 16)
                pool.wait_ge(S("split_used"), n + 1)
                pool.tensor_tensor(w_hi[:, par, 0:w], ring[:, slot, 0:w], one.broadcast_to((P, w)), ALU.mult)
                pool.drain()
                pool.tensor_tensor(w_lo[:, par, 0:w], ring[:, slot, 0:w], w_hi[:, par, 0:w].bitcast(F32), ALU.subtract)
                pool.drain().then_inc(S("split_ready"), 1)
                pool.sem_inc(S(f"raw_free{slot}"), 1)

            def split_items(items, l, kind, n, more=0):
                done = 0
                for p, item in enumerate(items):
                    if item[0] == "C":
                        slot, turn = place(l, kind, p, more)
                        split(slot, turn, n + done, done % 2)
                        done += 1

            for l in range(layers):
                for i in range(SMALL_HALVES):
                    split(i, HALVES_AT[l] // NS, l * SPLITS + i, i % 2, 4 * N_SMALL)
                with pool.Fori(0, KVH) as g:
                    split_items(group_items(l < DEPTH - 1), l, "group", split_of_group(l, g),
                                g * (LAYOUTS[l]["group_len"] // NS))
                n1 = split_of_lot(l, 1)
                split_items(FIRST_TILE, l, "first", n1)
                with pool.Fori(0, GDN_H) as h:
                    split_items(GDN_ITEMS, l, "gdn", h * (2 * LOT) + (n1 + 2), h * (len(GDN_ITEMS) // NS))
                with pool.Fori(0, SB_H - 2) as h:
                    split_items(SB_ITEMS, l, "sb", h * (2 * LOT) + (n1 + 2 + GDN_H * 2 * LOT), h * (len(SB_ITEMS) // NS))
                split_items(SB_2_ITEMS, l, "sb_2", n1 + 2 + (N_LOTS - 2) * 2 * LOT)
                split_items(SB_3_ITEMS, l, "sb_3", n1 + 6 + (N_LOTS - 2) * 2 * LOT)
                with pool.Fori(0, TT) as n:
                    for k2 in range(KT // 2):
                        split(k2 % NS, n * (KT // 2 // NS) + (turn_of_out[l] + k2 // NS),
                              n * (KT // 2) + (split_of_lot(l, N_LOTS) + k2), k2 % 2)
            pool.wait_ge(S("norm_act"), 2 * (layers - 1) + 1)
            pool.wait_ge(S("ln_in"), 16)
            pool.tensor_tensor(xres[:, 0, :], xres[:, 0, :], ln_gb[:, 0, :], ALU.mult)
            pool.drain()
            pool.tensor_tensor(xres[:, 0, :], xres[:, 0, :], ln_gb[:, 1, :], ALU.add).then_inc(S("pool_out"), 1)

        @block.vector
        def _(dve):
            def drained(op):
                def run(*args, **kw):
                    made = op(*args, **kw)
                    dve.drain()
                    return made
                return run

            tt, ts, stt, cp, reduce, reciprocal, bn_stats, bn_aggr, fill = map(drained, (
                dve.tensor_tensor, dve.tensor_scalar, dve.scalar_tensor_tensor, dve.tensor_copy,
                dve.tensor_reduce, dve.reciprocal, dve.bn_stats, dve.bn_aggr, dve.memset))
            M, Ad, Su, Mx = ALU.mult, ALU.add, ALU.subtract, ALU.max
            sync = dve.drain

            for sums in acc0:
                fill(sums, 0.0).then_inc(S("acc_zero"), 1)
            dve.wait_ge(S("const_in"), 48)
            dve.wait_ge(S("pool_ready"), 1)
            cp(ident_r[:, :], ident)
            cp(causal_r[:, :], C("causal"))
            dve.wait_ge(S("c_tanh"), 1)
            stt(cact[:, 1, :], cact[:, 0, :], 1.0, cact[:, 1, :], Ad, M)
            ts(cact[:, 1, :], cact[:, 1, :], 0.5, None, M)

            def rope(j_count, x32, n, at):
                dve.wait_ge(S("rot_done"), j_count + 1)
                tt(rope_a[:, 0:n], MB[0:32, 0:n], rope_cs[:, 1, at], M).then_inc(S("rot_used"), 1)
                tt(rope_b[:, 0:n], x32, rope_cs[:, 0, at], M)
                tt(x32, rope_a[:, 0:n], rope_b[:, 0:n], Ad).then_inc(S("roped"), 1)

            for part in range(2):
                dve.wait_ge(S("bmod_in"), 32)
                with dve.Fori(0, KT // NS) as k4:
                    for i in range(NS):
                        dve.wait_ge(S(f"mod_in{i}"), (k4 + (part * (KT // NS) + 1)) * 16)
                        stt(acc0[part], mod_ring[:, i, :], cact[:, 1, bass.ds(k4 * NS + i, 1)], acc0[part], M, Ad)\
                            .then_inc(S("mod_used"), 1)
                sync().then_inc(S("mod_sum"), 1)
            for part in range(2):
                dve.wait_ge(S("mod_done"), part + 1)
                cp(modT[:, part, :], MB[:, 0:KT]).then_inc(S("mod_copied"), 1)

            def add_mod(m, items, l, kind, more=0, k_first=0):
                slot, turn = place(l, kind, items.index(("M", m)), more)
                part = acc[:, m % 2 * HALF:(m % 2 + 1) * HALF]
                dve.wait_ge(S(f"slot_in{slot}"), (turn + 1) * 16)
                k = slice(m // 2 + k_first, m // 2 + k_first + 1) if isinstance(k_first, int) else \
                    bass.ds(k_first + m // 2, 1)
                stt(part, ring[:, slot, :], cact[:, 1, k], part, M, Ad).then_inc(S(f"raw_free{slot}"), 1)

            for l in range(layers):
                has_next = l < DEPTH - 1
                dve.wait_ge(S("small_in"), l * 16 + 16)
                if l == 0:
                    ts(h_mod[:, 0, :], modT[:, 1, :], 1.0, None, Ad)
                    cp(h_mod[:, 1, :], modT[:, 0, :])
                else:
                    stt(h_mod[:, 0, :], modT[:, 1, :], 1.0, ln_before[:, 0, :], Ad, M)
                    stt(h_mod[:, 1, :], modT[:, 1, :], 1.0, ln_before[:, 1, :], Ad, M)
                    tt(h_mod[:, 1, :], h_mod[:, 1, :], modT[:, 0, :], Ad)
                for k in range(KT + 2):
                    if k < KT and k % 2 == 0:
                        dve.wait_ge(S("xT_done"), l * KT + k + 1)
                        ts(A(16 + k % 4), XT[k % 4][:, :], h_mod[:, 0, k:k + 1], h_mod[:, 1, k:k + 1], M, Ad)\
                            .then_inc(S("h_even"), 1)
                    if k >= 2:
                        j = k - 2
                        dve.wait_ge(S("h_hi_ready"), l * KT + j + 1)
                        tt(h_lo[:, j, :], A(16 + j % 4), h_hi[:, j, :].bitcast(F32), Su).then_inc(S("h_ready"), 1)
                dve.wait_ge(S("gates_tanh"), l + 1)
                small = MB[:, 0:TT * 32].rearrange("p (t n) -> p t n", t=TT)
                th = A(17)[:, 0:TT * 24].rearrange("p (t n) -> p t n", t=TT)
                ga = A(18)[:, 0:24].rearrange("p (t h) -> p t h", t=TT)
                small_shape = (P, TT, GDN_H)
                tt(ga, small[:, :, 24:30], over(small_part("dt_bias").unsqueeze(1), small_shape), Ad).then_inc(S("ga_ready"), 1)
                ts(gates[:, :, :], th[:, :, 0:18], 0.5, 0.5, M, Ad)
                ts(coef[:, 1, :, :], th[:, :, 18:24], 0.5, 0.5, M, Ad)
                dve.wait_ge(S("ga_ln"), l + 1)
                ln = A(18)[:, 96:120].rearrange("p (t h) -> p t h", t=TT)
                sp_ = A(18)[:, 192:216].rearrange("p (t h) -> p t h", t=TT)
                stt(sp_, ga, 0.0, ln, Mx, Ad)
                ts(coef[:, 2, :, :], coef[:, 1, :, :], 0.5, None, M)
                stt(coef[:, 0, :, :], sp_, -1.0, over(ea[:, :].unsqueeze(1), small_shape), M, M).then_inc(S("g_ready"), 1)
                dve.wait_ge(S("gc_done"), l + 1)
                gc = coef[:, 3, :, :].rearrange("p t h -> p (t h)")
                cp(gc, SB_[0][:, 0:24])
                tt(A(18)[:, 160:184], SB_[0][:, 24:48], gc, Su)
                sync().then_inc(S("gc_ready"), 1)
                dve.wait_ge(S("gc_exp"), l + 1)
                tt(coef[:, 4, :, :].rearrange("p t h -> p (t h)"), coef[:, 1, :, :].rearrange("p t h -> p (t h)"),
                   A(18)[:, 128:152], M)
                sync().then_inc(S("coef_ready"), 1)
                if l:
                    dve.wait_ge(S("x_stored"), l * TT * 16)

                g_items = group_items(has_next)
                with dve.Fori(0, KVH) as g:
                    G = l * KVH + g
                    if has_next:
                        fill(acc[:, :], 0.0).then_inc(S("acc_zero"), 1)

                    def add_mods(m0, m1):
                        if has_next:
                            if m0 == 0:
                                dve.wait_ge(S("bmod_in"), (g + (sums_before[l] + 1)) * 16)
                            for m in range(m0, m1):
                                add_mod(m, g_items, l, "group", g * (LAYOUTS[l]["group_len"] // NS))

                    cp(gate_g[:, :, :], gates[:, :, bass.ds(g * 9, 9)])
                    for which in range(2):
                        dve.wait_ge(S("p_copied"), after("p_copied", l * LAYER_TILES + g * GROUP_TILES + which + 1))
                        src = v_raw[which]
                        windows = bass.AP(src.tensor, src.offset, [src.ap[0], [1, CMP_LEN], [CMP_STRIDE, N_CMP]])
                        tt(blocks_kv[which][:, 0:CMP_LEN * N_CMP].rearrange("p (t n) -> p t n", n=N_CMP), windows,
                           over(peT[:, which, :].unsqueeze(2), (P, CMP_LEN, N_CMP)), Ad).then_inc(S("blocks_ready"), 1)
                    for which in range(2):
                        dve.wait_ge(S("cmp_tanh"), G * 2 + which + 1)
                        hid = hidden[:, which, :]
                        stt(hid, hid_tanh[:, which, :], 1.0, TB[which][0:N_CMP, 0:HD], Ad, M)
                        ts(hid, hid, 0.5, None, M).then_inc(S("hid_ready"), 1)
                    dve.wait_ge(S("hidT_done"), G + 1)
                    for which in range(2):
                        cp(cmpb[:, 2 + which, 0:N_CMP], SB_[which][:, 0:N_CMP])
                    sync().then_inc(S("hidT_ready"), 1)
                    first = CMP_LEN - 1
                    rope(G * 6, cmpb[0:32, 0, 0:N_CMP], N_CMP, slice(first, first + (N_CMP - 1) * CMP_STRIDE + 1, CMP_STRIDE))
                    rope(G * 6 + 1, kS[0:32, :], SEQ, slice(0, SEQ))
                    rope(G * 6 + 2, kW[0:32, :], SEQ, slice(0, SEQ))
                    rope(G * 6 + 3, qT[0][0:32, :], SEQ, slice(0, SEQ))

                    def silu_z(H, dst):
                        dve.wait_ge(S("z_tanh"), H + 1)
                        stt(dst, z_tanh, 1.0, z_raw, Ad, M).then_inc(S("sz_ready"), 1)

                    silu_z(G * GROUP, szq[0])
                    for r in range(GROUP):
                        H = G * GROUP + r
                        for s in range(NSA_STEPS):
                            if s in MOD_STEPS[r]:
                                add_mods(*MOD_STEPS[r][s])
                            if s == 0:
                                dve.wait_ge(S("cmp_scores"), H + 1)
                                shape = (P, TT, N_CMP)
                                mx, sm = tiny[:, 24:28], tiny[:, 28:32]
                                scores = SB_[0][:, 0:TT * 32].rearrange("p (t n) -> p t n", t=TT)[:, :, 0:N_CMP]
                                stt(cmp_s, scores, SCALE, C("cmp_add").rearrange("p (t n) -> p t n", t=TT), M, Ad)\
                                    .then_inc(S("cmp_scored"), 1)
                                reduce(mx, cmp_s, AX, Mx)
                                tt(cmp_s, cmp_s, over(mx.unsqueeze(2), shape), Su).then_inc(S("cmp_scored2"), 1)
                                dve.wait_ge(S("cmp_exp"), H + 1)
                                tt(cmp_s, cmp_s, C("cmp_mul").rearrange("p (t n) -> p t n", t=TT), M)
                                reduce(sm, cmp_s, AX, Ad)
                                ts(sm, sm, 1e-30, None, Mx)
                                reciprocal(sm, sm)
                                tt(sm, sm, gate_g[:, :, 3 * r], M)
                                tt(cmp_p, cmp_s, over(sm.unsqueeze(2), shape), M).then_inc(S("cmp_probs"), 1)
                            if 1 <= s <= 8:
                                u = s - 1
                                i, w, b = u % TT, (u % TT + 1) * P, SB_[(u + 1) % 2]
                                dve.wait_ge(S("scores"), H * 8 + u + 1)
                                reduce(tiny[:, 30:31], b[:, 0:w], AX, Mx)
                                ts(tiny[:, u:u + 1], tiny[:, 30:31], -SCALE, None, M).then_inc(S("max_ready"), 1)
                                if s == 1:
                                    dve.wait_ge(S("cmp_pT"), H + 1)
                                    cp(cmp_pT, TB[0][0:N_CMP, :]).then_inc(S("cmp_pT_ready"), 1)
                                dve.wait_ge(S("exp_done"), after("exp_done", H * 8 + u + 1))
                                reciprocal(tiny[:, 31:32], tiny[:, 8 + u:9 + u])
                                ts(prob[u % 2][:, 0:w], prob[u % 2][:, 0:w], tiny[:, 31:32],
                                   gate_g[:, i, 3 * r + 1 + u // TT:3 * r + 2 + u // TT], M, M).then_inc(S("probs"), 1)
                            if s == 8 and r < GROUP - 1:
                                rope(G * 6 + 4 + r, qT[(r + 1) % 2][0:32, :], SEQ, slice(0, SEQ))
                        if r < GROUP - 1:
                            silu_z(H + 1, szq[(r + 1) % 2])
                        dve.wait_ge(S("pv_done"), after("pv_done", H * 8 + 8))
                        stt(yT[:, bass.ds(g * GROUP + r, 1), :].rearrange("p a n -> p (a n)"), OB[:, :], 0.5,
                            szq[r % 2], M, M).then_inc(S("y_ready"), 1)
                    if has_next:
                        sync().then_inc(S("mod_sum"), 1)
                        dve.wait_ge(S("mod_done"), g + (sums_before[l] + 1))
                        cp(modT[:, bass.ds(g, 1), :].rearrange("p a n -> p (a n)"), MB[:, 0:KT])\
                            .then_inc(S("mod_copied"), 1)

                fill(acc[:, :], 0.0).then_inc(S("acc_zero"), 1)

                per_token = lambda i: over(coef_h[:, i, :].unsqueeze(2), BIG)
                conv_heads = taps.rearrange("p (k h) -> p k h", h=GDN_H)

                def conv(h, src, dst, part, first, end):
                    if first == 0:
                        dve.wait_ge(S("p_copied"), after("p_copied", tile_of_lot(l, h) + src + 1))
                    for k in range(first, end):
                        tap, x_ = conv_h[:, k, part:part + 1], raw[:, src, k:k + SEQ]
                        if k == 0:
                            ts(A(dst), x_, tap, None, M)
                        else:
                            stt(A(dst), x_, tap, A(dst), M, Ad)
                    if end == TAPS:
                        sync().then_inc(S("gdn_conv"), 1)
                        dve.sem_inc(S(f"raw_used{src}"), 1)

                def front(h, part):
                    F = l * GDN_H + h
                    if part == -3:
                        one_head = slice(h, h + 1) if isinstance(h, int) else bass.ds(h, 1)
                        cp(coef_h[:, :, :], coef[:, :, :, one_head].rearrange("p a t h -> p (a t) h").rearrange(
                            "p (a t) h -> p a (t h)", t=TT))
                        cp(conv_h[:, :, :].rearrange("p t x -> p (t x)"),
                           conv_heads[:, :, one_head].rearrange("p k h -> p (k h)"))
                        conv(h, 0, 0, 1, 0, 2)
                    if part == -2:
                        conv(h, 0, 0, 1, 2, TAPS)
                    if part == -1:
                        conv(h, 1, 7, 0, 0, 2)
                    if part == 0:
                        dve.wait_ge(S("gdn_tanh"), F * 2 + 1)
                        stt(A(0), A(2), 1.0, A(0), Ad, M).then_inc(S("gdn_silu"), 1)
                        conv(h, 1, 7, 0, 2, 3)
                    if part == 1:
                        conv(h, 1, 7, 0, 3, TAPS)
                        tt(tiles(A(12)), over(C("cumul").unsqueeze(1), BIG), per_token(0), M).then_inc(S("gdn_gsel"), 1)
                    if part == 2:
                        dve.wait_ge(S("gdn_tanh"), F * 2 + 2)
                        stt(A(7), A(3), 1.0, A(7), Ad, M).then_inc(S("gdn_silu"), 1)
                        conv(h, 2, 10, 2, 0, 1)
                    if part == 3:
                        conv(h, 2, 10, 2, 1, 3)
                    if part == 4:
                        conv(h, 2, 10, 2, 3, TAPS)
                        dve.wait_ge(S("gdn_rsqrt"), F * 2 + 1)
                        tt(A(0), A(0), A(2), M).then_inc(S("gdn_k"), 1)
                    if part == 6:
                        dve.wait_ge(S("gdn_rsqrt"), F * 2 + 2)
                        tt(A(7), A(7), A(3), M).then_inc(S("gdn_q"), 1)
                    if part == 7:
                        dve.wait_ge(S("gdn_gcb"), F + 1)
                        tt(tiles(A(5)), tiles(MB[:, :]), per_token(3), Su)
                        ts(A(5), A(5), 0.0, None, Mx).then_inc(S("gdn_d"), 1)

                def delta(h, pipelined):
                    D = l * GDN_H + h

                    def ready(name):
                        dve.wait_ge(S(name), D + 1)

                    def mask(v):
                        m = ((1,) + LEVELS)[v]
                        return tt(tiles(A(14 + v % 2)), tiles(A(12)), over(C(f"mergeT{m}").unsqueeze(1), BIG), M)

                    fill(state[:, :], 0.0)
                    sync().then_inc(S("rec_state"), 1)
                    ready("gdn_decay")
                    tt(tiles(A(2)), tiles(A(5)), per_token(1), M)
                    ready("gdn_kk")
                    tt(A(3), TB[1][:, :], A(2), M).then_inc(S("gdn_lower"), 1)
                    tt(tiles(A(17)), tiles(A(5)), over(C("incl").unsqueeze(1), BIG), M)
                    ready("gdn_qk")
                    tt(A(17), SB_[0][:, :], A(17), M).then_inc(S("gdn_intra"), 1)
                    T = narrow(A(11))
                    for half in range(2):
                        rows = slice(half * CHUNK, (half + 1) * CHUNK)
                        dve.tensor_tensor(T[rows], own(A(3), half),
                                          over(C("merge1_c")[rows].unsqueeze(1), (CHUNK, TT, CHUNK)), M)
                    sync()
                    tt(T, over(C("ident_c").unsqueeze(1), NARROW), T, Su)
                    ready("gdn_lT_copied")
                    mask(1).then_inc(S("gdn_ct"), 1)
                    mask(0)
                    tt(tiles(A(13)), over(ident.unsqueeze(1), BIG), tiles(A(14)), Su)
                    sync().then_inc(S("gdn_T"), 1)
                    for v in range(len(LEVELS)):
                        if v < len(LEVELS) - 1:
                            mask(v + 2).then_inc(S("gdn_ct"), 1)
                        if v == 0:
                            ready("gdn_vtanh")
                            stt(A(10), A(5), 1.0, A(10), Ad, M).then_inc(S("gdn_v"), 1)
                        if v == 1:
                            ready("gdn_kT")
                            tt(tiles(A(1)), tiles(TB[0][:, :]), per_token(4), M)
                            tt(tiles(A(9)), tiles(TB[0][:, :]), per_token(5), M)
                        if v == 2:
                            ready("gdn_vT")
                            tt(tiles(A(8)), tiles(OB[:, :]), per_token(2), M)
                        if v == 3:
                            ready("gdn_egb")
                            tt(A(6), A(7), A(4), M).then_inc(S("gdn_qh"), 1)
                        if v == 4:
                            ready("gdn_ztanh")
                            stt(A(19), A(18), 1.0, raw[:, 3, TAPS - 1:], Ad, M).then_inc(S("raw_used3"), 1)
                        if v >= 2 and pipelined:
                            front(h + 1, v - 5)
                        if v < len(LEVELS) - 1:
                            dve.wait_ge(S("gdn_TCTn"), D * 4 + v + 1)
                            tt(T, T, narrow(SB_[0]), Su)
                        dve.wait_ge(S("gdn_TCT"), D * 5 + v + 1)
                        tt(A(13), A(13), SB_[1][:, :], Su)
                        sync().then_inc(S("gdn_T" if v < len(LEVELS) - 1 else "gdn_Tt"), 1)
                    for i in range(SEQ // CHUNK):
                        dve.wait_ge(S("rec_kv"), D * 8 + i + 1)
                        end = (i + 1) * CHUNK - 1
                        stt(state[:, :], state[:, :], A(4)[:, end:end + 1], TB[i % 2][:, 0:HD], M, Ad)\
                            .then_inc(S("rec_state"), 1)
                        if pipelined:
                            front(h + 1, i)
                    ready("gdn_ro")
                    tt(A(14), OB[:, :], A(15), M)
                    yt = yT[:, bass.ds(h + NSA_H, 1), :].rearrange("p a n -> p (a n)") if pipelined else \
                        yT[:, h + NSA_H, :]
                    stt(yt, A(14), gnorm, A(19), M, M).then_inc(S("y_ready"), 1)

                for part in range(-3, 8):
                    front(0, part)
                with dve.Fori(0, GDN_H - 1) as h:
                    delta(h, True)
                delta(GDN_H - 1, False)

                def split_y(k):
                    dve.wait_ge(S("y_hi"), l * MIX_T + k + 1)
                    tt(h_lo[:, k, :], yT[:, k, :], h_hi[:, k, :].bitcast(F32), Su).then_inc(S("y_split"), 1)

                def stick(h, kind, items, first_k, more=0):
                    last = kind == "sb_3"
                    B = l * SB_H + h
                    for i in range(2):
                        dve.wait_ge(S("p_copied"), after("p_copied", tile_of_lot(l, GDN_H + h) + i + 1))
                        ts(A(i), raw[:, i, TAPS - 1:], (1.0, SCALE)[i], None, M).then_inc(S(f"raw_used{i}"), 1)
                    sync().then_inc(S("sb_qk"), 1)
                    dve.wait_ge(S("sb_vT"), B + 1)
                    cp(A(2), MB[:, :]).then_inc(S("sb_v"), 1)
                    dve.sem_inc(S("raw_used2"), 1)

                    def silu_of_z():
                        dve.wait_ge(S("sb_ztanh"), B + 1)
                        stt(A(3), A(4), 1.0, raw[:, 3, TAPS - 1:], Ad, M).then_inc(S("raw_used3"), 1)

                    if not last:
                        silu_of_z()
                    for s in range(TT + 1):
                        if s < TT:
                            for m in (2 * s, 2 * s + 1):
                                add_mod(m, items, l, kind, more, first_k)
                            if last and s == TT - 1:
                                dve.sem_inc(S("mod_sum"), 1)
                        if s < TT:
                            j, w = TT - 1 - s, (s + 1) * P
                            dve.wait_ge(S("sb_ln"), B * TT + s + 1)
                            stt(A(9 + j)[:, 0:w], SB_[s % 2][:, 0:w], 0.0, A(5 + s % 2)[:, 0:w], Mx, Ad)
                            tt(A(13 + s % 2)[:, 0:w], SB_[s % 2][:, 0:w], A(9 + j)[:, 0:w], Su)\
                                .then_inc(S("lb_ready"), 1)
                            tt(A(9 + j)[:, 0:P], A(9 + j)[:, 0:P], C("past"), M)
                            sync().then_inc(S("spm_ready"), 1)
                        if s >= 1:
                            w = s * P
                            lb = A(13 + (s - 1) % 2)[:, 0:w]
                            dve.wait_ge(S("sb_acc"), B * TT + s)
                            tt(lb, lb, TB[(s - 1) % 2][:, 0:w], Su).then_inc(S("sb_arg"), 1)
                            a = A(16 - s % 2)[:, 0:P]
                            dve.wait_ge(S("sb_exp"), after("sb_exp", B * TT + s))
                            tt(a, a, C("past"), M).then_inc(S("sb_a"), 1)
                        if last and s >= 3:
                            for k in range((s - 3) * 5, (s - 2) * 5):
                                split_y(k)
                    if last:
                        silu_of_z()
                        for k in range(10, MIX_T - 1):
                            split_y(k)
                    dve.wait_ge(S("sb_pv"), after("sb_pv", B * TT + TT))
                    at = yT[:, NSA_H + GDN_H + h, :] if isinstance(h, int) else \
                        yT[:, bass.ds(h + (NSA_H + GDN_H), 1), :].rearrange("p a n -> p (a n)")
                    stt(at, OB[:, :], 0.5, A(3), M, M).then_inc(S("y_ready"), 1)

                dve.wait_ge(S("bmod_in"), (sums_before[l] + (3 if has_next else 1)) * 16)
                with dve.Fori(0, SB_H - 2) as h:
                    stick(h, "sb", SB_ITEMS, h * 4, h * (len(SB_ITEMS) // NS))
                stick(SB_H - 2, "sb_2", SB_2_ITEMS, 4 * (SB_H - 2))
                stick(SB_H - 1, "sb_3", SB_3_ITEMS, 4 * (SB_H - 1))
                split_y(MIX_T - 1)

                for n in range(TT):
                    dve.wait_ge(S("gate_done"), 2 * l + 1 + n // 2)
                    ts(gateb[:, n * SEQ:(n + 1) * SEQ], ODD[n][:, :], 1.0, None, Ad)
                sync().then_inc(S("gate_ready"), 1)
                for n in range(TT):
                    outs, cols = (bank[2:6], ODD)[n % 2], slice(n * SEQ, (n + 1) * SEQ)
                    dve.wait_ge(S(f"xo_in{n}"), 16 + l * 48)
                    if l:
                        g_, b_ = (raw[:, n % 2 * 2 + a, TAPS - 1:] for a in range(2))
                        shape = (P, TT, SEQ)
                        tt(xres[:, :, cols], xres[:, :, cols], over(g_.unsqueeze(1), shape), M)
                        tt(xres[:, :, cols], xres[:, :, cols], over(b_.unsqueeze(1), shape), Ad)\
                            .then_inc(S("lnb_used"), 1)
                    for t in range(TT):
                        if t < TT - 1:
                            dve.wait_ge(S("o_done"), (l * TT + n) * (TT - 1) + t + 1)
                        else:
                            dve.wait_ge(S("split_used"), after("split_used", split_of_lot(l, N_LOTS) + (n + 1) * (KT // 2)))
                        tt(A(16 + t), outs[t][:, :], gateb[:, cols], M).then_inc(S("o_used"), 1)
                        x_ = xres[:, t, cols]
                        stt(x_, x_, ALPHA, A(16 + t), M, Ad)
                        bn_stats(stats[:, t, n, :], x_)
                for t in range(TT):
                    bn_aggr(meanvar[:, t, :], stats[:, t, :, :])
                sync().then_inc(S("var_ready"), 1)
                dve.wait_ge(S("rstd_ready"), l + 1)
                stt(tiny[:, 36:40], meanvar[:, :, 0], -1.0, tiny[:, 20:24], M, M).then_inc(S("nmr_ready"), 1)
                if l < layers - 1:
                    for t in (2, 3):
                        x_ = xres[:, t, :]
                        ts(x_, x_, meanvar[:, t, 0:1], tiny[:, 20 + t:21 + t], Su, M).then_inc(S("norm_dve"), 1)
            dve.wait_ge(S("ln_in"), 16)
            for t in (1, 2, 3):
                x_ = xres[:, t, :]
                stt(x_, x_, meanvar[:, t, 0:1], ln_gb[:, 0, :], Su, M)
                stt(x_, x_, tiny[:, 20 + t:21 + t], ln_gb[:, 1, :], M, Ad).then_inc(S("dve_out"), 1)


def by_row_tiles(w):
    *lead, rows, n = w.shape
    return w.reshape(*lead, rows // P, P, n).swapaxes(-3, -2).reshape(*lead, P, rows // P * n)


def columns(w_in, start, i):
    return by_row_tiles(w_in[:, :, start + i * P:start + (i + 1) * P])


def halves(loads):
    return [loads[..., :HALF], loads[..., HALF:]]


def weight_stream(w_mod, w_in, w1_k, w1_v, w_out):
    loads = []

    def mod_half(l, part, m):
        return halves(w_mod[l, m // 2::KT, part * DM:(part + 1) * DM])[m % 2]

    def lot_tile(l, i):
        n, i = i // LOT + 1, i % LOT
        starts, h = ((C_GK, C_GQ, C_GV, C_GZ), n) if n < GDN_H else ((C_SK, C_SQ, C_SV, C_SZ), n - GDN_H)
        return halves(columns(w_in, starts[i], h)[l])

    def part(l, first, items, k_first=0):
        for item in items:
            loads.append(lot_tile(l, first + item[1])[item[2]] if item[0] == "C"
                         else mod_half(l, 2, item[1] + 2 * k_first))

    for l in range(DEPTH):
        for g in range(KVH):
            tiles = [halves(columns(w_in, start, g)[l]) for start in (C_KC, C_VC, C_KS, C_VS, C_KW, C_VW)]
            for r in range(GROUP):
                tiles += [halves(columns(w_in, start, g * GROUP + r)[l]) for start in (C_NQ, C_NZ)]
            tiles += [halves(columns(w_in, start, 0)[l]) for start in ((C_GK, C_GQ), (C_GV, C_GZ))[g]]
            w1 = [h for w in (w1_k, w1_v) for rows in (w[l, :DM], w[l, DM:]) for h in halves(by_row_tiles(rows))]
            for item in group_items(l < DEPTH - 1):
                if item[0] == "C":
                    loads.append(tiles[item[1]][item[2]])
                elif item[0] == "D":
                    loads.append(w1[item[1]])
                else:
                    loads.append(mod_half(l + 1, g, item[1]))
        part(l, 0, FIRST_TILE)
        for h in range(GDN_H):
            part(l, 1 + h * LOT, GDN_ITEMS)
        for h in range(SB_H - 2):
            part(l, 1 + (GDN_H + h) * LOT, SB_ITEMS, 4 * h)
        part(l, 1 + (N_LOTS - 2) * LOT, SB_2_ITEMS, 4 * (SB_H - 2))
        part(l, 3 + (N_LOTS - 2) * LOT, SB_3_ITEMS, 4 * (SB_H - 1))
        for n in range(TT):
            for k2 in range(KT // 2):
                loads.append(by_row_tiles(w_out[l, k2 * 2 * P:(k2 + 1) * 2 * P, n * SEQ:(n + 1) * SEQ]))
    return np.stack(loads)


def small_weights(w2_k, w2_v, conv_w, norm_g, pe_k, pe_v, dt_bias, a_log, ln_g, ln_b):
    taps = conv_w.reshape(DEPTH, TAPS * 18, P).swapaxes(1, 2)
    rows = [np.broadcast_to(v[:, None, :], (DEPTH, P, GDN_H)) for v in (dt_bias, a_log)]
    before = [np.roll(v, 1, 0).reshape(DEPTH, KT, P).swapaxes(1, 2) for v in (ln_g, ln_b)]
    return np.concatenate([w2_k, w2_v, taps, norm_g[:, :, None],
                           pe_k.swapaxes(1, 2), pe_v.swapaxes(1, 2), *rows, *before], 2)


def small_columns(w_in):
    few = np.concatenate([w_in[:, :, C_NG:C_NG + 18], w_in[:, :, C_GB:C_GB + 2 * GDN_H]], 2)
    return by_row_tiles(few).reshape(DEPTH, P, SMALL_HALVES, 4 * N_SMALL).swapaxes(1, 2)


def kernel(x, c, positions, w_mod, b_mod, w_in, w_out, ln_g, ln_b, cmp_pe_k, cmp_pe_v, cmp_w1_k,
           cmp_w2_k, cmp_w1_v, cmp_w2_v, gdn_conv_w, gdn_a_log, gdn_dt_bias, gdn_norm_g):
    import concourse.bacc as _bacc
    from concourse.bass_utils import run_bass_kernel_spmd as _run

    nc = _bacc.Bacc("TRN2", target_bir_lowering=False, num_devices=1)
    const, where = constants()
    arrays = {
        "x": x, "positions": positions, "c": c, "b_mod": b_mod,
        "mod0": np.concatenate([w_mod[0].reshape(P, KT, 3, DM)[:, :, part].swapaxes(0, 1) for part in range(2)]),
        "small_cols": small_columns(w_in),
        "stream": weight_stream(w_mod, w_in, cmp_w1_k, cmp_w1_v, w_out),
        "small": small_weights(cmp_w2_k, cmp_w2_v, gdn_conv_w, gdn_norm_g, cmp_pe_k, cmp_pe_v,
                               gdn_dt_bias, gdn_a_log, ln_g, ln_b),
        "lns": np.concatenate([ln_g, ln_b], 1),
        "const": const,
    }
    arrays = {f"in_{name}": np.ascontiguousarray(a) for name, a in arrays.items()}
    args = [nc.dram_tensor(n, a.shape, mybir.dt.from_np(a.dtype), kind="ExternalInput").ap()
            for n, a in arrays.items()]
    out = nc.dram_tensor("out_0", (1, SEQ, DM), F32, kind="ExternalOutput").ap()
    build(nc, *args, out, where)
    r = _run(nc, [arrays], core_ids=[0])
    return r.results[0]["out_0"]
```
